# Optimizing a Trainium2 kernel written in Bass

```python
import math
import jax, jax.numpy as jnp
from jax import lax
import numpy as np

D_MODEL = 1024
BATCH = 1
SEQ = 256
DEPTH = 2
DEC_BATCH = 8
DEC_SEQ = 1
PAST_LEN = 2048
PAGE_SIZE = 128

N_EVEN = (DEPTH + 1) // 2
N_ODD = DEPTH // 2
MIX_WIDTH = D_MODEL
HG_HEADS = 4
HG_DK = 128
HG_DV = MIX_WIDTH // 2 // HG_HEADS
GLA_HEADS = 4
GLA_DV = MIX_WIDTH // 2 // GLA_HEADS
GLA_DK = GLA_DV // 2
GLA_RANK = 16
GLA_GATE_NORM = 16.0
ML_HEADS = 4
ML_DV = MIX_WIDTH // ML_HEADS
ML_DK = ML_DV // 2
CONV_W = 4
ML_QK = 2 * ML_HEADS * ML_DK
D_FF_DENSE = 2816
D_FF_EXPERT = 3584
N_EXPERTS = 8
TOP_K = 2
CHUNK = 64
EPS = 1e-5
ALPHA = (2.0 * DEPTH) ** 0.25
BETA = (8.0 * DEPTH) ** -0.25

EVEN_WIDTHS = (HG_HEADS * HG_DK, HG_HEADS * HG_DK, HG_HEADS * HG_DV, HG_HEADS * HG_DV,
               GLA_HEADS * GLA_DK, GLA_HEADS * GLA_DK, GLA_HEADS * GLA_DV, GLA_HEADS * GLA_DV,
               GLA_RANK)
EVEN_IN = (2 * HG_HEADS * HG_DK + 2 * HG_HEADS * HG_DV + 2 * GLA_HEADS * GLA_DK
           + 2 * GLA_HEADS * GLA_DV + GLA_RANK)
ODD_WIDTHS = (ML_QK, ML_HEADS * ML_DV, ML_HEADS * ML_DV, 2 * ML_HEADS)
ODD_IN = ML_QK + 2 * ML_HEADS * ML_DV + 2 * ML_HEADS

kernel_name = "hgrn2_gla_mlstm_moe_decoder_step"

F32 = jnp.float32

def _split(z, widths):
    out, start = [], 0
    for w in widths:
        out.append(z[..., start:start + w])
        start += w
    return out

def _layernorm(x, g, b):
    xf = x.astype(F32)
    mu = jnp.mean(xf, -1, keepdims=True)
    var = jnp.mean(jnp.square(xf - mu), -1, keepdims=True)
    return ((xf - mu) * lax.rsqrt(var + EPS) * g.astype(F32) + b.astype(F32)).astype(x.dtype)

def _rms_swish_gate(o, gate, w):
    bsz, L, H, dv = o.shape
    o = o * lax.rsqrt(jnp.mean(jnp.square(o), -1, keepdims=True) + EPS) * w.astype(F32)
    return (o * jax.nn.silu(gate.reshape(bsz, L, H, dv))).reshape(bsz, L, H * dv)

def _to_chunks(t, nc, cs):
    bsz = t.shape[0]
    return jnp.moveaxis(t.reshape(bsz, nc, cs, *t.shape[2:]), 1, 0)

def _gated_linear_attention(q, k, v, log_a, s0):
    bsz, L, H, _ = q.shape
    cs = math.gcd(L, CHUNK)
    nc = L // cs
    causal = jnp.tril(jnp.ones((cs, cs), dtype=bool))

    def step(s, inp):
        qc, kc, vc, gc = inp
        bc = jnp.cumsum(gc, axis=1)
        o_inter = jnp.einsum('bthk,bhkv->bthv', qc * jnp.exp(bc), s)
        log_d = bc[:, :, None] - bc[:, None, :]
        decay = jnp.exp(jnp.where(causal[None, :, :, None, None], log_d, -jnp.inf))
        scores = jnp.einsum('bthk,bshk,btshk->btsh', qc, kc, decay)
        o = o_inter + jnp.einsum('btsh,bshv->bthv', scores, vc)
        b_last = bc[:, -1]
        s_new = (jnp.exp(b_last)[..., None] * s
                 + jnp.einsum('bshk,bshv->bhkv', kc * jnp.exp(b_last[:, None] - bc), vc))
        return s_new, o

    xs = tuple(_to_chunks(t, nc, cs) for t in (q, k, v, log_a))
    s_fin, o = lax.scan(step, s0.astype(F32), xs)
    o = jnp.moveaxis(o, 0, 1).reshape(bsz, L, H, v.shape[-1])
    return o, s_fin.astype(s0.dtype)

def _mlstm(q, k, v, ig, lf, C0, n0, m0):
    bsz, L, H, _ = q.shape
    cs = math.gcd(L, CHUNK)
    nc = L // cs
    causal = jnp.tril(jnp.ones((cs, cs), dtype=bool))

    def step(carry, inp):
        C, n, m = carry
        qc, kc, vc, ic, fc = inp
        b = jnp.cumsum(fc, axis=1)
        log_d = b[:, :, None, :] - b[:, None, :, :] + ic[:, None, :, :]
        log_d = jnp.where(causal[None, :, :, None], log_d, -jnp.inf)
        log_prev = b + m[:, None, :]
        m_t = jnp.maximum(jnp.max(log_d, axis=2), log_prev)
        d = jnp.exp(log_d - m_t[:, :, None, :])
        w_prev = jnp.exp(log_prev - m_t)
        scores = jnp.einsum('bthk,bshk->btsh', qc, kc) * d
        num = (jnp.einsum('btsh,bshv->bthv', scores, vc)
               + w_prev[..., None] * jnp.einsum('bthk,bhkv->bthv', qc, C))
        den = jnp.sum(scores, axis=2) + w_prev * jnp.einsum('bthk,bhk->bth', qc, n)
        h = num / jnp.maximum(jnp.abs(den), jnp.exp(-m_t))[..., None]
        m_new = m_t[:, -1]
        w_c = jnp.exp(b[:, -1] + m - m_new)
        w_s = jnp.exp(b[:, -1:, :] - b + ic - m_new[:, None, :])
        C_new = w_c[..., None, None] * C + jnp.einsum('bsh,bshk,bshv->bhkv', w_s, kc, vc)
        n_new = w_c[..., None] * n + jnp.einsum('bsh,bshk->bhk', w_s, kc)
        return (C_new, n_new, m_new), h

    xs = tuple(_to_chunks(t, nc, cs) for t in (q, k, v, ig, lf))
    (C, n, m), h = lax.scan(step, (C0.astype(F32), n0.astype(F32), m0.astype(F32)), xs)
    h = jnp.moveaxis(h, 0, 1).reshape(bsz, L, H, v.shape[-1])
    return h, C.astype(C0.dtype), n.astype(n0.dtype), m.astype(m0.dtype)

def _even_mixer(x, s_hg, s_gla, w_in, lb, w_gk, b_gk, gn_hg, gn_gla, w_out):
    bsz, L, _ = x.shape
    z = (x @ w_in).astype(F32)
    hq, hf, hi, hg, gq, gk, gv, gg, gr = _split(z, EVEN_WIDTHS)
    heads = lambda t, h: t.reshape(bsz, L, h, -1)
    f = lb + (1.0 - lb) * jax.nn.sigmoid(hf)
    one_minus_f = (1.0 - lb) * jax.nn.sigmoid(-hf)
    o_hg, s_hg_new = _gated_linear_attention(
        heads(jax.nn.silu(hq), HG_HEADS), heads(one_minus_f, HG_HEADS),
        heads(hi, HG_HEADS), heads(jnp.log(f), HG_HEADS), s_hg)
    log_a = jax.nn.log_sigmoid(gr @ w_gk.astype(F32) + b_gk.astype(F32)) / GLA_GATE_NORM
    o_gla, s_gla_new = _gated_linear_attention(
        heads(gq * GLA_DK ** -0.5, GLA_HEADS), heads(gk, GLA_HEADS),
        heads(gv, GLA_HEADS), heads(log_a, GLA_HEADS), s_gla)
    y = jnp.concatenate([_rms_swish_gate(o_hg, hg, gn_hg), _rms_swish_gate(o_gla, gg, gn_gla)], axis=-1)
    return y.astype(x.dtype) @ w_out, s_hg_new, s_gla_new

def _odd_mixer(x, C0, n0, m0, conv0, w_in, b_gate, conv_w, conv_b, hn_w, w_out):
    bsz, L, _ = x.shape
    z = (x @ w_in).astype(F32)
    u, v, o_pre, gates = _split(z, ODD_WIDTHS)
    full = jnp.concatenate([conv0.astype(F32), u], axis=1)
    cw = conv_w.astype(F32)
    uc = conv_b.astype(F32)
    for j in range(CONV_W):
        uc = uc + full[:, j:j + L] * cw[j]
    q, k = _split(jax.nn.silu(uc), (ML_HEADS * ML_DK, ML_HEADS * ML_DK))
    gates = gates + b_gate.astype(F32)
    ig, fg = gates[..., :ML_HEADS], gates[..., ML_HEADS:]
    heads = lambda t: t.reshape(bsz, L, ML_HEADS, -1)
    h, C, n, m = _mlstm(heads(q * ML_DK ** -0.5), heads(k), heads(v), ig,
                        jax.nn.log_sigmoid(fg), C0, n0, m0)
    mu = jnp.mean(h, -1, keepdims=True)
    var = jnp.mean(jnp.square(h - mu), -1, keepdims=True)
    h = (h - mu) * lax.rsqrt(var + EPS) * hn_w.astype(F32).reshape(ML_HEADS, ML_DV)
    y = jax.nn.sigmoid(o_pre) * h.reshape(bsz, L, ML_HEADS * ML_DV)
    return y.astype(x.dtype) @ w_out, C, n, m, full[:, L:].astype(conv0.dtype)

def _swiglu(x, w1, w3, w2):
    return (jax.nn.silu(x @ w1) * (x @ w3)) @ w2

def _moe(x, w_router, w1, w3, w2):
    logits = (x @ w_router).astype(F32)
    top_v, top_i = lax.top_k(logits, TOP_K)
    top_w = jax.nn.softmax(top_v, axis=-1)
    gate = jnp.sum(jax.nn.one_hot(top_i, N_EXPERTS, dtype=F32) * top_w[..., None], axis=-2)
    y = jnp.zeros(x.shape, F32)
    for e in range(N_EXPERTS):
        y = y + gate[..., e:e + 1] * _swiglu(x, w1[e], w3[e], w2[e]).astype(F32)
    return y.astype(x.dtype)

def _trunk(x, s_hg, s_gla, s_C, s_n, s_m, s_conv, p):
    lb_all = jnp.cumsum(jax.nn.softmax(p['hg_lower_bounds'].astype(F32), axis=0), axis=0)
    hg_out, gla_out, C_out, n_out, m_out, conv_out = [], [], [], [], [], []
    for layer in range(DEPTH):
        i = layer // 2
        if layer % 2 == 0:
            mix, hg_new, gla_new = _even_mixer(
                x, s_hg[i], s_gla[i], p['w_in_even'][i], lb_all[i], p['w_gk'][i], p['b_gk'][i],
                p['gn_hg'][i], p['gn_gla'][i], p['w_out_even'][i])
            hg_out.append(hg_new)
            gla_out.append(gla_new)
            x = _layernorm(ALPHA * x + mix, p['ln1_g'][layer], p['ln1_b'][layer])
            ffn = _swiglu(x, p['w1_dense'][i], p['w3_dense'][i], p['w2_dense'][i])
        else:
            mix, C_new, n_new, m_new, conv_new = _odd_mixer(
                x, s_C[i], s_n[i], s_m[i], s_conv[i], p['w_in_odd'][i], p['b_gate_odd'][i],
                p['conv_w'][i], p['conv_b'][i], p['hn_w'][i], p['w_out_odd'][i])
            C_out.append(C_new)
            n_out.append(n_new)
            m_out.append(m_new)
            conv_out.append(conv_new)
            x = _layernorm(ALPHA * x + mix, p['ln1_g'][layer], p['ln1_b'][layer])
            ffn = _moe(x, p['w_router'][i], p['w1_moe'][i], p['w3_moe'][i], p['w2_moe'][i])
        x = _layernorm(ALPHA * x + ffn, p['ln2_g'][layer], p['ln2_b'][layer])
    return (x, jnp.stack(hg_out), jnp.stack(gla_out), jnp.stack(C_out), jnp.stack(n_out),
            jnp.stack(m_out), jnp.stack(conv_out))

def setup_inputs(seed: int = 0) -> dict:
    key = jax.random.key(seed)
    ks = list(jax.random.split(key, 48))
    nrm = lambda shape, scale: jax.random.normal(ks.pop(), shape, F32) * scale
    D = D_MODEL
    b_gate = jnp.concatenate([
        -1.0 + nrm((N_ODD, ML_HEADS), 0.1),
        jnp.linspace(3.0, 6.0, ML_HEADS, dtype=F32)[None] + nrm((N_ODD, ML_HEADS), 0.1)], axis=-1)
    return {
        "x_prompt": nrm((BATCH, SEQ, D), 1.0),
        "x_sample": nrm((DEC_BATCH, DEC_SEQ, D), 1.0),
        "state_hgrn": nrm((N_EVEN, DEC_BATCH, HG_HEADS, HG_DK, HG_DV), 0.5),
        "state_gla": nrm((N_EVEN, DEC_BATCH, GLA_HEADS, GLA_DK, GLA_DV), 0.5),
        "state_mlstm_C": nrm((N_ODD, DEC_BATCH, ML_HEADS, ML_DK, ML_DV), 0.3),
        "state_mlstm_n": nrm((N_ODD, DEC_BATCH, ML_HEADS, ML_DK), 0.3),
        "state_mlstm_m": nrm((N_ODD, DEC_BATCH, ML_HEADS), 1.0),
        "state_mlstm_conv": nrm((N_ODD, DEC_BATCH, CONV_W - 1, ML_QK), 1.0),
        "w_in_even": nrm((N_EVEN, D, EVEN_IN), D ** -0.5),
        "hg_lower_bounds": nrm((N_EVEN + 1, HG_HEADS * HG_DK), 0.1),
        "w_gk": nrm((N_EVEN, GLA_RANK, GLA_HEADS * GLA_DK), GLA_RANK ** -0.5),
        "b_gk": nrm((N_EVEN, GLA_HEADS * GLA_DK), 0.1),
        "gn_hg": 1.0 + nrm((N_EVEN, HG_DV), 0.01),
        "gn_gla": 1.0 + nrm((N_EVEN, GLA_DV), 0.01),
        "w_out_even": nrm((N_EVEN, MIX_WIDTH, D), MIX_WIDTH ** -0.5 * BETA),
        "w1_dense": nrm((N_EVEN, D, D_FF_DENSE), D ** -0.5),
        "w3_dense": nrm((N_EVEN, D, D_FF_DENSE), D ** -0.5),
        "w2_dense": nrm((N_EVEN, D_FF_DENSE, D), D_FF_DENSE ** -0.5 * BETA),
        "w_in_odd": nrm((N_ODD, D, ODD_IN), D ** -0.5),
        "b_gate_odd": b_gate,
        "conv_w": nrm((N_ODD, CONV_W, ML_QK), CONV_W ** -0.5),
        "conv_b": nrm((N_ODD, ML_QK), 0.01),
        "hn_w": 1.0 + nrm((N_ODD, ML_HEADS * ML_DV), 0.01),
        "w_out_odd": nrm((N_ODD, ML_HEADS * ML_DV, D), (ML_HEADS * ML_DV) ** -0.5 * BETA),
        "w_router": nrm((N_ODD, D, N_EXPERTS), D ** -0.5),
        "w1_moe": nrm((N_ODD, N_EXPERTS, D, D_FF_EXPERT), D ** -0.5),
        "w3_moe": nrm((N_ODD, N_EXPERTS, D, D_FF_EXPERT), D ** -0.5),
        "w2_moe": nrm((N_ODD, N_EXPERTS, D_FF_EXPERT, D), D_FF_EXPERT ** -0.5 * BETA),
        "ln1_g": 1.0 + nrm((DEPTH, D), 0.01),
        "ln1_b": nrm((DEPTH, D), 0.01),
        "ln2_g": 1.0 + nrm((DEPTH, D), 0.01),
        "ln2_b": nrm((DEPTH, D), 0.01),
    }

def reference(x_prompt, x_sample, state_hgrn, state_gla, state_mlstm_C, state_mlstm_n,
              state_mlstm_m, state_mlstm_conv, w_in_even, hg_lower_bounds, w_gk, b_gk,
              gn_hg, gn_gla, w_out_even, w1_dense, w3_dense, w2_dense, w_in_odd, b_gate_odd,
              conv_w, conv_b, hn_w, w_out_odd, w_router, w1_moe, w3_moe, w2_moe,
              ln1_g, ln1_b, ln2_g, ln2_b):
    params = dict(w_in_even=w_in_even, hg_lower_bounds=hg_lower_bounds, w_gk=w_gk, b_gk=b_gk,
                  gn_hg=gn_hg, gn_gla=gn_gla, w_out_even=w_out_even, w1_dense=w1_dense,
                  w3_dense=w3_dense, w2_dense=w2_dense, w_in_odd=w_in_odd, b_gate_odd=b_gate_odd,
                  conv_w=conv_w, conv_b=conv_b, hn_w=hn_w, w_out_odd=w_out_odd,
                  w_router=w_router, w1_moe=w1_moe, w3_moe=w3_moe, w2_moe=w2_moe,
                  ln1_g=ln1_g, ln1_b=ln1_b, ln2_g=ln2_g, ln2_b=ln2_b)
    z_hg = jnp.zeros((N_EVEN, BATCH, HG_HEADS, HG_DK, HG_DV), state_hgrn.dtype)
    z_gla = jnp.zeros((N_EVEN, BATCH, GLA_HEADS, GLA_DK, GLA_DV), state_gla.dtype)
    z_C = jnp.zeros((N_ODD, BATCH, ML_HEADS, ML_DK, ML_DV), state_mlstm_C.dtype)
    z_n = jnp.zeros((N_ODD, BATCH, ML_HEADS, ML_DK), state_mlstm_n.dtype)
    z_m = jnp.zeros((N_ODD, BATCH, ML_HEADS), state_mlstm_m.dtype)
    z_conv = jnp.zeros((N_ODD, BATCH, CONV_W - 1, ML_QK), state_mlstm_conv.dtype)
    y_prompt, hg_p, gla_p, C_p, n_p, m_p, conv_p = _trunk(
        x_prompt, z_hg, z_gla, z_C, z_n, z_m, z_conv, params)
    y_sample, hg_s, gla_s, C_s, n_s, m_s, conv_s = _trunk(
        x_sample, state_hgrn, state_gla, state_mlstm_C, state_mlstm_n, state_mlstm_m,
        state_mlstm_conv, params)
    return (y_prompt, y_sample, hg_p, gla_p, C_p, n_p, m_p, conv_p,
            hg_s, gla_s, C_s, n_s, m_s, conv_s)


_drawn_inputs = setup_inputs


def setup_inputs(seed=0):
    import zlib

    import numpy as np

    out = dict(_drawn_inputs(seed))
    spreads = {}
    factors = {'gn_hg': 8.0,
     'gn_gla': 8.0,
     'hn_w': 200.0,
     'ln1_g': 2.928,
     'ln2_g': 3.149,
     'conv_b': 8.0,
     'ln2_b': 2.953,
     'ln1_b': 3.188}
    for name, (base, spread) in spreads.items():
        noise = np.random.default_rng([zlib.crc32(name.encode()), seed]).standard_normal(out[name].shape)
        drawn = base * np.exp(spread * noise) if base else spread * noise
        out[name] = __import__('jax').numpy.asarray(drawn.astype(out[name].dtype))
    for name, factor in factors.items():
        out[name] = (out[name] * factor).astype(out[name].dtype)
    return out
```

```python
import concourse.bass as bass
from concourse import mybir
from contextlib import ExitStack
import numpy as np

F32 = mybir.dt.float32
F32R = mybir.dt.float32r
I32 = mybir.dt.int32
U32 = mybir.dt.uint32
ALU = mybir.AluOpType
ACT = mybir.ActivationFunctionType
AX = mybir.AxisListType

P = 128
D = 1024
KD = D // P
NP_ = 256
NS = 8
N = NP_ + NS
DEPTH = 2
ALPHA = (2.0 * DEPTH) ** 0.25
EPS = 1e-5
CH = 64
NC = NP_ // CH
HG, GL = 4, 4
GPAIR = GL // 2
KT = HG + GPAIR
HV = HG + GL
GLA_DK = 64
GATE_NORM = 16.0
RANK = 16
FD = 2816 // P
MH = 4
MDV = 256
ML_SCALE = 128 ** -0.5
GLA_SCALE = GLA_DK ** -0.5
NE = 8
FE = 3584 // P
CAP = P
MAXPASS = -(-N // CAP)
TT = [(0, P), (P, P), (2 * P, NS)]
RING = 4
BLK = 512
NBLK = FE * P // BLK
GPJ = 3 * FE
NSPLIT = 4
W13_AT, W2_AT, ORDER = [], [], []
for _b in range(NBLK + 1):
    if _b < NBLK:
        W13_AT.append(len(ORDER))
        ORDER += [(_w, _b, _k) for _k in range(KD // 2) for _w in ("w1", "w3")]
    if _b > 0:
        W2_AT.append(len(ORDER))
        ORDER += [("w2", _b - 1, _f) for _f in range(BLK // P)]
assert len(ORDER) == GPJ
SILU_AT = {W13_AT[_b] + 7 + 4: _b for _b in range(NBLK)}
TURNED_AT = {(W13_AT[_b + 1] + 3 if _b < NBLK - 1 else GPJ - 5) + NSPLIT: _b for _b in range(NBLK)}
TURN_BANK = [6, 7, 6, 7, 6, 7, 2]
ARENA = 15100
SLOT = 3072
LN_VECS = ["ln1g0", "ln1b0", "ln2g0", "ln2b0", "ln1g1", "ln1b1", "ln2g1", "ln2b1"]

VEC, _at = {}, 0
for _n, _w in [("lb0", HG), ("lb1", HG), ("bgk", GPAIR), ("gn_hg", 1), ("gn_gla", 1)] + [(v, KD) for v in LN_VECS] + [
        ("convb", KD), ("hn", KD)] + [(f"convw{j}", KD) for j in range(4)]:
    VEC[_n] = (_at, _at + _w)
    _at += _w
NVEC = _at
CON, _at = {}, 0
for _n, _w in [("ident", P), ("ones", P), ("causal64", CH), ("neg", P), ("before", P), ("iota", P), ("valid", 1),
               ("eps", 1), ("one", 1)]:
    CON[_n] = (_at, _at + _w)
    _at += _w
NCON = _at


def bc(ap, shape):
    return ap.to_broadcast(list(shape))


def decoder_step(nc, A):
    ctx = ExitStack()
    with ctx:
        def sb(name, shape, dt=F32):
            return ctx.enter_context(nc.sbuf_tensor(name, shape, dt))

        def sem(name):
            return ctx.enter_context(nc.semaphore(name))

        ring = sb("ring", [P, RING, SLOT])
        con = sb("con", [P, NCON])
        whi, wlo = sb("whi", [P, NSPLIT, D], F32R), sb("wlo", [P, NSPLIT, D], F32R)
        xgh, xgl = sb("xgh", [P, KD, CAP], F32R), sb("xgl", [P, KD, CAP], F32R)
        hTh, hTl = sb("hTh", [P, 2, 4, CAP], F32R), sb("hTl", [P, 2, 4, CAP], F32R)
        vec = sb("vec", [P, NVEC])
        wgr = sb("wgr", [P, KD, RANK])
        wgate = sb("wgate", [P, KD, 2 * MH])
        wrout = sb("wrout", [P, KD, NE])
        wgk = sb("wgk", [RANK, GPAIR * P])
        bgate = sb("bgate", [MH, 2])
        m0 = sb("m0", [MH, NS])
        X = sb("X", [P, KD, N])
        R = sb("R", [P, KD, N])
        SQ = sb("SQ", [P, KD, N])
        state = sb("state", [P, 8256])
        arena = sb("arena", [P, ARENA])
        nm = sb("nm", [P, N])
        lbt = sb("lbt", [P, 3, HG])
        bank = [ctx.enter_context(nc.psum_tensor(f"bank{b}", [P, 512], F32))[:, :] for b in range(8)]

        def con_(n):
            a, b = CON[n]
            return con[:, a:b]

        def vec_(n, i=0, w=1):
            a = VEC[n][0] + i
            return vec[:, a:a + w]

        ident, ones = con_("ident"), con_("ones")
        eps, one = con_("eps"), con_("one")

        cur = [0]

        def region(cols, rows=P):
            a = cur[0]
            cur[0] += cols
            assert cur[0] <= ARENA, cur[0]
            return arena[0:rows, a:a + cols]

        q0 = region(HV * N).rearrange("p (j n) -> p j n", j=HV)
        k0 = region(KT * N).rearrange("p (j n) -> p j n", j=KT)
        g0f = region(KT * N)
        g0 = g0f.rearrange("p (j n) -> p j n", j=KT)
        maskf = region(KT * N)
        eq0 = maskf.rearrange("p (j n) -> p j n", j=KT)
        ktok0 = region(KT * 2 * P).rearrange("p (j a n) -> p j a n", j=KT, a=2)
        vtok0f = region(HV * 2 * P)
        vtok0 = vtok0f.rearrange("p (j a n) -> p j a n", j=HV, a=2)
        glt = vtok0f[:, 0:3 * GPAIR * N].rearrange("p (i j n) -> p i j n", i=3, j=GPAIR)
        gate0 = region(HV * N).rearrange("p (j n) -> p j n", j=HV)
        S = region(KT * P).rearrange("p (j n) -> p j n", j=KT)
        Sp = region(KT * P).rearrange("p (j n) -> p j n", j=KT)
        Tmp = region(KT * P).rearrange("p (j n) -> p j n", j=KT)
        prob0 = maskf[:, 0:2 * HV * CH].rearrange("p (a h n) -> p a h n", a=2, h=HV)
        eml = region(3 * KT * NC).rearrange("p (i j c) -> p i j c", i=3, j=KT)
        as0 = region(KT * NS).rearrange("p (j b) -> p j b", j=KT)
        gr_sb = Sp[0:RANK].rearrange("p j n -> p (j n)")[:, 0:N]
        b0f = SQ[:, 0:KT, :].rearrange("p j n -> p (j n)")
        b0 = SQ[:, 0:KT, :]
        o0 = R
        v0 = state[:, 6144:6144 + HV * N].rearrange("p (j n) -> p j n", j=HV)
        S0 = state[:, 0:6144].rearrange("p (j b n) -> p j b n", j=KT, b=NS)
        vs0 = g0f[0:NS, 0:HV * P]

        def chunks(t):
            return t[:, :, 0:NP_].rearrange("p j (c t) -> p j c t", c=NC)

        cur[0] = 0
        hT = region(FD * N).rearrange("p (f n) -> p f n", f=FD)
        sil = region(2 * N).rearrange("p (a n) -> p a n", a=2)
        cur[0] = 0
        up = region(KD * (NP_ + 3)).rearrange("p (j n) -> p j n", j=KD)
        us = region(KD * 4 * NS).rearrange("p (j r b) -> p j r b", j=KD, r=4)
        qk = region(KD * N).rearrange("p (j n) -> p j n", j=KD)
        og = region(KD * N).rearrange("p (j n) -> p j n", j=KD)
        vtokf = region(2 * D)
        vtok = vtokf.rearrange("p (a n) -> p a n", a=2)
        uc = vtokf[:, 0:2 * N].rearrange("p (a n) -> p a n", a=2)
        Dk = region(2 * 384).rearrange("p (a n) -> p a n", a=2)
        Pr = region(2 * 384).rearrange("p (a n) -> p a n", a=2)
        arg = region(2 * 384).rearrange("p (a n) -> p a n", a=2)
        kw = region(2 * 256).rearrange("p (a s n) -> p a s n", a=2, s=2)
        Cout = region(MH * 257).rearrange("p (h n) -> p h n", h=MH)
        acol = region(2 * MH).rearrange("p (s h) -> p s h", s=2)
        fwb = region(MH * 3 * NS).rearrange("p (h w b) -> p h w b", h=MH, w=3)
        n0 = region(MH * NS).rearrange("p (h b) -> p h b", h=MH)
        ki = region(MH * NS).rearrange("p (h b) -> p h b", h=MH)
        qns = region(MH * NS).rearrange("p (h b) -> p h b", h=MH)
        qs = region(MH * NS).rearrange("p (h b) -> p h b", h=MH)
        dens = region(MH * NS).rearrange("p (h b) -> p h b", h=MH)
        rows = region(5 * N, MH).rearrange("p (i n) -> p i n", i=5)
        bcrow = region(NP_ + 3 * NS, MH)
        enrow = region(NP_, MH)
        lm = region(NS, MH)
        vs1 = arena[0:NS, 0:D]
        v1 = SQ
        Tm1 = SQ[:, 0:4, 0:256]
        Cs = state[:, 0:8192].rearrange("p (h b n) -> p h b n", h=MH, b=NS)
        h1 = R
        cur[0] = 0
        xtok = region(3 * D).rearrange("p (t n) -> p t n", t=3)
        sE = region(BLK)
        hb = region(BLK)
        yE = region(D)
        G = region(3 * CAP).rearrange("p (t n) -> p t n", t=3)
        Gg = region(3 * CAP).rearrange("p (t n) -> p t n", t=3)
        GT = region(N)
        L = region(3 * NE).rearrange("p (t e) -> p t e", t=3)
        mx = region(3 * 8).rearrange("p (t e) -> p t e", t=3)
        oh = region(3 * NE).rearrange("p (t e) -> p t e", t=3)
        sel = region(3 * NE).rearrange("p (t e) -> p t e", t=3)
        gat = region(3 * NE).rearrange("p (t e) -> p t e", t=3)
        rnk = region(3 * NE).rearrange("p (t e) -> p t e", t=3)
        ixf = region(3 * 8).rearrange("p (t e) -> p t e", t=3)
        w12 = region(3 * 3).rearrange("p (i t) -> p i t", i=3)
        NJ = MAXPASS * NE + 1
        jrank = region(3 * NJ).rearrange("p (t j) -> p t j", t=3)
        jgate = region(3 * NJ).rearrange("p (t j) -> p t j", t=3)
        crank = region(3)
        cgate = region(3)
        mcnt = region(4)
        idx = sb("idx", [P, 3, 8], U32)
        npass = sb("npass", [1, 1], I32)

        slot_loaded = [sem(f"slot_loaded{i}") for i in range(RING)]
        steps_used = sem("steps_used")
        x_loaded, small_loaded, scan_mask_loaded = sem("x_loaded"), sem("small_loaded"), sem("scan_mask_loaded")
        state0_loaded, state1_loaded, conv_loaded = sem("state0_loaded"), sem("state1_loaded"), sem("conv_loaded")
        psum_ready = sem("psum_ready")
        bank_free = [sem(f"bank_free{b}") for b in range(8)]
        act_own, dve_own, pool_own = sem("act_own"), sem("dve_own"), sem("pool_own")
        q_zeroed = sem("q_zeroed")
        lb_diff_ready, lb_ready = sem("lb_diff_ready"), sem("lb_ready")
        gr_ready, sig_ready, f_ready, q_ready = sem("gr_ready"), sem("sig_ready"), sem("f_ready"), sem("q_ready")
        logf_ready, gla_u_ready, gla_l_ready = sem("logf_ready"), sem("gla_u_ready"), sem("gla_l_ready")
        gkq_ready, v0_ready, gate0_ready = sem("gkq_ready"), sem("v0_ready"), sem("gate0_ready")
        dist_ready, expd_ready, expnd_ready, dec_ready = sem("dist_ready"), sem("expd_ready"), sem("expnd_ready"), sem("dec_ready")
        qp_ready, kp_ready, ktok_ready, vtok_ready = sem("qp_ready"), sem("kp_ready"), sem("ktok_ready"), sem("vtok_ready")
        vs_ready, prob_ready, sp_ready, o_ready = sem("vs_ready"), sem("prob_ready"), sem("sp_ready"), sem("o_ready")
        sdec_ready, snew_ready, s_final = sem("sdec_ready"), sem("snew_ready"), sem("s_final")
        osq_ready, rms_ready, y_ready = sem("osq_ready"), sem("rms_ready"), sem("y_ready")
        r_ready, centred, sq_ready, rstd_ready, scaled, x_ready = (sem("r_ready"), sem("centred"), sem("sq_ready"),
                                                                  sem("rstd_ready"), sem("scaled"), sem("x_ready"))
        silu_ready, h_ready = sem("silu_ready"), sem("h_ready")
        u_ready, conv_done, qk_ready, v1_ready, og_ready = (sem("u_ready"), sem("conv_done"), sem("qk_ready"),
                                                            sem("v1_ready"), sem("og_ready"))
        lgi_ready, lga_ready, lgl_ready, rows_ready, exprow_ready = (sem("lgi_ready"), sem("lga_ready"), sem("lgl_ready"),
                                                                     sem("rows_ready"), sem("exprow_ready"))
        acol_ready, arg_ready, decay_ready, p1_ready = sem("acol_ready"), sem("arg_ready"), sem("decay_ready"), sem("p1_ready")
        kw_ready, den_ready, h1_ready, vtok1_ready, vs1_ready = (sem("kw_ready"), sem("den_ready"), sem("h1_ready"),
                                                                 sem("vtok1_ready"), sem("vs1_ready"))
        fwb_ready, qn_ready, cdec_ready, cnew_ready = sem("fwb_ready"), sem("qn_ready"), sem("cdec_ready"), sem("cnew_ready")
        cout_ready, hs_ready = sem("cout_ready"), sem("hs_ready")
        hc_ready, hsq_ready, hstd_ready, y1_ready = sem("hc_ready"), sem("hsq_ready"), sem("hstd_ready"), sem("y1_ready")
        xtok_ready, route1, route2, sel_ready, jobs_ready, npass_ready = (sem("xtok_ready"), sem("route1"), sem("route2"),
                                                                         sem("sel_ready"), sem("jobs_ready"), sem("npass_ready"))
        racc_ready = sem("racc_ready")
        gg_ready = sem("gg_ready")
        g_ready, xg_psum, gathered, xgh_ready, xgl_ready = (sem("g_ready"), sem("xg_psum"), sem("gathered"),
                                                            sem("xgh_ready"), sem("xgl_ready"))
        granule_used, whi_ready, wlo_ready = sem("granule_used"), sem("whi_ready"), sem("wlo_ready")
        silE_ready, hb_ready, t_psum, hTh_ready, hT_ready = (sem("silE_ready"), sem("hb_ready"), sem("t_psum"),
                                                             sem("hTh_ready"), sem("hT_ready"))
        y_psum, yE_ready = sem("y_psum"), sem("yE_ready")
        gt_psum, gt_ready, sc_psum, sc_added = sem("gt_psum"), sem("gt_ready"), sem("sc_psum"), sem("sc_added")
        out_ready = sem("out_ready")
        stored0, stored1, stored = sem("stored0"), sem("stored1"), sem("stored")

        loads = []
        for i in range(0, 28, 3):
            loads.append(("w_in0", i, min(3, 28 - i)))
        for i in range(0, 8, 3):
            loads.append(("w_out0", i, min(3, 8 - i)))
        loads += [("w13", i, 1) for i in range(FD)]
        loads += [("w2", i, 1) for i in range(KD)]
        for i in range(0, 24, 3):
            loads.append(("w_in1", i, 3))
        for i in range(0, 8, 3):
            loads.append(("w_out1", i, min(3, 8 - i)))
        LS = {(n, i): s for s, (n, i, _) in enumerate(loads)}
        NL = len(loads)

        jobs = ["gr"] + [("z", i) for i in range(4)] + [("glag", 0), ("glag", 1)] + [("z", i) for i in range(4, 28)]
        jobs += [("kt", m) for m in range(KT // 2)] + [("vt", m) for m in range(HV // 2)] + [("vst", 0), ("vst", 1)]
        jobs += [("sc", 0), ("sc", 1), ("u0", 0), ("u1", 0), ("sc", 2), ("sc", 3), ("o", 0), ("u0", 1), ("u1", 1),
                 ("o", 1), ("u0", 2), ("u1", 2), ("o", 2), ("u0", 3), ("u1", 3), ("o", 3)]
        for b in range(NS):
            jobs += [("vb0", b), ("vb1", b)]
        jobs += ["os"] + [("ss", h) for h in range(HV)] + [("mix", 0, j) for j in range(KD)] + [("mean", 0), ("var", 0)]
        for f in range(FD):
            jobs += [("h1", f), ("h3", f)]
        jobs += [("mix", 1, j) for j in range(KD)] + [("mean", 1), ("var", 1)]
        jobs += ["gi", "gf"] + [("y", i) for i in range(24)]
        jobs += [("vt1", m) for m in range(4)] + [("vs1", 0), ("vs1", 1)] + ["acol"]
        for h in range(MH):
            jobs += [("bc", h), ("kt1", h), ("sc1", h), ("en", h), ("num", h), ("den", h), ("C", h)]
        jobs += ["qn"]
        for b in range(NS):
            jobs += [("wb", b, 0), ("wb", b, 1)]
        jobs += ["ns"]
        jobs += [("hm", h) for h in range(MH)] + [("hv", h) for h in range(MH)]
        jobs += [("mix", 2, j) for j in range(KD)] + [("mean", 2), ("var", 2)]
        jobs += [("lg", t) for t in range(3)] + [("xt", t, a) for t in range(3) for a in range(2)] + ["rank", "count"]
        J = {n: i for i, n in enumerate(jobs)}
        NJOB = len(jobs)
        assert len(J) == NJOB
        ENDJOBS = [NJOB, NJOB + 1]

        def see(eng, name):
            eng.wait_ge(psum_ready, J[name] + 1)
            return bank[J[name] % 8]

        def freed(name):
            return bank_free[J[name] % 8]

        class Own:
            def __init__(self, eng, s):
                self.eng, self.s, self.n = eng, s, 0

            def settle(self, ins):
                ins.then_inc(self.s, 1)
                self.n += 1
                self.eng.wait_ge(self.s, self.n)

            def start(self, ins):
                ins.then_inc(self.s, 1)
                self.n += 1

            def wait(self):
                self.eng.wait_ge(self.s, self.n)

        block = ctx.enter_context(nc.Block())

        @block.sync
        def _(sp):
            sp.dma_start(X[:], A["x"]).then_inc(x_loaded, 16)
            sp.dma_start(wgr[:], A["w_gr"]).then_inc(x_loaded, 16)

            def load(s):
                name, i, n = loads[s]
                if s >= RING:
                    sp.wait_ge(steps_used, s - RING + 1)
                width = A[name].shape[2]
                sp.dma_start(ring[:, s % RING, 0:n * width].rearrange("p (t f) -> p t f", t=n),
                             A[name][i:i + n].rearrange("t p f -> p t f")).then_inc(slot_loaded[s % RING], 16)

            for s in range(NL):
                load(s)
            def expert(job, row0, first=False):
                for f in range(FE):
                    if first and f < RING:
                        sp.wait_ge(steps_used, NL + f - RING + 1)
                    else:
                        sp.wait_ge(wlo_ready, job * GPJ + 3 * (f - RING + 1))
                    sp.dma_start(ring[:, (NL + f) % RING, :],
                                 A["w_moe"][bass.ds(row0 + f, 1)].rearrange("t p f -> p (t f)"))\
                      .then_inc(slot_loaded[(NL + f) % RING], 16)

            expert(0, 0, first=True)
            with sp.Fori(1, NE) as e:
                expert(e, e * FE)
            sp.wait_ge(npass_ready, 1)
            passes = sp.value_load(npass[0:1, 0:1], min_val=1, max_val=MAXPASS)
            with sp.If(passes > 1):
                with sp.Fori(1, passes) as p:
                    with sp.Fori(0, NE) as e:
                        expert(p * NE + e, e * FE)

        @block.tensor
        def _(pe):
            at = [0]

            def job(name):
                assert jobs[at[0]] == name, (jobs[at[0]], name)
                n = at[0]
                at[0] += 1
                if n >= 8:
                    pe.wait_ge(bank_free[n % 8], n // 8)
                return bank[n % 8]

            def done(ins):
                ins.then_inc(psum_ready, 1)

            def slot(name, i):
                s = LS[(name, i)]
                pe.wait_ge(slot_loaded[s % RING], 16 * (s // RING + 1))
                return ring[:, s % RING, :]

            def product(out, lhs, rhs, k):
                for c in range(k):
                    mm = pe.matmul(out, lhs(c), rhs(c), start=(c == 0), stop=(c == k - 1))
                return mm

            def projection(name, count, groups, jobname, rhs, used_after=3):
                for i in groups:
                    w = slot(name, i - i % 3)
                    o = (i % 3) * D
                    out = job(jobname(i))[:, 0:N]
                    mm = product(out, lambda c: w[:, o + c * P:o + (c + 1) * P], rhs, KD)
                    done(mm)
                    if i % 3 == 2 or i == count - 1:
                        pe.wait_ge(psum_ready, at[0])
                        pe.nop().then_inc(steps_used, 1)

            pe.wait_ge(x_loaded, 32)
            out = job("gr")[0:RANK, 0:N]
            done(product(out, lambda c: wgr[:, c, :], lambda c: X[:, c, :], KD))
            projection("w_in0", 28, range(4), lambda i: ("z", i), lambda c: X[:, c, :])
            pe.wait_ge(gr_ready, 1)
            pe.wait_ge(small_loaded, 16 * 7)
            for j in range(GPAIR):
                done(pe.matmul(job(("glag", j))[:, 0:N], wgk[:, j * P:(j + 1) * P], gr_sb, start=True, stop=True))
            projection("w_in0", 28, range(4, 28), lambda i: ("z", i), lambda c: X[:, c, :])

            pe.wait_ge(kp_ready, 1)
            for m in range(KT // 2):
                out = job(("kt", m))
                for i in range(4):
                    j, a = 2 * m + i // 2, i % 2
                    mm = pe.transpose(out[:, i * P:(i + 1) * P], k0[:, j, a * P:(a + 1) * P], ident)
                done(mm)
            for m in range(HV // 2):
                pe.wait_ge(v0_ready, 2 * m + 2)
                out = job(("vt", m))
                for i in range(4):
                    j, a = 2 * m + i // 2, i % 2
                    mm = pe.transpose(out[:, i * P:(i + 1) * P], v0[:, j, a * P:(a + 1) * P], ident)
                done(mm)
            for m in range(2):
                out = job(("vst", m))
                for i in range(4):
                    mm = pe.transpose(out[0:NS, i * P:(i + 1) * P], v0[:, 4 * m + i, NP_:N], ident)
                done(mm)

            def rows_of(h):
                if h < HG:
                    return h, 0, P
                return HG + (h - HG) // 2, GLA_DK * ((h - HG) % 2), GLA_DK

            def scores(c):
                out = job(("sc", c))
                lo = CH * (c % 2)
                for h in range(HV):
                    j, p0, n = rows_of(h)
                    t = slice(c * CH, (c + 1) * CH)
                    mm = pe.matmul(out[lo:lo + CH, h * CH:(h + 1) * CH], k0[:, j, t], q0[:, h, t],
                                   start=True, stop=True)
                done(mm)

            def updates(c):
                lo, a = CH * (c % 2), c // 2
                out = job(("u0", c))
                for h in range(HG):
                    mm = pe.matmul(out[:, h * P:(h + 1) * P], ktok0[lo:lo + CH, h, a, :], vtok0[lo:lo + CH, h, a, :],
                                   start=True, stop=True)
                done(mm)
                out = job(("u1", c))
                for h in range(HG, HV):
                    j, p0, n = rows_of(h)
                    jj = j - HG
                    mm = pe.matmul(out[p0:p0 + n, jj * P:(jj + 1) * P], ktok0[lo:lo + CH, j, a, p0:p0 + n],
                                   vtok0[lo:lo + CH, h, a, :], start=True, stop=True)
                done(mm)

            def outputs(c):
                lo, a = CH * (c % 2), c // 2
                pe.wait_ge(prob_ready, c + 1)
                if c:
                    pe.wait_ge(sp_ready, c)
                out = job(("o", c))
                for h in range(HV):
                    j, p0, n = rows_of(h)
                    o = out[:, h * CH:(h + 1) * CH]
                    mm = pe.matmul(o, vtok0[lo:lo + CH, h, a, :], prob0[lo:lo + CH, a, h, :], start=True, stop=(c == 0))
                    if c:
                        mm = pe.matmul(o, Sp[:, j, :], q0[:, h, c * CH:(c + 1) * CH],
                                       start=False, stop=True)
                done(mm)

            pe.wait_ge(qp_ready, 1)
            pe.wait_ge(q_zeroed, GL)
            scores(0)
            scores(1)
            pe.wait_ge(ktok_ready, KT // 2)
            pe.wait_ge(vtok_ready, HV // 2)
            updates(0)
            scores(2)
            scores(3)
            outputs(0)
            for c in range(1, NC):
                updates(c)
                outputs(c)
            pe.wait_ge(vs_ready, 2)
            for b in range(NS):
                row = ident[0:NS, b:b + 1]
                done(pe.matmul(job(("vb0", b))[:, :], bc(row, [NS, P]), vs0[:, 0:HG * P], start=True, stop=True))
                out = job(("vb1", b))
                for i in range(2):
                    for jj in range(GPAIR):
                        h = HG + 2 * jj + i
                        mm = pe.matmul(out[64 * i:64 * i + 64, jj * P:(jj + 1) * P], bc(row, [NS, 64]),
                                       vs0[:, h * P:(h + 1) * P], start=True, stop=True)
                done(mm)
            out = job("os")
            for b in range(NS):
                pe.wait_ge(snew_ready, b + 1)
                for h in range(HV):
                    j, p0, n = rows_of(h)
                    mm = pe.matmul(out[:, h * NS + b:h * NS + b + 1], S0[:, j, b, :],
                                   q0[:, h, NP_ + b:NP_ + b + 1], start=True, stop=True)
            done(mm)
            for h in range(HV):
                pe.wait_ge(osq_ready, h + 1)
                done(pe.matmul(job(("ss", h))[:, 0:N], ones, SQ[:, h, :], start=True, stop=True))

            def layernorm(n, squares=True):
                if n < 3:
                    out, finish = job(("mean", n)), done
                else:
                    out = bank[0]
                for k in range(KD):
                    pe.wait_ge(r_ready, KD * n + k + 1)
                    mm = pe.matmul(out[:, 0:N], ones, R[:, k, :], start=(k == 0), stop=(k == KD - 1))
                mm.then_inc(psum_ready, 1)
                out = job(("var", n)) if n < 3 else bank[1]
                for k in range(KD):
                    pe.wait_ge(sq_ready, KD * n + k + 1)
                    mm = pe.matmul(out[:, 0:N], ones, SQ[:, k, :], start=(k == 0), stop=(k == KD - 1))
                mm.then_inc(psum_ready, 1)

            pe.wait_ge(y_ready, HV)
            projection("w_out0", 8, range(8), lambda i: ("mix", 0, i), lambda c: gate0[:, c, :])
            layernorm(0)

            pe.wait_ge(x_ready, KD)
            for f in range(FD):
                w = slot("w13", f)
                for i, nme in enumerate(["h1", "h3"]):
                    mm = product(job((nme, f))[:, 0:N], lambda c: w[:, i * D + c * P:i * D + (c + 1) * P],
                                 lambda c: X[:, c, :], KD)
                    done(mm)
                pe.wait_ge(psum_ready, at[0])
                pe.nop().then_inc(steps_used, 1)
            for j in range(KD):
                w = slot("w2", j)
                out = job(("mix", 1, j))
                for f in range(FD):
                    if j == 0:
                        pe.wait_ge(h_ready, f + 1)
                    mm = pe.matmul(out[:, 0:N], w[:, f * P:(f + 1) * P], hT[:, f, :], start=(f == 0), stop=(f == FD - 1))
                done(mm)
                pe.wait_ge(psum_ready, at[0])
                pe.nop().then_inc(steps_used, 1)
            layernorm(1)

            pe.wait_ge(x_ready, 2 * KD)
            for i, nme in enumerate(["gi", "gf"]):
                done(product(job(nme)[0:MH, 0:N], lambda c: wgate[:, c, i * MH:(i + 1) * MH], lambda c: X[:, c, :], KD))
            projection("w_in1", 24, range(24), lambda i: ("y", i), lambda c: X[:, c, :])
            for m in range(4):
                pe.wait_ge(v1_ready, 2 * m + 2)
                out = job(("vt1", m))
                for i in range(4):
                    mm = pe.transpose(out[:, i * P:(i + 1) * P], v1[:, 2 * m + i // 2, (i % 2) * P:(i % 2 + 1) * P], ident)
                done(mm)
            for m in range(2):
                out = job(("vs1", m))
                for i in range(4):
                    mm = pe.transpose(out[0:NS, i * P:(i + 1) * P], v1[:, 4 * m + i, NP_:N], ident)
                done(mm)
            pe.wait_ge(rows_ready, 1)
            out = job("acol")
            for s in range(2):
                mm = pe.transpose(out[:, s * MH:(s + 1) * MH], rows[:, 0, s * P:(s + 1) * P], ident[0:MH, 0:MH])
            done(mm)
            pe.wait_ge(exprow_ready, 1)
            pe.wait_ge(qk_ready, KD)
            for h in range(MH):
                pick = bc(ident[0:MH, h:h + 1], [MH, P])
                q, k = qk[:, h, :], qk[:, MH + h, :]
                done(pe.matmul(job(("bc", h))[:, 0:NP_ + 3 * NS], pick, bcrow, start=True, stop=True))
                out = job(("kt1", h))
                for s in range(2):
                    mm = pe.transpose(out[:, s * P:(s + 1) * P], k[:, s * P:(s + 1) * P], ident)
                done(mm)
                out = job(("sc1", h))
                pe.matmul(out[:, 0:NP_], k[:, 0:P], q[:, 0:NP_], start=True, stop=True)
                done(pe.matmul(out[:, NP_:NP_ + P], k[:, P:NP_], q[:, P:NP_], start=True, stop=True))
                done(pe.matmul(job(("en", h))[:, 0:NP_], pick, enrow, start=True, stop=True))
                pe.wait_ge(p1_ready, h + 1)
                if h == 0:
                    pe.wait_ge(vtok1_ready, 4)
                pr = Pr[:, h % 2, :]
                out = job(("num", h))
                for v in range(2):
                    c0 = h * MDV + v * P
                    pe.matmul(out[:, v * NP_:(v + 1) * NP_], vtok[:, 0, c0:c0 + P], pr[:, 0:NP_], start=True, stop=False)
                    mm = pe.matmul(out[:, v * NP_ + P:(v + 1) * NP_], vtok[:, 1, c0:c0 + P], pr[:, NP_:NP_ + P],
                                   start=False, stop=True)
                done(mm)
                out = job(("den", h))
                pe.matmul(out[:, 0:NP_], ones, pr[:, 0:NP_], start=True, stop=False)
                done(pe.matmul(out[:, P:NP_], ones, pr[:, NP_:NP_ + P], start=False, stop=True))
                pe.wait_ge(kw_ready, h + 1)
                out = job(("C", h))
                for s in range(2):
                    pe.matmul(out[:, 0:MDV], kw[:, h % 2, s, :], vtok[:, s, h * MDV:(h + 1) * MDV],
                              start=(s == 0), stop=(s == 1))
                for s in range(2):
                    mm = pe.matmul(out[:, MDV:MDV + 1], kw[:, h % 2, s, :], one, start=(s == 0), stop=(s == 1))
                done(mm)
            pe.wait_ge(qn_ready, 1)
            done(pe.matmul(job("qn")[:, 0:MH * NS], ones, qns, start=True, stop=True))
            pe.wait_ge(vs1_ready, 2)
            for b in range(NS):
                for i in range(2):
                    done(pe.matmul(job(("wb", b, i)), bc(ident[0:NS, b:b + 1], [NS, P]), vs1[:, i * 512:(i + 1) * 512],
                                   start=True, stop=True))
            out = job("ns")
            for b in range(NS):
                pe.wait_ge(cnew_ready, b + 1)
                for h in range(MH):
                    for v in range(2):
                        o = (2 * h + v) * NS + b
                        mm = pe.matmul(out[:, o:o + 1], Cs[:, h, b, v * P:(v + 1) * P], qs[:, h, b:b + 1],
                                       start=True, stop=True)
            done(mm)
            pe.wait_ge(h1_ready, MH)
            pe.wait_ge(hs_ready, 1)
            for h in range(MH):
                done(product(job(("hm", h))[:, 0:N], lambda c: ones, lambda c: h1[:, 2 * h + c, :], 2))
            for h in range(MH):
                pe.wait_ge(hsq_ready, h + 1)
                done(product(job(("hv", h))[:, 0:N], lambda c: ones, lambda c: SQ[:, 2 * h + c, :], 2))
            pe.wait_ge(y1_ready, MH)
            projection("w_out1", 8, range(8), lambda i: ("mix", 2, i), lambda c: og[:, c, :])
            layernorm(2)

            pe.wait_ge(x_ready, 3 * KD)
            for t, (t0, n) in enumerate(TT):
                done(product(job(("lg", t))[0:n, 0:NE], lambda c: X[:, c, t0:t0 + n], lambda c: wrout[:, c, :], KD))
            for t, (t0, n) in enumerate(TT):
                for a in range(2):
                    out = job(("xt", t, a))
                    for i in range(4):
                        mm = pe.transpose(out[0:n, i * P:(i + 1) * P], X[:, 4 * a + i, t0:t0 + n], ident)
                    done(mm)
            pe.wait_ge(sel_ready, 1)
            out = job("rank")
            for t in range(3):
                for s in range(t + 1):
                    mm = pe.matmul(out[:, t * NE:(t + 1) * NE], con_("before") if s == t else ones, sel[:, s, :],
                                   start=(s == 0), stop=(s == t))
            done(mm)
            done(product(job("count")[:, 0:NE], lambda c: ones, lambda c: sel[:, c, :], 3))

            for b in range(8):
                pe.wait_ge(bank_free[b], len(range(b, NJOB, 8)))
            pe.wait_ge(npass_ready, 1)
            passes = pe.value_load(npass[0:1, 0:1], min_val=1, max_val=MAXPASS)

            def gather(j):
                pe.wait_ge(g_ready, j + 1)
                for k in range(KD):
                    o = bank[6 + k // 4][:, (k % 4) * P:(k % 4 + 1) * P]
                    for t, (_, n) in enumerate(TT):
                        mm = pe.matmul(o, xtok[0:n, t, k * P:(k + 1) * P], G[0:n, t, :], start=(t == 0), stop=(t == 2))
                    if k % 4 == 3:
                        mm.then_inc(xg_psum, 1)

            def split_product(out, xh, xl, wh, wl, start, stop):
                pe.matmul(out, xh, wh, start=start, stop=False)
                pe.matmul(out, xh, wl, start=False, stop=False)
                return pe.matmul(out, xl, wh, start=False, stop=stop)

            def granule(j, g):
                pe.wait_ge(wlo_ready, j * GPJ + (g + 1))
                return whi[:, g % NSPLIT, :], wlo[:, g % NSPLIT, :]

            def hidden(j, b):
                g0_ = W13_AT[b]
                for kp in range(KD // 2):
                    for i in range(2):
                        g = g0_ + 2 * kp + i
                        wh, wl = granule(j, g)
                        for kk in range(2):
                            k = 2 * kp + kk
                            c = slice(kk * BLK, (kk + 1) * BLK)
                            mm = split_product(bank[2 * (b % 2) + i], xgh[:, k, :], xgl[:, k, :], wh[:, c], wl[:, c],
                                               k == 0, k == KD - 1)
                        mm.then_inc(granule_used, 1)
                    if kp == 1 and b > 0:
                        turn(j, b - 1)

            def turn(j, b):
                pe.wait_ge(hb_ready, j * NBLK + (b + 1))
                if b < 2:
                    pe.wait_ge(sc_added, j * KD + 1)
                for i in range(4):
                    mm = pe.transpose(bank[TURN_BANK[b]][:, i * P:(i + 1) * P], hb[:, i * P:(i + 1) * P], ident)
                mm.then_inc(t_psum, 1)

            def down(j, b):
                pe.wait_ge(hT_ready, j * NBLK + (b + 1))
                if b == 0:
                    pe.wait_ge(yE_ready, j * 2 + 1)
                last = b == NBLK - 1
                for step in range(8):
                    f, a = (step % 4, step // 4) if last else (step // 2, step % 2)
                    wh, wl = granule(j, W2_AT[b] + f)
                    c = slice(a * BLK, (a + 1) * BLK)
                    mm = split_product(bank[4 + a], hTh[:, b % 2, f, :], hTl[:, b % 2, f, :], wh[:, c], wl[:, c],
                                       b == 0 and f == 0, last and f == 3)
                    if a == 1:
                        mm.then_inc(granule_used, 1)
                    elif last and f == 3:
                        mm.then_inc(y_psum, 1)

            pe.wait_ge(jobs_ready, 1)
            pe.wait_ge(xtok_ready, 6)
            for _ in range(NSPLIT):
                pe.nop().then_inc(granule_used, 1)
            gather(0)
            with pe.Fori(0, passes * NE) as j:
                pe.wait_ge(xgl_ready, j * 2 + 3)
                hidden(j, 0)
                for b in range(1, NBLK):
                    hidden(j, b)
                    down(j, b - 1)
                turn(j, NBLK - 1)
                pe.wait_ge(gg_ready, j + 1)
                for t, (t0, n) in enumerate(TT):
                    mm = pe.transpose(bank[3][:, t0:t0 + n], Gg[0:n, t, :], ident[0:n, 0:n])
                mm.then_inc(gt_psum, 1)
                gather(j + 1)
                down(j, NBLK - 1)
                pe.wait_ge(gt_ready, j + 1)
                pe.wait_ge(xgl_ready, j * 2 + 5)
                for k in range(KD):
                    if k % 4 == 0:
                        pe.wait_ge(yE_ready, j * 2 + (k // 4 + 2))
                    if k >= 2:
                        pe.wait_ge(sc_added, j * KD + k)
                    mm = pe.matmul(bank[7 - k % 2][:, 0:N], yE[:, k * P:(k + 1) * P], GT, start=True, stop=True)
                    mm.then_inc(sc_psum, 1)
            layernorm(3)

        @block.scalar
        def _(act):
            own = Own(act, act_own)
            A_ = nc.scalar.activation
            act.dma_start(con[:], A["con"]).then_inc(small_loaded, 16)
            act.dma_start(vec[:], A["vec"]).then_inc(small_loaded, 16)
            act.dma_start(wgk[:], A["w_gk"]).then_inc(small_loaded, 16)
            act.dma_start(wgate[:], A["w_gate"]).then_inc(small_loaded, 16)
            act.dma_start(wrout[:], A["w_router"]).then_inc(small_loaded, 16)
            act.dma_start(bgate[:], A["b_gate"]).then_inc(small_loaded, 16)
            act.dma_start(m0[:], A["m0"]).then_inc(small_loaded, 16)
            act.dma_start(maskf, A["scan_mask"]).then_inc(scan_mask_loaded, 16)
            act.dma_start(state[:, 0:6144], A["state0"]).then_inc(state0_loaded, 16)
            act.wait_ge(small_loaded, 16 * 7)
            act.wait_ge(lb_diff_ready, 1)
            A_(lbt[:, 1, :], lbt[:, 0, :], ACT.Sigmoid).then_inc(lb_ready, 1)

            def take(name, out, func, n=N, rows=P, **kw):
                return A_(out, see(act, name)[0:rows, 0:n], func, **kw)

            take("gr", gr_sb, ACT.Copy, rows=RANK).then_inc(freed("gr"), 1)
            act.wait_ge(freed("gr"), 1)
            act.nop().then_inc(gr_ready, 1)
            for h in range(HG):
                take(("z", h), g0[:, h, :], ACT.Sigmoid).then_inc(sig_ready, 1)
                take(("z", h), k0[:, h, :], ACT.Sigmoid, scale=-1.0).then_inc(freed(("z", h)), 1)
            for h in range(HG):
                take(("z", 4 + h), q0[:, h, :], ACT.Silu).then_inc(freed(("z", 4 + h)), 1)
            for h in range(HV):
                take(("z", 8 + h), gate0[:, h, :], ACT.Silu).then_inc(freed(("z", 8 + h)), 1)
            act.wait_ge(f_ready, HG)
            own.start(A_(g0[:, 0:HG, :], g0[:, 0:HG, :], ACT.Ln))
            act.wait_ge(gla_u_ready, GPAIR)
            own.settle(A_(glt[:, 1], glt[:, 0], ACT.Abs))
            own.settle(A_(glt[:, 1], glt[:, 1], ACT.Exp, scale=-1.0))
            A_(glt[:, 1], glt[:, 1], ACT.Ln, bias=one).then_inc(gla_l_ready, 1)
            for j in range(GPAIR):
                take(("z", 16 + j), k0[:, HG + j, :], ACT.Copy).then_inc(freed(("z", 16 + j)), 1)
            for j in range(GPAIR):
                z = see(act, ("z", 18 + j))
                for i in range(2):
                    r = slice(GLA_DK * i, GLA_DK * (i + 1))
                    own.start(A_(q0[r, HG + 2 * j + i, :], z[r, 0:N], ACT.Copy, scale=GLA_SCALE))
                own.wait()
                act.nop().then_inc(freed(("z", 18 + j)), 1)
            for h in range(HG):
                take(("z", 20 + h), v0[:, h, :], ACT.Copy).then_inc(freed(("z", 20 + h)), 1)
            act.wait_ge(dist_ready, 3)
            own.start(A_(chunks(eq0), chunks(g0), ACT.Exp))
            own.start(A_(eml[:, 0], chunks(b0)[:, :, :, CH // 2 - 1], ACT.Exp))
            own.start(A_(eml[:, 1], chunks(b0)[:, :, :, CH - 1], ACT.Exp))
            own.start(A_(as0, b0[:, :, NP_:N], ACT.Exp))
            own.start(A_(eml[:, 2], eml[:, 2], ACT.Exp))
            own.wait()
            act.nop().then_inc(expd_ready, 1)
            own.settle(A_(chunks(g0), chunks(g0), ACT.Exp, scale=-1.0))
            act.nop().then_inc(expnd_ready, 1)
            for h in range(HG, HV):
                take(("z", 20 + h), v0[:, h, :], ACT.Copy).then_inc(freed(("z", 20 + h)), 1)
            for h in range(HV):
                act.wait_ge(freed(("z", 20 + h)), J[("z", 20 + h)] // 8 + 1)
                act.nop().then_inc(v0_ready, 1)
            act.wait_ge(gla_l_ready, 1)
            act.wait_ge(dist_ready, 3)
            for m in range(HV // 2):
                take(("vt", m), vtok0[:, 2 * m:2 * m + 2].rearrange("p j a n -> p (j a n)"), ACT.Copy, n=512)\
                    .then_inc(freed(("vt", m)), 1)
            for m in range(HV // 2):
                act.wait_ge(freed(("vt", m)), J[("vt", m)] // 8 + 1)
                act.nop().then_inc(vtok_ready, 1)
            act.wait_ge(kp_ready, 1)
            for m in range(2):
                take(("vst", m), vs0[:, m * 512:(m + 1) * 512], ACT.Copy, n=512, rows=NS).then_inc(freed(("vst", m)), 1)
            for m in range(2):
                act.wait_ge(freed(("vst", m)), J[("vst", m)] // 8 + 1)
                act.nop().then_inc(vs_ready, 1)
            for c in range(NC):
                own.start(A_(o0[:, :, c * CH:(c + 1) * CH], see(act, ("o", c))[:, :].rearrange("p (h t) -> p h t", h=HV),
                             ACT.Copy))
                own.wait()
                act.nop().then_inc(freed(("o", c)), 1)
            own.settle(A_(o0[:, :, NP_:N], see(act, "os")[:, 0:HV * NS].rearrange("p (h t) -> p h t", h=HV), ACT.Copy))
            act.nop().then_inc(freed("os"), 1)
            act.nop().then_inc(o_ready, 1)
            for h in range(HV):
                A_(SQ[:, h, :], o0[:, h, :], ACT.Square).then_inc(osq_ready, 1)
            for h in range(HV):
                own.settle(take(("ss", h), SQ[:, h, :], ACT.Ln, scale=1.0 / P, bias=eps))
                act.nop().then_inc(freed(("ss", h)), 1)
                own.start(A_(SQ[:, h, :], SQ[:, h, :], ACT.Exp, scale=-0.5))
                own.wait()
                act.nop().then_inc(rms_ready, 1)

            def layernorm(n):
                act.wait_ge(centred, 2 * n + 1)
                for k in range(KD):
                    if k == KD // 2:
                        act.wait_ge(centred, 2 * n + 2)
                    A_(SQ[:, k, :], R[:, k, :], ACT.Square).then_inc(sq_ready, 1)
                if n < 3:
                    out = see(act, ("var", n))
                else:
                    act.wait_ge(psum_ready, NJOB + 2)
                    out = bank[1]
                own.settle(A_(nm[:], out[:, 0:N], ACT.Ln, scale=1.0 / D, bias=eps))
                if n < 3:
                    act.nop().then_inc(freed(("var", n)), 1)
                A_(nm[:], nm[:], ACT.Exp, scale=-0.5).then_inc(rstd_ready, 1)

            layernorm(0)
            for f in range(FD):
                if f >= 2:
                    act.wait_ge(h_ready, f - 1)
                own.settle(take(("h1", f), sil[:, f % 2, :], ACT.Silu))
                act.nop().then_inc(freed(("h1", f)), 1)
                act.nop().then_inc(silu_ready, 1)
            layernorm(1)

            act.wait_ge(stored0, 32)
            act.dma_start(us[:, :, 0:3, :].rearrange("p j r b -> p j (r b)"), A["conv0"]).then_inc(conv_loaded, 16)
            act.dma_start(n0, A["n0"]).then_inc(conv_loaded, 16)
            act.wait_ge(vtok_ready, HV // 2)
            act.dma_start(state[:, 0:8192], A["state1"]).then_inc(state1_loaded, 16)
            act.wait_ge(lgi_ready, 1)
            own.settle(A_(rows[:, 2, :], rows[:, 1, :], ACT.Abs))
            own.settle(A_(rows[:, 2, :], rows[:, 2, :], ACT.Exp, scale=-1.0))
            A_(rows[:, 2, :], rows[:, 2, :], ACT.Ln, bias=one[0:MH]).then_inc(lga_ready, 1)
            for i in range(KD):
                take(("y", i), up[:, i, 3:3 + NP_], ACT.Copy, n=NP_).then_inc(u_ready, 1)
                own.start(A_(us[:, i, 3, :], see(act, ("y", i))[:, NP_:N], ACT.Copy))
                act.wait_ge(u_ready, i + 1)
                own.wait()
                act.nop().then_inc(freed(("y", i)), 1)
            for i in range(KD):
                act.wait_ge(conv_done, i + 1)
                A_(qk[:, i, :], uc[:, i % 2, :], ACT.Silu).then_inc(qk_ready, 1)
                own.start(take(("y", 8 + i), v1[:, i, :], ACT.Copy))
                own.wait()
                act.nop().then_inc(freed(("y", 8 + i)), 1)
                act.nop().then_inc(v1_ready, 1)
            for i in range(KD):
                own.settle(take(("y", 16 + i), og[:, i, :], ACT.Sigmoid))
                act.nop().then_inc(freed(("y", 16 + i)), 1)
            act.nop().then_inc(og_ready, 1)
            act.wait_ge(lgl_ready, 1)
            own.start(A_(enrow, rows[:, 4, 0:NP_], ACT.Exp, scale=-1.0))
            own.start(A_(bcrow[:, NP_:NP_ + 2 * NS], bcrow[:, NP_:NP_ + 2 * NS], ACT.Exp))
            own.start(A_(bcrow[:, NP_ + 2 * NS:NP_ + 3 * NS], rows[:, 4, NP_:N], ACT.Exp, scale=-1.0))
            own.wait()
            act.nop().then_inc(exprow_ready, 1)
            act.wait_ge(qk_ready, KD)
            for m in range(4):
                for s in range(2):
                    own.start(A_(vtok[:, s, 2 * m * P:(2 * m + 2) * P].rearrange("p (j n) -> p j n", j=2),
                                 see(act, ("vt1", m))[:, :].rearrange("p (j s n) -> p j s n", j=2, s=2)[:, :, s, :],
                                 ACT.Copy))
                own.wait()
                act.nop().then_inc(freed(("vt1", m)), 1)
                act.nop().then_inc(vtok1_ready, 1)
            act.wait_ge(stored1, 16 * 3)
            act.wait_ge(conv_done, KD)
            for m in range(2):
                own.settle(take(("vs1", m), vs1[:, m * 512:(m + 1) * 512], ACT.Copy, n=512, rows=NS))
                act.nop().then_inc(freed(("vs1", m)), 1)
                act.nop().then_inc(vs1_ready, 1)
            own.settle(take("acol", acol.rearrange("p s h -> p (s h)"), ACT.Copy, n=2 * MH))
            act.nop().then_inc(freed("acol"), 1)
            for h in range(MH):
                act.wait_ge(arg_ready, h + 1)
                if h >= 2:
                    act.wait_ge(p1_ready, h - 1)
                    act.wait_ge(kw_ready, h - 1)
                own.start(A_(Dk[:, h % 2, 0:NP_], arg[:, h % 2, 0:NP_], ACT.Exp, bias=acol[:, 0, h:h + 1]))
                own.start(A_(Dk[:, h % 2, NP_:384], arg[:, h % 2, NP_:384], ACT.Exp, bias=acol[:, 1, h:h + 1]))
                own.wait()
                act.nop().then_inc(decay_ready, 1)
                own.settle(take(("C", h), Cout[:, h, :], ACT.Copy, n=257))
                act.nop().then_inc(freed(("C", h)), 1)
                act.nop().then_inc(cout_ready, 1)
            act.wait_ge(hc_ready, 4)
            for h in range(MH):
                own.settle(A_(SQ[:, 2 * h:2 * h + 2, :], h1[:, 2 * h:2 * h + 2, :], ACT.Square))
                act.nop().then_inc(hsq_ready, 1)
            for h in range(MH):
                own.settle(take(("hv", h), SQ[:, 2 * h, :], ACT.Ln, scale=1.0 / MDV, bias=eps))
                act.nop().then_inc(freed(("hv", h)), 1)
                own.settle(A_(SQ[:, 2 * h, :], SQ[:, 2 * h, :], ACT.Exp, scale=-0.5))
                act.nop().then_inc(hstd_ready, 1)
            layernorm(2)

            act.wait_ge(stored1, 16 * 5)
            act.wait_ge(route1, 1)
            A_(w12[:, 0, :], w12[:, 0, :], ACT.Exp).then_inc(route2, 1)
            for t, (t0, n) in enumerate(TT):
                for a in range(2):
                    own.settle(take(("xt", t, a), xtok[0:n, t, a * 512:(a + 1) * 512], ACT.Copy, n=512, rows=n))
                    act.nop().then_inc(freed(("xt", t, a)), 1)
                    act.nop().then_inc(xtok_ready, 1)
            act.wait_ge(npass_ready, 1)
            passes = act.value_load(npass[0:1, 0:1], min_val=1, max_val=MAXPASS)

            def take_gathered(j):
                for a in range(2):
                    act.wait_ge(xg_psum, j * 2 + (a + 1))
                    A_(xgh[:, 4 * a:4 * a + 4, :].rearrange("p k n -> p (k n)"), bank[6 + a], ACT.Copy)\
                        .then_inc(xgh_ready, 1)

            take_gathered(0)
            act.nop().then_inc(yE_ready, 1)
            with act.Fori(0, passes * NE) as j:
                for g in range(GPJ):
                    s = NL + g // 3
                    if g % 3 == 0:
                        act.wait_ge(slot_loaded[s % RING], 16 * (s // RING + 1) + j * (16 * FE // RING))
                    act.wait_ge(granule_used, j * GPJ + (g + 1))
                    A_(whi[:, g % NSPLIT, :], ring[:, s % RING, (g % 3) * D:(g % 3 + 1) * D], ACT.Copy)\
                        .then_inc(whi_ready, 1)
                    if g in SILU_AT:
                        b = SILU_AT[g]
                        act.wait_ge(granule_used, j * GPJ + (W13_AT[b] + 8 + NSPLIT))
                        A_(sE, bank[2 * (b % 2)], ACT.Silu).then_inc(silE_ready, 1)
                    if g in TURNED_AT:
                        b = TURNED_AT[g]
                        act.wait_ge(t_psum, j * NBLK + (b + 1))
                        A_(hTh[:, b % 2].rearrange("p f n -> p (f n)"), bank[TURN_BANK[b]], ACT.Copy).then_inc(hTh_ready, 1)
                act.wait_ge(gt_psum, j + 1)
                A_(GT, bank[3][:, 0:N], ACT.Copy).then_inc(gt_ready, 1)
                take_gathered(j + 1)
                act.wait_ge(y_psum, j + 1)
                A_(yE[:, 0:BLK], bank[4], ACT.Copy).then_inc(yE_ready, 1)
                act.wait_ge(granule_used, j * GPJ + (GPJ + NSPLIT))
                A_(yE[:, BLK:D], bank[5], ACT.Copy).then_inc(yE_ready, 1)
            layernorm(3)

        @block.vector
        def _(dve):
            own = Own(dve, dve_own)
            V = nc.vector
            dve.wait_ge(small_loaded, 16 * 7)
            V.tensor_tensor(lbt[:, 0, :], vec_("lb0", 0, HG), vec_("lb1", 0, HG), ALU.subtract).then_inc(lb_diff_ready, 1)
            dve.wait_ge(lb_ready, 1)
            own.settle(V.tensor_scalar(lbt[:, 2, :], lbt[:, 1, :], -1.0, 1.0, ALU.mult, ALU.add))
            for h in range(HG):
                dve.wait_ge(sig_ready, h + 1)
                own.start(V.tensor_scalar(g0[:, h, :], g0[:, h, :], lbt[:, 2, h:h + 1], lbt[:, 1, h:h + 1], ALU.mult, ALU.add))
                dve.wait_ge(freed(("z", h)), J[("z", h)] // 8 + 1)
                own.start(V.tensor_scalar(k0[:, h, :], k0[:, h, :], lbt[:, 2, h:h + 1], None, ALU.mult))
                own.wait()
                dve.nop().then_inc(f_ready, 1)
            for j in range(GPAIR):
                own.settle(V.tensor_scalar(glt[:, 0, j, :], see(dve, ("glag", j))[:, 0:N], vec_("bgk", j), None, ALU.add))
                V.tensor_scalar(glt[:, 2, j, :], glt[:, 0, j, :], 0.0, None, ALU.min).then_inc(gla_u_ready, 1)
                dve.wait_ge(gla_u_ready, j + 1)
                dve.nop().then_inc(freed(("glag", j)), 1)
            dve.wait_ge(gla_l_ready, 1)
            own.settle(V.tensor_tensor(glt[:, 2], glt[:, 2], glt[:, 1], ALU.subtract))
            own.settle(V.tensor_scalar(g0[:, HG:KT, :], glt[:, 2], 1.0 / GATE_NORM, None, ALU.mult))
            dve.wait_ge(scan_mask_loaded, 16)
            own.settle(V.tensor_tensor_scan(b0f, maskf, g0f, 0.0, ALU.mult, ALU.add))
            bb = chunks(b0)
            V.tensor_tensor(chunks(g0), bb, bc(bb[:, :, :, CH // 2 - 1:CH // 2], [P, KT, NC, CH]), ALU.subtract)\
                .then_inc(dist_ready, 1)
            V.tensor_tensor(eml[:, 2], bb[:, :, :, CH - 1], bb[:, :, :, CH // 2 - 1], ALU.subtract).then_inc(dist_ready, 1)
            dve.wait_ge(dist_ready, 2)
            dve.nop().then_inc(dist_ready, 1)
            dve.wait_ge(expd_ready, 1)
            dve.wait_ge(freed(("z", 19)), J[("z", 19)] // 8 + 1)
            dve.wait_ge(f_ready, HG)
            dve.wait_ge(q_zeroed, GL)
            qc = q0[:, 0:HG, 0:NP_]
            own.start(V.tensor_tensor(qc, qc, eq0[:, 0:HG, 0:NP_], ALU.mult))
            for j in range(GPAIR):
                qc = q0[:, HG + 2 * j:HG + 2 * j + 2, 0:NP_]
                own.start(V.tensor_tensor(qc, qc, bc(eq0[:, HG + j:HG + j + 1, 0:NP_], [P, 2, NP_]), ALU.mult))
            own.wait()
            dve.nop().then_inc(qp_ready, 1)
            dve.wait_ge(expnd_ready, 1)
            V.tensor_tensor(chunks(k0), chunks(k0), chunks(g0), ALU.mult).then_inc(kp_ready, 1)
            for m in range(KT // 2):
                own.settle(V.tensor_copy(ktok0[:, 2 * m:2 * m + 2].rearrange("p j a n -> p (j a n)"), see(dve, ("kt", m))[:, :]))
                dve.nop().then_inc(freed(("kt", m)), 1)
                dve.wait_ge(freed(("kt", m)), J[("kt", m)] // 8 + 1)
                dve.nop().then_inc(ktok_ready, 1)

            def probabilities(c):
                lo = CH * (c % 2)
                own.settle(V.tensor_tensor(prob0[lo:lo + CH, c // 2],
                                           see(dve, ("sc", c))[lo:lo + CH, :].rearrange("p (h n) -> p h n", h=HV),
                                           bc(con_("causal64")[lo:lo + CH].unsqueeze(1), [CH, HV, CH]), ALU.mult))
                dve.nop().then_inc(freed(("sc", c)), 1)
                dve.wait_ge(freed(("sc", c)), J[("sc", c)] // 8 + 1)
                dve.nop().then_inc(prob_ready, 1)

            def factor(i, c, j0=0, j1=KT):
                return bc(eml[:, i, j0:j1, c:c + 1], [P, j1 - j0, P])

            def advance(c):
                target = S if c == 0 else Tmp
                for nme, j0, j1 in (("u0", 0, HG), ("u1", HG, KT)):
                    own.settle(V.tensor_tensor(target[:, j0:j1, :],
                                               see(dve, (nme, c))[:, 0:(j1 - j0) * P].rearrange("p (j n) -> p j n", n=P),
                                               factor(2, c, j0, j1), ALU.mult))
                    dve.nop().then_inc(freed((nme, c)), 1)
                if c:
                    own.settle(V.tensor_tensor(S, S, factor(1, c), ALU.mult))
                    own.settle(V.tensor_tensor(S, S, Tmp, ALU.add))
                if c < NC - 1:
                    if c:
                        dve.wait_ge(psum_ready, J[("o", c)] + 1)
                    V.tensor_tensor(Sp, S, factor(0, c + 1), ALU.mult).then_inc(sp_ready, 1)
                else:
                    dve.nop().then_inc(s_final, 1)

            probabilities(0)
            probabilities(1)
            advance(0)
            probabilities(2)
            probabilities(3)
            for c in range(1, NC):
                advance(c)
            dve.wait_ge(sdec_ready, 1)
            for b in range(NS):
                for nme, j0, j1 in (("vb0", 0, HG), ("vb1", HG, KT)):
                    own.settle(V.tensor_tensor(Tmp[:, j0:j1, :],
                                               see(dve, (nme, b))[:, 0:(j1 - j0) * P].rearrange("p (j n) -> p j n", n=P),
                                               bc(k0[:, j0:j1, NP_ + b:NP_ + b + 1], [P, j1 - j0, P]), ALU.mult))
                    dve.nop().then_inc(freed((nme, b)), 1)
                V.tensor_tensor(S0[:, :, b, :], S0[:, :, b, :], Tmp, ALU.add).then_inc(snew_ready, 1)
                dve.wait_ge(snew_ready, b + 1)
            dve.wait_ge(o_ready, 1)
            dve.wait_ge(freed(("z", 15)), J[("z", 15)] // 8 + 1)
            for h in range(HV):
                w = vec_("gn_hg") if h < HG else vec_("gn_gla")
                dve.wait_ge(rms_ready, h + 1)
                own.settle(V.scalar_tensor_tensor(out=o0[:, h, :], in0=o0[:, h, :], scalar=w, in1=SQ[:, h, :],
                                                  op0=ALU.mult, op1=ALU.mult))
                V.tensor_tensor(gate0[:, h, :], gate0[:, h, :], o0[:, h, :], ALU.mult).then_inc(y_ready, 1)
                dve.wait_ge(y_ready, h + 1)

            def residual(n):
                for k in range(KD):
                    V.scalar_tensor_tensor(out=R[:, k, :], in0=X[:, k, :], scalar=ALPHA, in1=see(dve, ("mix", n, k))[:, 0:N],
                                           op0=ALU.mult, op1=ALU.add).then_inc(r_ready, 1)
                    dve.wait_ge(r_ready, KD * n + k + 1)
                    dve.nop().then_inc(freed(("mix", n, k)), 1)

            def layernorm(n):
                g, b = ("ln1g", "ln1b") if n % 2 == 0 else ("ln2g", "ln2b")
                g, b = f"{g}{n // 2}", f"{b}{n // 2}"
                if n < 3:
                    out = see(dve, ("mean", n))
                else:
                    dve.wait_ge(psum_ready, NJOB + 1)
                    out = bank[0]
                own.settle(V.tensor_scalar(nm[:], out[:, 0:N], -1.0 / D, None, ALU.mult))
                if n < 3:
                    dve.nop().then_inc(freed(("mean", n)), 1)
                H = KD // 2
                for i in range(2):
                    r = R[:, i * H:(i + 1) * H, :]
                    V.tensor_tensor(r, r, bc(nm[:].unsqueeze(1), [P, H, N]), ALU.add).then_inc(centred, 1)
                dve.wait_ge(rstd_ready, n + 1)
                for i in range(2):
                    r = R[:, i * H:(i + 1) * H, :]
                    own.start(V.tensor_tensor(r, r, bc(nm[:].unsqueeze(1), [P, H, N]), ALU.mult))
                own.wait()
                for k in range(KD):
                    V.tensor_scalar(X[:, k, :], R[:, k, :], vec_(g, k), vec_(b, k), ALU.mult, ALU.add).then_inc(x_ready, 1)
                dve.wait_ge(x_ready, KD * (n + 1))

            residual(0)
            layernorm(0)
            for f in range(FD):
                dve.wait_ge(silu_ready, f + 1)
                V.tensor_tensor(hT[:, f, :], sil[:, f % 2, :], see(dve, ("h3", f))[:, 0:N], ALU.mult).then_inc(h_ready, 1)
                dve.wait_ge(h_ready, f + 1)
                dve.nop().then_inc(freed(("h3", f)), 1)
            residual(1)
            layernorm(1)

            dve.wait_ge(stored0, 32)
            own.start(V.tensor_scalar(rows[:, 0, :], see(dve, "gi")[0:MH, 0:N], bgate[:, 0:1], None, ALU.add))
            own.start(V.tensor_scalar(rows[:, 1, :], see(dve, "gf")[0:MH, 0:N], bgate[:, 1:2], None, ALU.add))
            own.start(V.memset(up[:, :, 0:3], 0.0))
            own.wait()
            dve.nop().then_inc(freed("gi"), 1)
            dve.nop().then_inc(freed("gf"), 1)
            dve.nop().then_inc(lgi_ready, 1)
            own.settle(V.tensor_scalar(rows[:, 3, :], rows[:, 1, :], 0.0, None, ALU.min))
            dve.wait_ge(lga_ready, 1)
            own.settle(V.tensor_tensor(rows[:, 1, :], rows[:, 3, :], rows[:, 2, :], ALU.subtract))
            pr = slice(0, NP_)
            sm = slice(NP_, N)
            own.settle(V.tensor_tensor_scan(rows[:, 2, pr], bc(one[0:MH], [MH, NP_]), rows[:, 1, pr], 0.0, ALU.mult, ALU.add))
            own.settle(V.tensor_tensor(lm, rows[:, 1, sm], m0[:], ALU.add))
            own.settle(V.tensor_tensor(rows[:, 4, sm], lm, rows[:, 0, sm], ALU.max))
            own.start(V.tensor_tensor(bcrow[:, NP_:NP_ + NS], rows[:, 0, sm], rows[:, 4, sm], ALU.subtract))
            own.start(V.tensor_tensor(bcrow[:, NP_ + NS:NP_ + 2 * NS], lm, rows[:, 4, sm], ALU.subtract))
            own.settle(V.tensor_tensor(rows[:, 0, pr], rows[:, 0, pr], rows[:, 2, pr], ALU.subtract))
            own.settle(V.tensor_tensor_scan(rows[:, 3, pr], rows[:, 0, pr], rows[:, 0, pr], 0.0, ALU.max, ALU.max))
            own.start(V.tensor_tensor(rows[:, 4, pr], rows[:, 2, pr], rows[:, 3, pr], ALU.add))
            own.start(V.tensor_scalar(bcrow[:, 0:NP_], rows[:, 3, pr], -1.0, None, ALU.mult))
            own.wait()
            dve.nop().then_inc(rows_ready, 1)
            dve.nop().then_inc(lgl_ready, 1)
            dve.wait_ge(conv_loaded, 32)
            for i in range(KD):
                dve.wait_ge(freed(("y", i)), J[("y", i)] // 8 + 1)
                if i >= 2:
                    dve.wait_ge(qk_ready, i - 1)
                for r in range(4):
                    w = vec_(f"convw{r}", i)
                    for out, src in ((uc[:, i % 2, 0:NP_], up[:, i, r:r + NP_]), (uc[:, i % 2, NP_:N], us[:, i, r, :])):
                        if r == 0:
                            ins = V.tensor_scalar(out, src, w, vec_("convb", i), ALU.mult, ALU.add)
                        else:
                            ins = V.scalar_tensor_tensor(out=out, in0=src, scalar=w, in1=out, op0=ALU.mult, op1=ALU.add)
                        own.start(ins)
                    own.wait()
                dve.nop().then_inc(conv_done, 1)
            dve.wait_ge(qk_ready, KD)
            own.start(V.tensor_scalar(qs, qk[:, 0:MH, NP_:N], ML_SCALE, None, ALU.mult))
            for h in range(MH):
                a = h % 2
                neg = con_("neg")
                m = see(dve, ("bc", h))
                if h >= 2:
                    dve.wait_ge(decay_ready, h - 1)
                own.start(V.tensor_tensor(arg[:, a, 0:P], m[:, 0:P], neg, ALU.add))
                own.start(V.tensor_copy(arg[:, a, P:NP_], m[:, P:NP_]))
                own.start(V.tensor_tensor(arg[:, a, NP_:384], m[:, P:NP_], neg, ALU.add))
                own.start(V.tensor_copy(fwb[:, h].rearrange("p w b -> p (w b)"), m[:, NP_:NP_ + 3 * NS]))
                own.wait()
                dve.nop().then_inc(freed(("bc", h)), 1)
                dve.nop().then_inc(arg_ready, 1)
                dve.wait_ge(decay_ready, h + 1)
                if h >= 2:
                    dve.wait_ge(psum_ready, J[("C", h - 2)] + 1)
                kt = see(dve, ("kt1", h))
                own.start(V.tensor_scalar(kw[:, a, 0, :], kt[:, 0:P], Dk[:, a, NP_ - 1:NP_], None, ALU.mult))
                own.start(V.tensor_scalar(kw[:, a, 1, :], kt[:, P:2 * P], Dk[:, a, 383:384], None, ALU.mult))
                own.start(V.scalar_tensor_tensor(out=Pr[:, a, :], in0=see(dve, ("sc1", h))[:, 0:384], scalar=ML_SCALE,
                                                 in1=Dk[:, a, :], op0=ALU.mult, op1=ALU.mult))
                own.wait()
                for s_ in (freed(("kt1", h)), freed(("sc1", h)), p1_ready, kw_ready):
                    dve.nop().then_inc(s_, 1)
                t1, t2 = arg[:, a, 0:NP_], nm[:, 0:NP_]
                own.settle(V.tensor_scalar(t1, see(dve, ("den", h))[:, 0:NP_], -1.0, None, ALU.mult))
                own.settle(V.tensor_tensor(t1, t1, see(dve, ("den", h))[:, 0:NP_], ALU.max))
                own.settle(V.tensor_tensor(t1, t1, see(dve, ("en", h))[:, 0:NP_], ALU.max))
                own.settle(V.reciprocal(t2, t1))
                own.settle(V.tensor_tensor(h1[:, 2 * h:2 * h + 2, 0:NP_],
                                           see(dve, ("num", h))[:, :].rearrange("p (v n) -> p v n", v=2),
                                           bc(t2.unsqueeze(1), [P, 2, NP_]), ALU.mult))
                for s_ in (freed(("den", h)), freed(("en", h)), freed(("num", h)), h1_ready):
                    dve.nop().then_inc(s_, 1)
            own.settle(V.tensor_tensor(ki, qk[:, MH:2 * MH, NP_:N], fwb[:, :, 0, :], ALU.mult))
            own.settle(V.tensor_tensor(n0, n0, fwb[:, :, 1, :], ALU.mult))
            own.settle(V.tensor_tensor(n0, n0, ki, ALU.add))
            own.settle(V.tensor_tensor(qns, n0, qs, ALU.mult))
            dve.nop().then_inc(fwb_ready, 1)
            dve.nop().then_inc(qn_ready, 1)
            qn = see(dve, "qn")[:, 0:MH * NS].rearrange("p (h b) -> p h b", h=MH)
            own.settle(V.tensor_scalar(dens, qn, -1.0, None, ALU.mult))
            own.settle(V.tensor_tensor(dens, dens, qn, ALU.max))
            own.settle(V.tensor_tensor(dens, dens, fwb[:, :, 2, :], ALU.max))
            own.settle(V.reciprocal(dens, dens))
            dve.nop().then_inc(freed("qn"), 1)
            dve.wait_ge(cdec_ready, 1)
            dve.wait_ge(vs1_ready, 2)
            for b in range(NS):
                for i in range(2):
                    own.settle(V.tensor_tensor(Tm1[:, 2 * i:2 * i + 2, :],
                                               see(dve, ("wb", b, i))[:, :].rearrange("p (h n) -> p h n", h=2),
                                               bc(ki[:, 2 * i:2 * i + 2, b:b + 1], [P, 2, MDV]), ALU.mult))
                    dve.nop().then_inc(freed(("wb", b, i)), 1)
                V.tensor_tensor(Cs[:, :, b, :], Cs[:, :, b, :], Tm1, ALU.add).then_inc(cnew_ready, 1)
                dve.wait_ge(cnew_ready, b + 1)
            for v in range(2):
                own.settle(V.tensor_tensor(h1[:, v:KD:2, NP_:N],
                                           see(dve, "ns")[:, 0:MH * 2 * NS].rearrange("p (h v b) -> p h v b", h=MH, v=2)[:, :, v, :],
                                           dens, ALU.mult))
            dve.nop().then_inc(freed("ns"), 1)
            dve.nop().then_inc(hs_ready, 1)
            for h in range(MH):
                own.settle(V.tensor_scalar(nm[:], see(dve, ("hm", h))[:, 0:N], -1.0 / MDV, None, ALU.mult))
                dve.nop().then_inc(freed(("hm", h)), 1)
                hh = h1[:, 2 * h:2 * h + 2, :]
                own.settle(V.tensor_tensor(hh, hh, bc(nm[:].unsqueeze(1), [P, 2, N]), ALU.add))
                dve.nop().then_inc(hc_ready, 1)
            dve.wait_ge(og_ready, 1)
            for h in range(MH):
                dve.wait_ge(hstd_ready, h + 1)
                for v in range(2):
                    own.settle(V.scalar_tensor_tensor(out=h1[:, 2 * h + v, :], in0=h1[:, 2 * h + v, :],
                                                      scalar=vec_("hn", 2 * h + v), in1=SQ[:, 2 * h, :],
                                                      op0=ALU.mult, op1=ALU.mult))
                own.settle(V.tensor_tensor(og[:, 2 * h:2 * h + 2, :], og[:, 2 * h:2 * h + 2, :],
                                           h1[:, 2 * h:2 * h + 2, :], ALU.mult))
                dve.nop().then_inc(y1_ready, 1)
            residual(2)
            layernorm(2)

            dve.wait_ge(stored1, 16 * 5)
            own.start(V.memset(L, 0.0))
            own.wait()
            for t, (t0, n) in enumerate(TT):
                own.settle(V.tensor_copy(L[0:n, t, :], see(dve, ("lg", t))[0:n, 0:NE]))
                dve.nop().then_inc(freed(("lg", t)), 1)
                own.settle(V.max(mx[:, t, :], L[:, t, :]))
                own.settle(V.max_index(idx[:, t, :], mx[:, t, :], L[:, t, :]))
            own.start(V.tensor_tensor(w12[:, 0, :], mx[:, :, 1], mx[:, :, 0], ALU.subtract))
            own.start(V.tensor_copy(ixf, idx[:]))
            own.wait()
            dve.nop().then_inc(route1, 1)
            dve.wait_ge(route2, 1)
            own.settle(V.tensor_scalar(w12[:, 2, :], w12[:, 0, :], 1.0, None, ALU.add))
            own.settle(V.reciprocal(w12[:, 1, :], w12[:, 2, :]))
            own.settle(V.tensor_tensor(w12[:, 2, :], w12[:, 0, :], w12[:, 1, :], ALU.mult))
            io = bc(con_("iota")[:, 0:NE].unsqueeze(1), [P, 3, NE])
            for i in range(2):
                own.settle(V.tensor_tensor(oh, io, bc(ixf[:, :, i:i + 1], [P, 3, NE]), ALU.is_equal))
                if i == 0:
                    own.settle(V.tensor_copy(sel, oh))
                    own.settle(V.tensor_tensor(gat, oh, bc(w12[:, 1, :].unsqueeze(2), [P, 3, NE]), ALU.mult))
                else:
                    own.settle(V.tensor_tensor(sel, sel, oh, ALU.add))
                    own.settle(V.tensor_tensor(oh, oh, bc(w12[:, 2, :].unsqueeze(2), [P, 3, NE]), ALU.mult))
                    own.settle(V.tensor_tensor(gat, gat, oh, ALU.add))
            own.settle(V.tensor_scalar(sel[:, 2, :], sel[:, 2, :], con_("valid"), None, ALU.mult))
            dve.nop().then_inc(sel_ready, 1)
            own.settle(V.tensor_reduce(mcnt[:, 0:1], see(dve, "count")[:, 0:NE], AX.X, ALU.max))
            dve.nop().then_inc(freed("count"), 1)
            own.settle(V.tensor_scalar(mcnt[:, 1:2], mcnt[:, 0:1], float(CAP), 1.0, ALU.is_gt, ALU.add))
            own.settle(V.tensor_scalar(mcnt[:, 2:3], mcnt[:, 0:1], float(2 * CAP), None, ALU.is_gt))
            own.settle(V.tensor_tensor(mcnt[:, 3:4], mcnt[:, 1:2], mcnt[:, 2:3], ALU.add))
            V.tensor_copy(npass[:], mcnt[0:1, 3:4]).then_inc(npass_ready, 1)
            own.settle(V.tensor_scalar(rnk, see(dve, "rank")[:, 0:3 * NE].rearrange("p (t e) -> p t e", t=3), 1.0, None, ALU.add))
            dve.nop().then_inc(freed("rank"), 1)
            own.settle(V.tensor_tensor(rnk, rnk, sel, ALU.mult))
            own.start(V.memset(jrank, -1.0))
            own.start(V.memset(jgate, 0.0))
            own.wait()
            for p in range(MAXPASS):
                own.start(V.tensor_scalar(jrank[:, :, p * NE:(p + 1) * NE], rnk, -1.0 - p * CAP, None, ALU.add))
                own.start(V.tensor_copy(jgate[:, :, p * NE:(p + 1) * NE], gat))
            own.start(V.tensor_scalar(R[:], X[:], ALPHA, None, ALU.mult))
            own.wait()
            dve.nop().then_inc(jobs_ready, 1)
            dve.wait_ge(npass_ready, 1)
            passes = dve.value_load(npass[0:1, 0:1], min_val=1, max_val=MAXPASS)

            def selection(j):
                V.tensor_copy(crank.unsqueeze(2), jrank[:, :, bass.ds(j, 1)]).then_inc(racc_ready, 1)
                V.tensor_copy(cgate.unsqueeze(2), jgate[:, :, bass.ds(j, 1)]).then_inc(racc_ready, 1)
                dve.wait_ge(racc_ready, j * 2 + 2)
                for t in range(3):
                    V.tensor_scalar(G[:, t, :], con_("iota"), crank[:, t:t + 1], None, ALU.is_equal).then_inc(gathered, 1)
                dve.wait_ge(gathered, j * 3 + 3)

            def gated():
                for t in range(3):
                    ins = V.tensor_scalar(Gg[:, t, :], con_("iota"), crank[:, t:t + 1], cgate[:, t:t + 1],
                                          ALU.is_equal, ALU.mult)
                return ins

            def split_gathered(j):
                for a in range(2):
                    dve.wait_ge(xgh_ready, j * 2 + (a + 1))
                    V.tensor_tensor(xgl[:, 4 * a:4 * a + 4, :].rearrange("p k n -> p (k n)"), bank[6 + a],
                                    xgh[:, 4 * a:4 * a + 4, :].bitcast(F32).rearrange("p k n -> p (k n)"),
                                    ALU.subtract).then_inc(xgl_ready, 1)

            dve.nop().then_inc(xgl_ready, 1)
            dve.nop().then_inc(sc_added, 1)
            selection(0)
            dve.nop().then_inc(g_ready, 1)
            gated().then_inc(gg_ready, 1)
            split_gathered(0)
            with dve.Fori(0, passes * NE) as j:
                for g in range(GPJ):
                    s = NL + g // 3
                    dve.wait_ge(whi_ready, j * GPJ + (g + 1))
                    V.tensor_tensor(wlo[:, g % NSPLIT, :], ring[:, s % RING, (g % 3) * D:(g % 3 + 1) * D],
                                    whi[:, g % NSPLIT, :].bitcast(F32), ALU.subtract).then_inc(wlo_ready, 1)
                    if g in SILU_AT:
                        b = SILU_AT[g]
                        dve.wait_ge(silE_ready, j * NBLK + (b + 1))
                        V.tensor_tensor(hb, sE, bank[2 * (b % 2) + 1], ALU.mult).then_inc(hb_ready, 1)
                    if g in TURNED_AT:
                        b = TURNED_AT[g]
                        dve.wait_ge(hTh_ready, j * NBLK + (b + 1))
                        V.tensor_tensor(hTl[:, b % 2].rearrange("p f n -> p (f n)"), bank[TURN_BANK[b]],
                                        hTh[:, b % 2].bitcast(F32).rearrange("p f n -> p (f n)"),
                                        ALU.subtract).then_inc(hT_ready, 1)
                    if g == GPJ // 2:
                        selection(j + 1)
                        dve.nop().then_inc(g_ready, 1)
                split_gathered(j + 1)
                dve.wait_ge(gt_psum, j + 1)
                gated().then_inc(gg_ready, 1)
                for k in range(KD):
                    dve.wait_ge(sc_psum, j * KD + (k + 1))
                    V.tensor_tensor(R[:, k, :], R[:, k, :], bank[7 - k % 2][:, 0:N], ALU.add).then_inc(sc_added, 1)
            dve.wait_ge(sc_added, passes * (NE * KD) + 1)
            for k in range(KD):
                dve.nop().then_inc(r_ready, 1)
            layernorm(3)
            dve.nop().then_inc(out_ready, 1)

        @block.gpsimd
        def _(pool):
            Pv = nc.gpsimd
            for j in range(GPAIR):
                Pv.memset(q0[GLA_DK:P, HG + 2 * j, :], 0.0).then_inc(q_zeroed, 1)
                Pv.memset(q0[0:GLA_DK, HG + 2 * j + 1, :], 0.0).then_inc(q_zeroed, 1)
            pool.wait_ge(q_zeroed, GL)
            pool.wait_ge(state0_loaded, 16)
            pool.wait_ge(expd_ready, 1)
            n = 0
            for j in range(KT):
                Pv.tensor_tensor(S0[:, j], S0[:, j], bc(as0[:, j].unsqueeze(2), [P, NS, P]), ALU.mult).then_inc(pool_own, 1)
                n += 1
            pool.wait_ge(pool_own, n)
            pool.nop().then_inc(sdec_ready, 1)
            pool.wait_ge(s_final, 1)
            pool.dma_start(A["o_state0p"], S).then_inc(stored0, 16)
            pool.wait_ge(snew_ready, NS)
            pool.dma_start(A["o_state0s"], state[:, 0:6144]).then_inc(stored0, 16)
            pool.wait_ge(u_ready, KD)
            pool.wait_ge(freed(("y", KD - 1)), J[("y", KD - 1)] // 8 + 1)
            pool.wait_ge(conv_loaded, 32)
            with nc.allow_non_contiguous_dma(reason="three columns of each row"):
                pool.dma_start(A["o_convp"], up[:, :, NP_:NP_ + 3]).then_inc(stored1, 16)
                pool.dma_start(A["o_convs"], us[:, :, 1:4, :].rearrange("p j r b -> p j (r b)")).then_inc(stored1, 16)
                pool.wait_ge(rows_ready, 1)
                pool.dma_start(A["o_m"], rows[:, 4, NP_ - 1:N]).then_inc(stored1, 16)
            pool.wait_ge(state1_loaded, 16)
            pool.wait_ge(fwb_ready, 1)
            for h in range(MH):
                Pv.tensor_tensor(Cs[:, h], Cs[:, h], bc(fwb[:, h, 1, :].unsqueeze(2), [P, NS, MDV]), ALU.mult)\
                    .then_inc(pool_own, 1)
                n += 1
            pool.wait_ge(pool_own, n)
            pool.nop().then_inc(cdec_ready, 1)
            pool.wait_ge(cout_ready, MH)
            pool.dma_start(A["o_Cp"], Cout).then_inc(stored1, 16)
            pool.dma_start(A["o_ns"], n0).then_inc(stored1, 16)
            pool.wait_ge(cnew_ready, NS)
            pool.dma_start(A["o_Cs"], state[:, 0:8192]).then_inc(stored, 16)
            pool.wait_ge(out_ready, 1)
            pool.dma_start(A["o_y"], X[:]).then_inc(stored, 16)
            pool.wait_ge(stored0, 32)
            pool.wait_ge(stored1, 16 * 5)
            pool.wait_ge(stored, 16 * 2)


_OUT = {
    "o_y": (P, KD, N), "o_state0p": (P, KT, P), "o_state0s": (P, KT * NS * P), "o_convp": (P, KD, 3),
    "o_convs": (P, KD, 3 * NS), "o_m": (MH, 1 + NS), "o_Cp": (P, MH, MDV + 1), "o_ns": (P, MH, NS),
    "o_Cs": (P, MH * NS * MDV),
}


def _tiles(w):
    k, n = w.shape
    return w.reshape(k // P, P, n // P, P).transpose(2, 1, 0, 3).reshape(n // P, P, k)


def _columns(v):
    return v.reshape(-1, P).T


def _constants():
    p = np.arange(P)[:, None]
    f = np.arange(P)[None, :]
    parts = {
        "ident": (p == f), "ones": np.ones((P, P)), "causal64": (p % CH <= f[:, :CH]),
        "neg": np.where(p > f, -1e30, 0.0), "before": (p < f), "iota": np.broadcast_to(f, (P, P)),
        "valid": (p < NS), "eps": np.full((P, 1), EPS), "one": np.ones((P, 1)),
    }
    con = np.concatenate([np.asarray(parts[n], np.float32) for n in CON], 1)
    mask = np.ones((KT, N), np.float32)
    mask[:, 0:NP_:CH] = 0
    mask[:, NP_:] = 0
    return con, np.ascontiguousarray(np.broadcast_to(mask.reshape(1, -1), (P, KT * N)))


def _layout(i):
    i = {k: np.asarray(v) for k, v in i.items()}
    a = {}
    x = np.concatenate([i["x_prompt"][0], i["x_sample"][:, 0]], 0)
    a["x"] = x.T.reshape(KD, P, N).transpose(1, 0, 2)
    w = i["w_in_even"][0]
    ends = np.cumsum([0, 512, 512, 512, 512, 256, 256, 512, 512, RANK])
    hq, hf, hi, hg, gq, gk, gv, gg, gr = (w[:, s:e] for s, e in zip(ends[:-1], ends[1:]))
    a["w_in0"] = np.concatenate([_tiles(t) for t in (hf, hq, hg, gg, gk, gq, hi, gv)], 0)
    a["w_gr"] = gr.reshape(KD, P, RANK).transpose(1, 0, 2)
    a["w_gk"] = i["w_gk"][0]
    a["w_out0"] = _tiles(i["w_out_even"][0])
    a["w13"] = np.concatenate([_tiles(i["w1_dense"][0]), _tiles(i["w3_dense"][0])], 2)
    a["w2"] = _tiles(i["w2_dense"][0])
    w = i["w_in_odd"][0]
    a["w_in1"] = _tiles(w[:, :3 * D])
    a["w_gate"] = w[:, 3 * D:].reshape(KD, P, 2 * MH).transpose(1, 0, 2)
    a["w_out1"] = _tiles(i["w_out_odd"][0])
    a["w_router"] = i["w_router"][0].reshape(KD, P, NE).transpose(1, 0, 2)

    def up(w):
        return w.reshape(NE, KD // 2, 2, P, NBLK, BLK).transpose(0, 4, 1, 3, 2, 5).reshape(NE, NBLK, KD // 2, P, D)

    parts = {"w1": up(i["w1_moe"][0]), "w3": up(i["w3_moe"][0]), "w2": i["w2_moe"][0].reshape(NE, NBLK, BLK // P, P, D)}
    moe = np.empty((NE, FE, P, 3, D), np.float32)
    for g, (name, b, c) in enumerate(ORDER):
        moe[:, g // 3, :, g % 3] = parts[name][:, b, c]
    a["w_moe"] = moe.reshape(NE * FE, P, 3 * D)
    lb = i["hg_lower_bounds"]
    v = {"lb0": lb[0], "lb1": lb[1], "bgk": i["b_gk"][0], "gn_hg": i["gn_hg"][0], "gn_gla": i["gn_gla"][0],
         "convb": i["conv_b"][0], "hn": i["hn_w"][0]}
    for n in LN_VECS:
        v[n] = i[f"{n[:3]}_{n[3]}"][int(n[4])]
    for j in range(4):
        v[f"convw{j}"] = i["conv_w"][0, j]
    a["vec"] = np.concatenate([_columns(v[n]) for n in VEC], 1)
    a["b_gate"] = i["b_gate_odd"][0].reshape(2, MH).T
    a["m0"] = i["state_mlstm_m"][0].T
    hgs = i["state_hgrn"][0].transpose(2, 1, 0, 3)
    gls = i["state_gla"][0].reshape(NS, GPAIR, 2 * GLA_DK, P).transpose(2, 1, 0, 3)
    a["state0"] = np.concatenate([hgs, gls], 1).reshape(P, -1)
    a["state1"] = i["state_mlstm_C"][0].transpose(2, 1, 0, 3).reshape(P, -1)
    a["n0"] = i["state_mlstm_n"][0].transpose(2, 1, 0)
    a["conv0"] = i["state_mlstm_conv"][0].reshape(NS, 3, KD, P).transpose(3, 2, 1, 0).reshape(P, KD, 3 * NS)
    a["con"], a["scan_mask"] = _constants()
    return {k: np.ascontiguousarray(t) for k, t in a.items()}


def kernel(**inputs):
    import concourse.bacc as _bacc
    from concourse.bass_utils import run_bass_kernel_spmd as _run

    arrays = _layout(inputs)
    nc = _bacc.Bacc("TRN2", target_bir_lowering=False, num_devices=1, dynamic_dma_scratch_size=4096)
    A = {n: nc.dram_tensor(f"in_{n}", t.shape, mybir.dt.from_np(t.dtype), kind="ExternalInput").ap()
         for n, t in arrays.items()}
    for n, shape in _OUT.items():
        A[n] = nc.dram_tensor(n, shape, F32, kind="ExternalOutput").ap()
    decoder_step(nc, A)
    r = _run(nc, [{f"in_{n}": t for n, t in arrays.items()}], core_ids=[0]).results[0]
    o = {n: np.asarray(r[n]).reshape(s) for n, s in _OUT.items()}
    y = o["o_y"].transpose(2, 1, 0).reshape(N, D)
    sp = o["o_state0p"]
    ss = o["o_state0s"].reshape(P, KT, NS, P)
    hg_p = sp[:, :HG].transpose(1, 0, 2)[None, None]
    gla_p = sp[:, HG:].transpose(1, 0, 2).reshape(GL, GLA_DK, P)[None, None]
    hg_s = ss[:, :HG].transpose(2, 1, 0, 3)[None]
    gla_s = ss[:, HG:].transpose(2, 1, 0, 3).reshape(NS, GL, GLA_DK, P)[None]
    C_p = o["o_Cp"][:, :, :MDV].transpose(1, 0, 2)[None, None]
    n_p = o["o_Cp"][:, :, MDV].T[None, None]
    m_p = o["o_m"][:, 0][None, None]
    conv_p = o["o_convp"].transpose(2, 1, 0).reshape(3, D)[None, None]
    C_s = o["o_Cs"].reshape(P, MH, NS, MDV).transpose(2, 1, 0, 3)[None]
    n_s = o["o_ns"].transpose(2, 1, 0)[None]
    m_s = o["o_m"][:, 1:].T[None]
    conv_s = o["o_convs"].reshape(P, KD, 3, NS).transpose(3, 2, 1, 0).reshape(NS, 3, D)[None]
    out = (y[:NP_][None], y[NP_:][:, None], hg_p, gla_p, C_p, n_p, m_p, conv_p, hg_s, gla_s, C_s, n_s, m_s, conv_s)
    return tuple(np.ascontiguousarray(t) for t in out)
```

```python
import concourse.bass as bass
from concourse import mybir
from contextlib import ExitStack
import numpy as np

F32 = mybir.dt.float32
F32R = mybir.dt.float32r
I32 = mybir.dt.int32
U32 = mybir.dt.uint32
ALU = mybir.AluOpType
ACT = mybir.ActivationFunctionType
AX = mybir.AxisListType

P = 128
D = 1024
KD = D // P
NP_ = 256
NS = 8
N = NP_ + NS
DEPTH = 2
ALPHA = (2.0 * DEPTH) ** 0.25
EPS = 1e-5
CH = 64
NC = NP_ // CH
HG, GL = 4, 4
GPAIR = GL // 2
KT = HG + GPAIR
HV = HG + GL
GLA_DK = 64
GATE_NORM = 16.0
RANK = 16
FD = 2816 // P
MH = 4
MDV = 256
ML_SCALE = 128 ** -0.5
GLA_SCALE = GLA_DK ** -0.5
NE = 8
FE = 3584 // P
CAP = P
MAXPASS = -(-N // CAP)
TT = [(0, P), (P, P), (2 * P, NS)]
RING = 4
BLK = 512
NBLK = FE * P // BLK
GPJ = 3 * FE
NSPLIT = 4
W13_AT, W2_AT, ORDER = [], [], []
for _b in range(NBLK + 1):
    if _b < NBLK:
        W13_AT.append(len(ORDER))
        ORDER += [(_w, _b, _k) for _k in range(KD // 2) for _w in ("w1", "w3")]
    if _b > 0:
        W2_AT.append(len(ORDER))
        ORDER += [("w2", _b - 1, _f) for _f in range(BLK // P)]
assert len(ORDER) == GPJ
SILU_AT = {W13_AT[_b] + 7 + 4: _b for _b in range(NBLK)}
TURNED_AT = {(W13_AT[_b + 1] + 3 if _b < NBLK - 1 else GPJ - 5) + NSPLIT: _b for _b in range(NBLK)}
TURN_BANK = [6, 7, 6, 7, 6, 7, 2]
SCATTER_BANK = [6, 7, 3, 2, 4, 5, 6, 7]
ARENA = 15000
SLOT = 3072
SAMPLES_BEHIND = [[], [0, 1], [2, 3], [4, 5], [6, 7]]
HAHEAD = 3
PAIRS = len(SAMPLES_BEHIND) - 1
LN_VECS = ["ln1g0", "ln1b0", "ln2g0", "ln2b0", "ln1g1", "ln1b1", "ln2g1", "ln2b1"]

LN_OF = [("ln1g0", "ln1b0"), ("ln2g0", "ln2b0"), ("ln1g1", "ln1b1"), ("ln2g1", "ln2b1")]

VEC, _at = {}, 0
for _n, _w in [("lb0", HG), ("lb1", HG), ("bgk", GPAIR), ("gn_hg", 1), ("gn_gla", 1)] + [(v, KD) for v in LN_VECS] + [
        ("convb", KD), ("hn", KD)] + [(f"convw{j}", KD) for j in range(4)]:
    VEC[_n] = (_at, _at + _w)
    _at += _w
NVEC = _at
CON, _at = {}, 0
for _n, _w in [("ident", P), ("ones", P), ("causal64", CH), ("neg", P), ("before", P), ("iota", P), ("valid", 1),
               ("eps", 1), ("one", 1)]:
    CON[_n] = (_at, _at + _w)
    _at += _w
NCON = _at


def bc(ap, shape):
    return ap.to_broadcast(list(shape))


def decoder_step(nc, A):
    ctx = ExitStack()
    with ctx:
        def sb(name, shape, dt=F32):
            return ctx.enter_context(nc.sbuf_tensor(name, shape, dt))

        def sem(name):
            return ctx.enter_context(nc.semaphore(name))

        ring = sb("ring", [P, RING, SLOT])
        con = sb("con", [P, NCON])
        whi, wlo = sb("whi", [P, NSPLIT, D], F32R), sb("wlo", [P, NSPLIT, D], F32R)
        high, low = sb("high", [P, KD * N], F32R), sb("low", [P, KD * N], F32R)
        Xh, Xl = (t[:, :].rearrange("p (k n) -> p k n", k=KD) for t in (high, low))
        xgh, xgl = (t[:, 0:KD * CAP].rearrange("p (k n) -> p k n", k=KD) for t in (high, low))
        hTh, hTl = (t[:, KD * CAP:KD * CAP + 2 * BLK].rearrange("p (b f n) -> p b f n", b=2, f=4) for t in (high, low))
        unit = sb("unit", [NS, NS], F32R)
        vec = sb("vec", [P, NVEC])
        wgr = sb("wgr", [P, KD, RANK])
        wgate = sb("wgate", [P, KD, 2 * MH])
        wrout = sb("wrout", [P, KD, NE])
        wgk = sb("wgk", [RANK, GPAIR * P])
        bgate = sb("bgate", [MH, 2])
        m0 = sb("m0", [MH, NS])
        X = sb("X", [P, KD, N])
        R = sb("R", [P, KD, N])
        SQ = sb("SQ", [P, KD, N])
        state = sb("state", [P, 8256])
        arena = sb("arena", [P, ARENA])
        nm = sb("nm", [P, N])
        lbt = sb("lbt", [P, 3, HG])
        bank = [ctx.enter_context(nc.psum_tensor(f"bank{b}", [P, 512], F32))[:, :] for b in range(8)]

        vsh, vsl = high[0:NS, 0:D], low[0:NS, 0:D]

        spare = lbt[:, 0, 0:1]

        def con_(n):
            a, b = CON[n]
            return con[:, a:b]

        def vec_(n, i=0, w=1):
            a = VEC[n][0] + i
            return vec[:, a:a + w]

        ident, ones = con_("ident"), con_("ones")
        eps, one = con_("eps"), con_("one")

        cur = [0]

        def region(cols, rows=P):
            a = cur[0]
            cur[0] += cols
            assert cur[0] <= ARENA, cur[0]
            return arena[0:rows, a:a + cols]

        q0 = region(HV * N).rearrange("p (j n) -> p j n", j=HV)
        k0 = region(KT * N).rearrange("p (j n) -> p j n", j=KT)
        g0f = region(KT * N)
        g0 = g0f.rearrange("p (j n) -> p j n", j=KT)
        maskf = region(KT * N)
        eq0 = maskf.rearrange("p (j n) -> p j n", j=KT)
        ktok0 = region(KT * 2 * P).rearrange("p (j a n) -> p j a n", j=KT, a=2)
        vtok0f = region(HV * 2 * P)
        vtok0 = vtok0f.rearrange("p (j a n) -> p j a n", j=HV, a=2)
        glt = vtok0f[:, 0:3 * GPAIR * N].rearrange("p (i j n) -> p i j n", i=3, j=GPAIR)
        gate0 = region(HV * N).rearrange("p (j n) -> p j n", j=HV)
        S = region(KT * P).rearrange("p (j n) -> p j n", j=KT)
        Sp = region(KT * P).rearrange("p (j n) -> p j n", j=KT)
        Tmp = region(KT * P).rearrange("p (j n) -> p j n", j=KT)
        prob0 = maskf[:, 0:2 * HV * CH].rearrange("p (a h n) -> p a h n", a=2, h=HV)
        eml = region(3 * KT * NC).rearrange("p (i j c) -> p i j c", i=3, j=KT)
        as0 = region(KT * NS).rearrange("p (j b) -> p j b", j=KT)
        gr_sb = Sp[0:RANK].rearrange("p j n -> p (j n)")[:, 0:N]
        b0f = SQ[:, 0:KT, :].rearrange("p j n -> p (j n)")
        b0 = SQ[:, 0:KT, :]
        o0 = R
        v0 = state[:, 6144:6144 + HV * N].rearrange("p (j n) -> p j n", j=HV)
        S0 = state[:, 0:6144].rearrange("p (j b n) -> p j b n", j=KT, b=NS)

        def chunks(t):
            return t[:, :, 0:NP_].rearrange("p j (c t) -> p j c t", c=NC)

        cur[0] = 0
        hT = region(FD * N).rearrange("p (f n) -> p f n", f=FD)
        sil = region(2 * N).rearrange("p (a n) -> p a n", a=2)
        cur[0] = 0
        up = region(KD * (NP_ + 3)).rearrange("p (j n) -> p j n", j=KD)
        us = region(KD * 4 * NS).rearrange("p (j r b) -> p j r b", j=KD, r=4)
        qk = region(KD * N).rearrange("p (j n) -> p j n", j=KD)
        og = region(KD * N).rearrange("p (j n) -> p j n", j=KD)
        vtokf = region(2 * D)
        vtok = vtokf.rearrange("p (a n) -> p a n", a=2)
        uc = vtokf[:, 0:2 * N].rearrange("p (a n) -> p a n", a=2)
        Dk = region(2 * 384).rearrange("p (a n) -> p a n", a=2)
        Pr = region(2 * 384).rearrange("p (a n) -> p a n", a=2)
        arg = region(2 * 384).rearrange("p (a n) -> p a n", a=2)
        kw = region(2 * 256).rearrange("p (a s n) -> p a s n", a=2, s=2)
        Cout = region(MH * 257).rearrange("p (h n) -> p h n", h=MH)
        acol = region(2 * MH).rearrange("p (s h) -> p s h", s=2)
        fwb = region(MH * 3 * NS).rearrange("p (h w b) -> p h w b", h=MH, w=3)
        n0 = region(MH * NS).rearrange("p (h b) -> p h b", h=MH)
        ki = region(MH * NS).rearrange("p (h b) -> p h b", h=MH)
        qns = region(2 * MH * NS).rearrange("p (i h b) -> p i h b", i=2, h=MH)
        kv = region(MH * 2 * NS).rearrange("p (h v b) -> p h v b", h=MH, v=2)
        qs = region(MH * NS).rearrange("p (h b) -> p h b", h=MH)
        dens = region(MH * NS).rearrange("p (h b) -> p h b", h=MH)
        rows = region(5 * N, MH).rearrange("p (i n) -> p i n", i=5)
        bcrow = region(NP_ + 3 * NS, MH)
        enrow = region(NP_, MH)
        lm = region(NS, MH)
        v1 = SQ
        hsq = qk
        kvb = [SQ[:, 0:4, 0:MDV], SQ[:, 4:8, 0:MDV]]
        Cs = state[:, 0:8192].rearrange("p (h b n) -> p h b n", h=MH, b=NS)
        h1 = R
        cur[0] = 0
        xtok = region(3 * D).rearrange("p (t n) -> p t n", t=3)
        sE = region(BLK)
        hb = region(BLK)
        yE = region(D)
        G = region(3 * CAP).rearrange("p (t n) -> p t n", t=3)
        Gg = region(3 * CAP).rearrange("p (t n) -> p t n", t=3)
        GT = region(N)
        L = region(3 * NE).rearrange("p (t e) -> p t e", t=3)
        mx = region(3 * 8).rearrange("p (t e) -> p t e", t=3)
        oh = region(3 * NE).rearrange("p (t e) -> p t e", t=3)
        sel = region(3 * NE).rearrange("p (t e) -> p t e", t=3)
        gat = region(3 * NE).rearrange("p (t e) -> p t e", t=3)
        rnk = region(3 * NE).rearrange("p (t e) -> p t e", t=3)
        ixf = region(3 * 8).rearrange("p (t e) -> p t e", t=3)
        w12 = region(3 * 3).rearrange("p (i t) -> p i t", i=3)
        NJ = MAXPASS * NE
        jrank = region(3 * NJ).rearrange("p (t j) -> p t j", t=3)
        jgate = region(3 * NJ).rearrange("p (t j) -> p t j", t=3)
        crank = region(3)
        cgate = region(3)
        mcnt = region(4)
        idx = sb("idx", [P, 3, 8], U32)
        nmore = sb("nmore", [1, 1], I32)

        slot_loaded = [sem(f"slot_loaded{i}") for i in range(RING)]
        high_ready, low_ready = sem("high_ready"), sem("low_ready")
        xh_ready, xl_ready = sem("xh_ready"), sem("xl_ready")
        x_loaded, small_loaded, scan_mask_loaded = sem("x_loaded"), sem("small_loaded"), sem("scan_mask_loaded")
        state0_loaded, state1_loaded, conv_loaded = sem("state0_loaded"), sem("state1_loaded"), sem("conv_loaded")
        psum_ready = sem("psum_ready")
        bank_free = [sem(f"bank_free{b}") for b in range(8)]
        act_own, dve_own, pool_own = sem("act_own"), sem("dve_own"), sem("pool_own")
        q_zeroed = sem("q_zeroed")
        lb_diff_ready, lb_ready = sem("lb_diff_ready"), sem("lb_ready")
        gr_ready, sig_ready, f_ready = sem("gr_ready"), sem("sig_ready"), sem("f_ready")
        gla_u_ready, gla_l_ready = sem("gla_u_ready"), sem("gla_l_ready")
        v0_ready = sem("v0_ready")
        dist_ready, expd_ready, expnd_ready = sem("dist_ready"), sem("expd_ready"), sem("expnd_ready")
        qp_ready, kp_ready, ktok_ready, vtok_ready = sem("qp_ready"), sem("kp_ready"), sem("ktok_ready"), sem("vtok_ready")
        unit_ready, vsh_ready = sem("unit_ready"), sem("vsh_ready")
        vs_ready, prob_ready, sp_ready, o_ready = sem("vs_ready"), sem("prob_ready"), sem("sp_ready"), sem("o_ready")
        sdec_ready, snew_ready, s_final = sem("sdec_ready"), sem("snew_ready"), sem("s_final")
        osq_ready, rms_ready, y_ready = sem("osq_ready"), sem("rms_ready"), sem("y_ready")
        r_ready, centred, sq_ready, rstd_ready, scaled, x_ready = (sem("r_ready"), sem("centred"), sem("sq_ready"),
                                                                  sem("rstd_ready"), sem("scaled"), sem("x_ready"))
        silu_ready, h_ready = sem("silu_ready"), sem("h_ready")
        hh_ready, hl_ready, w2_used = sem("hh_ready"), sem("hl_ready"), sem("w2_used")
        u_ready, conv_done, qk_ready, v1_ready, og_ready = (sem("u_ready"), sem("conv_done"), sem("qk_ready"),
                                                            sem("v1_ready"), sem("og_ready"))
        lgi_ready, lga_ready, lgl_ready, rows_ready, exprow_ready = (sem("lgi_ready"), sem("lga_ready"), sem("lgl_ready"),
                                                                     sem("rows_ready"), sem("exprow_ready"))
        arg_ready, decay_ready, p1_ready = sem("arg_ready"), sem("decay_ready"), sem("p1_ready")
        kw_ready, h1_ready, vtok1_ready = sem("kw_ready"), sem("h1_ready"), sem("vtok1_ready")
        vsh1_ready, vs1_ready = sem("vsh1_ready"), sem("vs1_ready")
        fwb_ready, qn_ready, kv_ready, cnew_ready = sem("fwb_ready"), sem("qn_ready"), sem("kv_ready"), sem("cnew_ready")
        qs_ready = sem("qs_ready")
        cout_ready, hs_ready = sem("cout_ready"), sem("hs_ready")
        hc_ready, hsq_ready, hstd_ready, y1_ready = sem("hc_ready"), sem("hsq_ready"), sem("hstd_ready"), sem("y1_ready")
        xtok_ready, route1, route2, sel_ready, jobs_ready, more_ready = (sem("xtok_ready"), sem("route1"), sem("route2"),
                                                                         sem("sel_ready"), sem("jobs_ready"), sem("more_ready"))
        racc_ready = sem("racc_ready")
        gg_ready = sem("gg_ready")
        g_ready, xg_psum, gathered, xgh_ready, xgl_ready = (sem("g_ready"), sem("xg_psum"), sem("gathered"),
                                                            sem("xgh_ready"), sem("xgl_ready"))
        granule_used, whi_ready, wlo_ready = sem("granule_used"), sem("whi_ready"), sem("wlo_ready")
        silE_ready, hb_ready, t_psum, hTh_ready, hT_ready = (sem("silE_ready"), sem("hb_ready"), sem("t_psum"),
                                                             sem("hTh_ready"), sem("hT_ready"))
        y_psum, yE_ready = sem("y_psum"), sem("yE_ready")
        gt_psum, gt_ready, sc_psum, sc_added = sem("gt_psum"), sem("gt_ready"), sem("sc_psum"), sem("sc_added")
        out_ready = sem("out_ready")
        stored0, stored1, stored = sem("stored0"), sem("stored1"), sem("stored")

        loads = []
        for i in range(0, 28, 3):
            loads.append(("w_in0", i, min(3, 28 - i)))
        for i in range(0, 8, 3):
            loads.append(("w_out0", i, min(3, 8 - i)))
        loads += [("w13", i, 1) for i in range(FD)]
        for i in range(0, FD, 3):
            loads.append(("w2", i, min(3, FD - i)))
        for i in range(0, 24, 3):
            loads.append(("w_in1", i, 3))
        for i in range(0, 8, 3):
            loads.append(("w_out1", i, min(3, 8 - i)))
        LS = {(n, i): s for s, (n, i, _) in enumerate(loads)}
        NL = len(loads)

        jobs = ["gr"] + [("z", i) for i in range(4)] + [("glag", 0), ("glag", 1)] + [("z", i) for i in range(4, 28)]
        jobs += [("kt", m) for m in range(KT // 2)] + [("vt", m) for m in range(HV // 2)] + [("vst", 0), ("vst", 1)]
        jobs += [("sc", 0), ("sc", 1), ("u0", 0), ("u1", 0), ("sc", 2), ("sc", 3), ("o", 0),
                 ("u0", 1), ("u1", 1)]
        for c in range(1, NC + 1):
            if c < NC - 1:
                jobs += [("u0", c + 1), ("u1", c + 1)]
            if c < NC:
                jobs += [("o", c)]
            for b in SAMPLES_BEHIND[c]:
                jobs += [("vb0", b), ("vb1", b)]
            if c >= 2:
                jobs += [("os", c - 2)]
        jobs += [("os", NC - 1)] + [("ss", h) for h in range(HV)] + [("mix", 0, j) for j in range(KD)] + [("mean", 0), ("var", 0)]
        for f in range(FD):
            jobs += [("h1", f), ("h3", f)]
        jobs += [("mix", 1, j) for j in range(KD)] + [("mean", 1), ("var", 1)]
        jobs += ["gi", "gf"] + [("y", i) for i in range(20)]
        for g in range(PAIRS):
            jobs += [("y", 20 + g), ("ns", g)]
        jobs += [("vt1", m) for m in range(4)] + [("vs1", 0), ("vs1", 1)] + ["acol"]
        jobs += ["fw", ("bc", 0), ("bc", 1)]
        for h in range(MH + 1):
            if h < MH:
                jobs += [("kt1", h), ("sc1", h), ("en", h)]
            for b in SAMPLES_BEHIND[h]:
                jobs += [("wb", b, 0), ("wb", b, 1)]
            if h == 0:
                jobs += ["qn"]
            if h < MH:
                jobs += [("num", h), ("den", h)]
            if h < MH:
                jobs += [("C", h)]
            if h + 2 < MH:
                jobs += [("bc", h + 2)]
        jobs += [("hm", h) for h in range(MH)] + [("hv", h) for h in range(MH)]
        jobs += [("mix", 2, j) for j in range(KD)] + [("mean", 2), ("var", 2)]
        jobs += [("lg", t) for t in range(3)] + [("xt", t, a) for t in range(3) for a in range(2)] + ["rank", "count"]
        J = {n: i for i, n in enumerate(jobs)}
        NJOB = len(jobs)
        assert len(J) == NJOB

        tiles = [(LS[("w_in0", i - i % 3)], i % 3, ("z", i)) for i in range(28)]
        tiles += [(LS[("w_out0", i - i % 3)], i % 3, ("mix", 0, i)) for i in range(KD)]
        T13 = len(tiles)
        tiles += [(LS[("w13", f)], i, (n, f)) for f in range(FD) for i, n in enumerate(("h1", "h3"))]
        T2 = len(tiles)
        tiles += [(LS[("w2", f - f % 3)], f % 3, ("w2", f)) for f in range(FD)]
        TIN1 = len(tiles)
        tiles += [(LS[("w_in1", i - i % 3)], i % 3, ("y", i)) for i in range(24)]
        TOUT1 = len(tiles)
        tiles += [(LS[("w_out1", i - i % 3)], i % 3, ("mix", 2, i)) for i in range(KD)]
        TOUT0, NT = 28, len(tiles)
        last_tile = {load: n for n, (load, _, _) in enumerate(tiles)}

        def wait_slot_used(eng, load):
            eng.wait_ge(low_ready, last_tile[load] + 1)

        def wait_tile_used(eng, g):
            name = tiles[g][2]
            if name[0] != "w2":
                eng.wait_ge(psum_ready, J[name] + 1)
            elif name[1] < FD - 1:
                eng.wait_ge(w2_used, name[1] + 1)
            else:
                eng.wait_ge(psum_ready, J[("mix", 1, KD - 1)] + 1)

        def wait_h_free(eng, f):
            if f < KD:
                eng.wait_ge(psum_ready, J[("h3", FD - 1)] + 1)
            else:
                eng.wait_ge(w2_used, f - KD + 1)

        def see(eng, name):
            eng.wait_ge(psum_ready, J[name] + 1)
            return bank[J[name] % 8]

        def freed(name):
            return bank_free[J[name] % 8]

        class Own:
            def __init__(self, eng, s):
                self.eng, self.s, self.n = eng, s, 0

            def settle(self, ins):
                ins.then_inc(self.s, 1)
                self.n += 1
                self.eng.wait_ge(self.s, self.n)

            def start(self, ins):
                ins.then_inc(self.s, 1)
                self.n += 1

            def wait(self):
                self.eng.wait_ge(self.s, self.n)

        block = ctx.enter_context(nc.Block())

        @block.sync
        def _(sp):
            sp.dma_start(X[:], A["x"]).then_inc(x_loaded, 16)
            sp.dma_start(wgr[:], A["w_gr"]).then_inc(x_loaded, 16)

            def load(s):
                name, i, n = loads[s]
                if s >= RING:
                    wait_slot_used(sp, s - RING)
                width = A[name].shape[2]
                sp.dma_start(ring[:, s % RING, 0:n * width].rearrange("p (t f) -> p t f", t=n),
                             A[name][i:i + n].rearrange("t p f -> p t f")).then_inc(slot_loaded[s % RING], 16)

            for s in range(NL):
                load(s)
            def expert(job, row0, first=False):
                for f in range(FE):
                    if first and f < RING:
                        wait_slot_used(sp, NL + f - RING)
                    else:
                        sp.wait_ge(wlo_ready, job * GPJ + 3 * (f - RING + 1))
                    sp.dma_start(ring[:, (NL + f) % RING, :],
                                 A["w_moe"][bass.ds(row0 + f, 1)].rearrange("t p f -> p (t f)"))\
                      .then_inc(slot_loaded[(NL + f) % RING], 16)

            expert(0, 0, first=True)
            with sp.Fori(1, NE) as e:
                expert(e, e * FE)
            sp.wait_ge(more_ready, 1)
            more = sp.value_load(nmore[0:1, 0:1], min_val=0, max_val=MAXPASS - 1)
            with sp.If(more > 0):
                with sp.Fori(1, more + 1) as p:
                    with sp.Fori(0, NE) as e:
                        expert(p * NE + e, e * FE)

        @block.tensor
        def _(pe):
            at = [0]

            def job(name):
                assert jobs[at[0]] == name, (jobs[at[0]], name)
                n = at[0]
                at[0] += 1
                if n >= 8:
                    pe.wait_ge(bank_free[n % 8], n // 8)
                return bank[n % 8]

            def done(ins):
                ins.then_inc(psum_ready, 1)

            def product(out, lhs, rhs, k):
                for c in range(k):
                    mm = pe.matmul(out, lhs(c), rhs(c), start=(c == 0), stop=(c == k - 1))
                return mm

            def split_product(out, xh, xl, wh, wl, start, stop):
                pe.matmul(out, xh, wh, start=start, stop=False)
                pe.matmul(out, xh, wl, start=False, stop=False)
                return pe.matmul(out, xl, wh, start=False, stop=stop)

            def projection(first, last, stage):
                for g in range(first, last):
                    out = job(tiles[g][2])[:, 0:N]
                    pe.wait_ge(low_ready, g + 1)
                    for c in range(KD):
                        if g == first:
                            pe.wait_ge(xl_ready, KD * stage + c + 1)
                        w = slice(c * P, (c + 1) * P)
                        mm = split_product(out, whi[:, g % NSPLIT, w], wlo[:, g % NSPLIT, w], Xh[:, c, :], Xl[:, c, :],
                                           c == 0, c == KD - 1)
                    done(mm)

            pe.wait_ge(x_loaded, 32)
            out = job("gr")[0:RANK, 0:N]
            done(product(out, lambda c: wgr[:, c, :], lambda c: X[:, c, :], KD))
            projection(0, 4, 0)
            pe.wait_ge(gr_ready, 1)
            pe.wait_ge(small_loaded, 16 * 7)
            for j in range(GPAIR):
                done(pe.matmul(job(("glag", j))[:, 0:N], wgk[:, j * P:(j + 1) * P], gr_sb, start=True, stop=True))
            projection(4, TOUT0, 0)

            pe.wait_ge(kp_ready, 1)
            for m in range(KT // 2):
                out = job(("kt", m))
                for i in range(4):
                    j, a = 2 * m + i // 2, i % 2
                    mm = pe.transpose(out[:, i * P:(i + 1) * P], k0[:, j, a * P:(a + 1) * P], ident)
                done(mm)
            for m in range(HV // 2):
                pe.wait_ge(v0_ready, 2 * m + 2)
                out = job(("vt", m))
                for i in range(4):
                    j, a = 2 * m + i // 2, i % 2
                    mm = pe.transpose(out[:, i * P:(i + 1) * P], v0[:, j, a * P:(a + 1) * P], ident)
                done(mm)
            for m in range(2):
                out = job(("vst", m))
                for i in range(4):
                    mm = pe.transpose(out[0:NS, i * P:(i + 1) * P], v0[:, 4 * m + i, NP_:N], ident)
                done(mm)

            def rows_of(h):
                if h < HG:
                    return h, 0, P
                return HG + (h - HG) // 2, GLA_DK * ((h - HG) % 2), GLA_DK

            def heads_of(j):
                return (j, j + 1) if j < HG else (2 * j - HG, 2 * j - HG + 2)

            def scores(c):
                out = job(("sc", c))
                lo = CH * (c % 2)
                t = slice(c * CH, (c + 1) * CH)
                for j in range(KT):
                    h0, h1_ = heads_of(j)
                    mm = pe.matmul(out[lo:lo + CH, h0 * CH:h1_ * CH], k0[:, j, t], q0[:, h0:h1_, t], start=True, stop=True)
                done(mm)

            def updates(c):
                lo, a = CH * (c % 2), c // 2
                out = job(("u0", c))
                for h in range(HG):
                    mm = pe.matmul(out[:, h * P:(h + 1) * P], ktok0[lo:lo + CH, h, a, :], vtok0[lo:lo + CH, h, a, :],
                                   start=True, stop=True)
                done(mm)
                out = job(("u1", c))
                for h in range(HG, HV):
                    j, p0, n = rows_of(h)
                    jj = j - HG
                    mm = pe.matmul(out[p0:p0 + n, jj * P:(jj + 1) * P], ktok0[lo:lo + CH, j, a, p0:p0 + n],
                                   vtok0[lo:lo + CH, h, a, :], start=True, stop=True)
                done(mm)

            def outputs(c):
                lo, a = CH * (c % 2), c // 2
                pe.wait_ge(prob_ready, c + 1)
                if c:
                    pe.wait_ge(sp_ready, c)
                out = job(("o", c))
                for j in range(KT):
                    h0, h1_ = heads_of(j)
                    if c:
                        pe.matmul(out[:, h0 * CH:h1_ * CH], Sp[:, j, :], q0[:, h0:h1_, c * CH:(c + 1) * CH],
                                  start=True, stop=False)
                    for h in range(h0, h1_):
                        mm = pe.matmul(out[:, h * CH:(h + 1) * CH], vtok0[lo:lo + CH, h, a, :], prob0[lo:lo + CH, a, h, :],
                                       start=(c == 0), stop=(c == 0 or h == h1_ - 1))
                done(mm)

            def spread(out, b, part):
                pick = bc(unit[:, b:b + 1], [NS, P])
                pe.matmul(out, pick, part(vsh), start=True, stop=False)
                done(pe.matmul(out, pick, part(vsl), start=False, stop=True))

            def sample_outputs(g):
                out = job(("os", g))[:, 0:HV * 2].rearrange("p (h b) -> p h b", h=HV)
                for b in (2 * g, 2 * g + 1):
                    pe.wait_ge(snew_ready, b + 1)
                    for j in range(KT):
                        hh = slice(j, j + 1) if j < HG else slice(2 * j - HG, 2 * j - HG + 2)
                        mm = pe.matmul(out[:, hh, b % 2], S0[:, j, b, :], q0[:, hh, NP_ + b], start=True, stop=True)
                done(mm)

            pe.wait_ge(qp_ready, 1)
            pe.wait_ge(q_zeroed, GL)
            scores(0)
            scores(1)
            pe.wait_ge(ktok_ready, KT // 2)
            pe.wait_ge(vtok_ready, HV // 2)
            updates(0)
            scores(2)
            scores(3)
            outputs(0)
            updates(1)
            pe.wait_ge(unit_ready, 1)
            pe.wait_ge(vs_ready, 2)
            for c in range(1, NC + 1):
                if c < NC - 1:
                    updates(c + 1)
                if c < NC:
                    outputs(c)
                for b in SAMPLES_BEHIND[c]:
                    spread(job(("vb0", b))[:, :], b, lambda v: v[:, 0:HG * P])
                    spread(job(("vb1", b))[:, :], b, lambda v: v[:, HG * P:HV * P])
                if c >= 2:
                    sample_outputs(c - 2)
            sample_outputs(PAIRS - 1)
            for h in range(HV):
                pe.wait_ge(osq_ready, h + 1)
                done(pe.matmul(job(("ss", h))[:, 0:N], ones, SQ[:, h, :], start=True, stop=True))

            def layernorm(n):
                out = job(("mean", n)) if n < 3 else bank[0]
                for k in range(KD):
                    pe.wait_ge(r_ready, KD * n + k + 1)
                    mm = pe.matmul(out[:, 0:N], ones, R[:, k, :], start=(k == 0), stop=(k == KD - 1))
                mm.then_inc(psum_ready, 1)
                out = job(("var", n)) if n < 3 else bank[1]
                for k in range(KD):
                    pe.wait_ge(sq_ready, KD * n + k + 1)
                    mm = pe.matmul(out[:, 0:N], ones, SQ[:, k, :], start=(k == 0), stop=(k == KD - 1))
                mm.then_inc(psum_ready, 1)

            pe.wait_ge(y_ready, HV)
            projection(TOUT0, T13, 1)
            layernorm(0)

            pe.wait_ge(x_ready, KD)
            projection(T13, T2, 2)
            outs = []
            for f in range(FD):
                g = T2 + f
                pe.wait_ge(low_ready, g + 1)
                pe.wait_ge(hl_ready, f + 1)
                for j in range(KD):
                    if f == 0:
                        outs.append(job(("mix", 1, j))[:, 0:N])
                    w = slice(j * P, (j + 1) * P)
                    mm = split_product(outs[j], whi[:, g % NSPLIT, w], wlo[:, g % NSPLIT, w], Xh[:, f % KD, :], Xl[:, f % KD, :],
                                       f == 0, f == FD - 1)
                    if f == FD - 1:
                        done(mm)
                if f < FD - 1:
                    mm.then_inc(w2_used, 1)
            layernorm(1)

            pe.wait_ge(x_ready, 2 * KD)
            for i, nme in enumerate(["gi", "gf"]):
                done(product(job(nme)[0:MH, 0:N], lambda c: wgate[:, c, i * MH:(i + 1) * MH], lambda c: X[:, c, :], KD))
            projection(TIN1, TIN1 + 20, 3)
            pe.wait_ge(state1_loaded, 16)
            pe.wait_ge(qs_ready, 1)
            for g in range(PAIRS):
                projection(TIN1 + 20 + g, TIN1 + 21 + g, 3)
                out = job(("ns", g))
                for b in (2 * g, 2 * g + 1):
                    for i in range(2 * MH):
                        mm = pe.matmul(out[:, 2 * i + b % 2:2 * i + b % 2 + 1], Cs[:, i // 2, b, (i % 2) * P:(i % 2 + 1) * P],
                                       qs[:, i // 2, b:b + 1], start=True, stop=True)
                done(mm)
            for m in range(4):
                pe.wait_ge(v1_ready, 2 * m + 2)
                out = job(("vt1", m))
                for i in range(4):
                    mm = pe.transpose(out[:, i * P:(i + 1) * P], v1[:, 2 * m + i // 2, (i % 2) * P:(i % 2 + 1) * P], ident)
                done(mm)
            for m in range(2):
                out = job(("vs1", m))
                for i in range(4):
                    mm = pe.transpose(out[0:NS, i * P:(i + 1) * P], v1[:, 4 * m + i, NP_:N], ident)
                done(mm)
            def spread_two(h):
                for b in SAMPLES_BEHIND[h]:
                    pe.wait_ge(vs1_ready, 2)
                    for i in range(2):
                        spread(job(("wb", b, i)), b, lambda v: v[:, i * 512:(i + 1) * 512])

            pe.wait_ge(rows_ready, 1)
            out = job("acol")
            for s in range(2):
                mm = pe.transpose(out[:, s * MH:(s + 1) * MH], rows[:, 0, s * P:(s + 1) * P], ident[0:MH, 0:MH])
            done(mm)
            pe.wait_ge(exprow_ready, 1)
            pe.wait_ge(qk_ready, KD)
            picks = [bc(ident[0:MH, h:h + 1], [MH, P]) for h in range(MH)]
            out = job("fw")
            for h in range(MH):
                mm = pe.matmul(out[:, h * 3 * NS:(h + 1) * 3 * NS], picks[h], bcrow[:, NP_:NP_ + 3 * NS], start=True, stop=True)
            done(mm)
            for h in range(2):
                done(pe.matmul(job(("bc", h))[:, 0:NP_], picks[h], bcrow[:, 0:NP_], start=True, stop=True))
            for h in range(MH):
                q, k = qk[:, h, :], qk[:, MH + h, :]
                out = job(("kt1", h))
                for s in range(2):
                    mm = pe.transpose(out[:, s * P:(s + 1) * P], k[:, s * P:(s + 1) * P], ident)
                done(mm)
                out = job(("sc1", h))
                pe.matmul(out[:, 0:NP_], k[:, 0:P], q[:, 0:NP_], start=True, stop=True)
                done(pe.matmul(out[:, NP_:NP_ + P], k[:, P:NP_], q[:, P:NP_], start=True, stop=True))
                done(pe.matmul(job(("en", h))[:, 0:NP_], picks[h], enrow, start=True, stop=True))
                spread_two(h)
                if h == 0:
                    pe.wait_ge(qn_ready, 1)
                    done(pe.matmul(job("qn")[:, 0:2 * MH * NS], ones, qns, start=True, stop=True))
                pe.wait_ge(p1_ready, h + 1)
                if h == 0:
                    pe.wait_ge(vtok1_ready, 4)
                pr = Pr[:, h % 2, :]
                out = job(("num", h))
                for v in range(2):
                    c0 = h * MDV + v * P
                    pe.matmul(out[:, v * NP_:(v + 1) * NP_], vtok[:, 0, c0:c0 + P], pr[:, 0:NP_], start=True, stop=False)
                    mm = pe.matmul(out[:, v * NP_ + P:(v + 1) * NP_], vtok[:, 1, c0:c0 + P], pr[:, NP_:NP_ + P],
                                   start=False, stop=True)
                done(mm)
                out = job(("den", h))
                pe.matmul(out[:, 0:NP_], ones, pr[:, 0:NP_], start=True, stop=False)
                done(pe.matmul(out[:, P:NP_], ones, pr[:, NP_:NP_ + P], start=False, stop=True))
                pe.wait_ge(kw_ready, h + 1)
                out = job(("C", h))
                for s in range(2):
                    pe.matmul(out[:, 0:MDV], kw[:, h % 2, s, :], vtok[:, s, h * MDV:(h + 1) * MDV],
                              start=(s == 0), stop=(s == 1))
                for s in range(2):
                    mm = pe.matmul(out[:, MDV:MDV + 1], kw[:, h % 2, s, :], one, start=(s == 0), stop=(s == 1))
                done(mm)
                if h + 2 < MH:
                    done(pe.matmul(job(("bc", h + 2))[:, 0:NP_], picks[h + 2], bcrow[:, 0:NP_], start=True, stop=True))
            spread_two(MH)
            pe.wait_ge(h1_ready, MH)
            pe.wait_ge(hs_ready, 1)
            for h in range(MH):
                done(product(job(("hm", h))[:, 0:N], lambda c: ones, lambda c: h1[:, 2 * h + c, :], 2))
            for h in range(MH):
                pe.wait_ge(hsq_ready, h + 1)
                done(product(job(("hv", h))[:, 0:N], lambda c: ones, lambda c: hsq[:, 2 * h + c, :], 2))
            pe.wait_ge(y1_ready, MH)
            projection(TOUT1, NT, 4)
            layernorm(2)

            pe.wait_ge(x_ready, 3 * KD)
            for t, (t0, n) in enumerate(TT):
                done(product(job(("lg", t))[0:n, 0:NE], lambda c: X[:, c, t0:t0 + n], lambda c: wrout[:, c, :], KD))
            for t, (t0, n) in enumerate(TT):
                for a in range(2):
                    out = job(("xt", t, a))
                    for i in range(4):
                        mm = pe.transpose(out[0:n, i * P:(i + 1) * P], X[:, 4 * a + i, t0:t0 + n], ident)
                    done(mm)
            pe.wait_ge(sel_ready, 1)
            out = job("rank")
            for t in range(3):
                for s in range(t + 1):
                    mm = pe.matmul(out[:, t * NE:(t + 1) * NE], con_("before") if s == t else ones, sel[:, s, :],
                                   start=(s == 0), stop=(s == t))
            done(mm)
            done(product(job("count")[:, 0:NE], lambda c: ones, lambda c: sel[:, c, :], 3))

            for b in range(8):
                pe.wait_ge(bank_free[b], len(range(b, NJOB, 8)))
            pe.wait_ge(more_ready, 1)
            more = pe.value_load(nmore[0:1, 0:1], min_val=0, max_val=MAXPASS - 1)

            def gather(j):
                pe.wait_ge(g_ready, j + 1)
                for k in range(KD):
                    o = bank[6 + k // 4][:, (k % 4) * P:(k % 4 + 1) * P]
                    for t, (_, n) in enumerate(TT):
                        mm = pe.matmul(o, xtok[0:n, t, k * P:(k + 1) * P], G[0:n, t, :], start=(t == 0), stop=(t == 2))
                    if k % 4 == 3:
                        mm.then_inc(xg_psum, 1)

            def granule(j, g):
                pe.wait_ge(wlo_ready, j * GPJ + (g + 1))
                return whi[:, g % NSPLIT, :], wlo[:, g % NSPLIT, :]

            def hidden(j, b):
                g0_ = W13_AT[b]
                if b == 1:
                    pe.wait_ge(sc_added, j * KD + 1)
                for kp in range(KD // 2):
                    for i in range(2):
                        g = g0_ + 2 * kp + i
                        wh, wl = granule(j, g)
                        for kk in range(2):
                            k = 2 * kp + kk
                            c = slice(kk * BLK, (kk + 1) * BLK)
                            mm = split_product(bank[2 * (b % 2) + i], xgh[:, k, :], xgl[:, k, :], wh[:, c], wl[:, c],
                                               k == 0, k == KD - 1)
                        mm.then_inc(granule_used, 1)
                    if kp == 1 and b > 0:
                        turn(j, b - 1)

            def turn(j, b):
                pe.wait_ge(hb_ready, j * NBLK + (b + 1))
                for i in range(4):
                    mm = pe.transpose(bank[TURN_BANK[b]][:, i * P:(i + 1) * P], hb[:, i * P:(i + 1) * P], ident)
                mm.then_inc(t_psum, 1)

            def down(j, b):
                pe.wait_ge(hT_ready, j * NBLK + (b + 1))
                if b == 0:
                    pe.wait_ge(yE_ready, j * 2 + 1)
                last = b == NBLK - 1
                for step in range(8):
                    f, a = (step % 4, step // 4) if last else (step // 2, step % 2)
                    wh, wl = granule(j, W2_AT[b] + f)
                    c = slice(a * BLK, (a + 1) * BLK)
                    mm = split_product(bank[4 + a], hTh[:, b % 2, f, :], hTl[:, b % 2, f, :], wh[:, c], wl[:, c],
                                       b == 0 and f == 0, last and f == 3)
                    if a == 1:
                        mm.then_inc(granule_used, 1)
                    elif last and f == 3:
                        mm.then_inc(y_psum, 1)

            def expert(j, last=False):
                pe.wait_ge(xgl_ready, j * 2 + 3)
                hidden(j, 0)
                for b in range(1, NBLK):
                    hidden(j, b)
                    down(j, b - 1)
                turn(j, NBLK - 1)
                pe.wait_ge(gg_ready, j + 1)
                for t, (t0, n) in enumerate(TT):
                    mm = pe.transpose(bank[3][:, t0:t0 + n], Gg[0:n, t, :], ident[0:n, 0:n])
                mm.then_inc(gt_psum, 1)
                if not last:
                    gather(j + 1)
                down(j, NBLK - 1)
                pe.wait_ge(gt_ready, j + 1)
                if not last:
                    pe.wait_ge(xgl_ready, j * 2 + 5)
                for k in range(KD):
                    if k % 4 == 0:
                        pe.wait_ge(yE_ready, j * 2 + (k // 4 + 2))
                    if k >= 6:
                        pe.wait_ge(sc_added, j * KD + (k - 4))
                    mm = pe.matmul(bank[SCATTER_BANK[k]][:, 0:N], yE[:, k * P:(k + 1) * P], GT, start=True, stop=True)
                    mm.then_inc(sc_psum, 1)

            pe.wait_ge(jobs_ready, 1)
            pe.wait_ge(xtok_ready, 6)
            for _ in range(NSPLIT):
                pe.nop().then_inc(granule_used, 1)
            gather(0)
            with pe.Fori(0, more * NE + (NE - 1)) as j:
                expert(j)
            expert(more * NE + (NE - 1), last=True)
            layernorm(3)

        @block.scalar
        def _(act):
            own = Own(act, act_own)
            A_ = nc.scalar.activation
            act.dma_start(con[:], A["con"]).then_inc(small_loaded, 16)
            act.dma_start(vec[:], A["vec"]).then_inc(small_loaded, 16)
            act.dma_start(wgk[:], A["w_gk"]).then_inc(small_loaded, 16)
            act.dma_start(wgate[:], A["w_gate"]).then_inc(small_loaded, 16)
            act.dma_start(wrout[:], A["w_router"]).then_inc(small_loaded, 16)
            act.dma_start(bgate[:], A["b_gate"]).then_inc(small_loaded, 16)
            act.dma_start(m0[:], A["m0"]).then_inc(small_loaded, 16)
            act.dma_start(maskf, A["scan_mask"]).then_inc(scan_mask_loaded, 16)
            act.dma_start(state[:, 0:6144], A["state0"]).then_inc(state0_loaded, 16)

            def round_input(src, k):
                A_(Xh[:, k, :], src[:, k, :], ACT.Copy).then_inc(xh_ready, 1)

            def round_tile(g):
                load, part, _ = tiles[g]
                act.wait_ge(slot_loaded[load % RING], 16 * (load // RING + 1))
                if g >= NSPLIT:
                    wait_tile_used(act, g - NSPLIT)
                A_(whi[:, g % NSPLIT, :], ring[:, load % RING, part * D:(part + 1) * D], ACT.Copy).then_inc(high_ready, 1)

            act.wait_ge(x_loaded, 32)
            for k in range(KD):
                round_input(X, k)
            for g in range(NSPLIT):
                round_tile(g)
            act.wait_ge(small_loaded, 16 * 7)
            act.wait_ge(lb_diff_ready, 1)
            A_(lbt[:, 1, :], lbt[:, 0, :], ACT.Sigmoid).then_inc(lb_ready, 1)

            def take(name, out, func, n=N, rows=P, **kw):
                return A_(out, see(act, name)[0:rows, 0:n], func, **kw)

            take("gr", gr_sb, ACT.Copy, rows=RANK).then_inc(freed("gr"), 1)
            act.wait_ge(freed("gr"), 1)
            act.nop().then_inc(gr_ready, 1)
            for h in range(HG):
                round_tile(h + NSPLIT)
                take(("z", h), g0[:, h, :], ACT.Sigmoid).then_inc(sig_ready, 1)
                take(("z", h), k0[:, h, :], ACT.Sigmoid, scale=-1.0).then_inc(freed(("z", h)), 1)
            for h in range(HG):
                round_tile(4 + h + NSPLIT)
                take(("z", 4 + h), q0[:, h, :], ACT.Silu).then_inc(freed(("z", 4 + h)), 1)
            for h in range(HV):
                round_tile(8 + h + NSPLIT)
                take(("z", 8 + h), gate0[:, h, :], ACT.Silu).then_inc(freed(("z", 8 + h)), 1)
            act.wait_ge(f_ready, HG)
            own.start(A_(g0[:, 0:HG, :], g0[:, 0:HG, :], ACT.Ln))
            act.wait_ge(gla_u_ready, GPAIR)
            own.settle(A_(glt[:, 1], glt[:, 0], ACT.Abs))
            own.settle(A_(glt[:, 1], glt[:, 1], ACT.Exp, scale=-1.0))
            A_(glt[:, 1], glt[:, 1], ACT.Ln, bias=one).then_inc(gla_l_ready, 1)
            for j in range(GPAIR):
                round_tile(16 + j + NSPLIT)
                take(("z", 16 + j), k0[:, HG + j, :], ACT.Copy).then_inc(freed(("z", 16 + j)), 1)
            for j in range(GPAIR):
                round_tile(18 + j + NSPLIT)
                z = see(act, ("z", 18 + j))
                for i in range(2):
                    r = slice(GLA_DK * i, GLA_DK * (i + 1))
                    own.start(A_(q0[r, HG + 2 * j + i, :], z[r, 0:N], ACT.Copy, scale=GLA_SCALE))
                own.wait()
                act.nop().then_inc(freed(("z", 18 + j)), 1)
            for h in range(HG):
                round_tile(20 + h + NSPLIT)
                take(("z", 20 + h), v0[:, h, :], ACT.Copy).then_inc(freed(("z", 20 + h)), 1)
            act.wait_ge(dist_ready, 3)
            own.start(A_(chunks(eq0), chunks(g0), ACT.Exp))
            own.start(A_(eml[:, 0], chunks(b0)[:, :, :, CH // 2 - 1], ACT.Exp))
            own.start(A_(eml[:, 1], chunks(b0)[:, :, :, CH - 1], ACT.Exp))
            own.start(A_(as0, b0[:, :, NP_:N], ACT.Exp))
            own.start(A_(eml[:, 2], eml[:, 2], ACT.Exp))
            own.wait()
            act.nop().then_inc(expd_ready, 1)
            own.settle(A_(chunks(g0), chunks(g0), ACT.Exp, scale=-1.0))
            act.nop().then_inc(expnd_ready, 1)
            for h in range(HG, HV):
                round_tile(20 + h + NSPLIT)
                take(("z", 20 + h), v0[:, h, :], ACT.Copy).then_inc(freed(("z", 20 + h)), 1)
            for h in range(HV):
                act.wait_ge(freed(("z", 20 + h)), J[("z", 20 + h)] // 8 + 1)
                act.nop().then_inc(v0_ready, 1)
            act.wait_ge(gla_l_ready, 1)
            act.wait_ge(dist_ready, 3)
            for m in range(HV // 2):
                take(("vt", m), vtok0[:, 2 * m:2 * m + 2].rearrange("p j a n -> p (j a n)"), ACT.Copy, n=512)\
                    .then_inc(freed(("vt", m)), 1)
            for m in range(HV // 2):
                act.wait_ge(freed(("vt", m)), J[("vt", m)] // 8 + 1)
                act.nop().then_inc(vtok_ready, 1)
            for m in range(2):
                take(("vst", m), vsh[:, m * 512:(m + 1) * 512], ACT.Copy, n=512, rows=NS).then_inc(vsh_ready, 1)
            for c in range(NC):
                own.start(A_(o0[:, :, c * CH:(c + 1) * CH], see(act, ("o", c))[:, :].rearrange("p (h t) -> p h t", h=HV),
                             ACT.Copy))
                own.wait()
                act.nop().then_inc(freed(("o", c)), 1)
            for g in range(PAIRS):
                own.start(A_(o0[:, :, NP_ + 2 * g:NP_ + 2 * g + 2],
                             see(act, ("os", g))[:, 0:HV * 2].rearrange("p (h t) -> p h t", h=HV), ACT.Copy))
                own.wait()
                act.nop().then_inc(freed(("os", g)), 1)
            act.nop().then_inc(o_ready, 1)
            for h in range(HV):
                A_(SQ[:, h, :], o0[:, h, :], ACT.Square).then_inc(osq_ready, 1)
            A_(spare, one, ACT.Ln)
            for h in range(HV):
                take(("ss", h), SQ[:, h, :], ACT.Ln, scale=1.0 / P, bias=eps).then_inc(freed(("ss", h)), 1)
            for h in range(HV):
                act.wait_ge(freed(("ss", h)), J[("ss", h)] // 8 + 1)
                A_(SQ[:, h, :], SQ[:, h, :], ACT.Exp, scale=-0.5).then_inc(rms_ready, 1)
            for h in range(HV):
                act.wait_ge(y_ready, h + 1)
                round_input(gate0, h)
            for i in range(KD):
                round_tile(TOUT0 + i + NSPLIT)

            def layernorm(n):
                for k in range(KD):
                    if k % 2 == 0:
                        act.wait_ge(centred, KD // 2 * n + k // 2 + 1)
                    A_(SQ[:, k, :], R[:, k, :], ACT.Square).then_inc(sq_ready, 1)
                A_(spare, one, ACT.Ln)
                if n < 3:
                    out = see(act, ("var", n))
                else:
                    act.wait_ge(psum_ready, NJOB + 2)
                    out = bank[1]
                own.settle(A_(nm[:], out[:, 0:N], ACT.Ln, scale=1.0 / D, bias=eps))
                if n < 3:
                    act.nop().then_inc(freed(("var", n)), 1)
                A_(nm[:], nm[:], ACT.Exp, scale=-0.5).then_inc(rstd_ready, 1)
                for k in range(KD):
                    act.wait_ge(scaled, KD * n + k + 1)
                    A_(X[:, k, :], R[:, k, :], ACT.Identity, bias=vec_(LN_OF[n][1], k)).then_inc(x_ready, 1)
                    if n < 2:
                        A_(Xh[:, k, :], R[:, k, :], ACT.Identity, bias=vec_(LN_OF[n][1], k)).then_inc(xh_ready, 1)

            layernorm(0)
            for f in range(FD):
                if f >= 2:
                    act.wait_ge(h_ready, f - 1)
                own.settle(take(("h1", f), sil[:, f % 2, :], ACT.Silu))
                act.nop().then_inc(freed(("h1", f)), 1)
                act.nop().then_inc(silu_ready, 1)
                round_tile(T13 + 2 * f + NSPLIT)
                round_tile(T13 + 2 * f + 1 + NSPLIT)

            def round_hidden(f):
                act.wait_ge(h_ready, f + 1)
                wait_h_free(act, f)
                A_(Xh[:, f % KD, :], hT[:, f, :], ACT.Copy).then_inc(hh_ready, 1)

            for f in range(HAHEAD):
                round_hidden(f)
            for f in range(FD):
                round_tile(T2 + f + NSPLIT)
                if f + HAHEAD < FD:
                    round_hidden(f + HAHEAD)
            layernorm(1)

            act.wait_ge(stored0, 32)
            act.dma_start(us[:, :, 0:3, :].rearrange("p j r b -> p j (r b)"), A["conv0"]).then_inc(conv_loaded, 16)
            act.dma_start(n0, A["n0"]).then_inc(conv_loaded, 16)
            act.wait_ge(vtok_ready, HV // 2)
            act.dma_start(state[:, 0:8192], A["state1"]).then_inc(state1_loaded, 16)
            act.wait_ge(lgi_ready, 1)
            own.settle(A_(rows[:, 2, :], rows[:, 1, :], ACT.Abs))
            own.settle(A_(rows[:, 2, :], rows[:, 2, :], ACT.Exp, scale=-1.0))
            A_(rows[:, 2, :], rows[:, 2, :], ACT.Ln, bias=one[0:MH]).then_inc(lga_ready, 1)

            def silu_qk(i):
                act.wait_ge(conv_done, i + 1)
                A_(qk[:, i, :], uc[:, i % 2, :], ACT.Silu).then_inc(qk_ready, 1)

            for i in range(KD):
                round_tile(TIN1 + i + NSPLIT)
                if i % 2 == 0 and i > 0:
                    silu_qk(i // 2 - 1)
                take(("y", i), up[:, i, 3:3 + NP_], ACT.Copy, n=NP_).then_inc(u_ready, 1)
                own.start(A_(us[:, i, 3, :], see(act, ("y", i))[:, NP_:N], ACT.Copy))
                act.wait_ge(u_ready, i + 1)
                own.wait()
                act.nop().then_inc(freed(("y", i)), 1)
            for i in range(KD):
                round_tile(TIN1 + KD + i + NSPLIT)
                if i % 2 == 0:
                    silu_qk(KD // 2 + i // 2 - 1)
                own.start(take(("y", 8 + i), v1[:, i, :], ACT.Copy))
                own.wait()
                act.nop().then_inc(freed(("y", 8 + i)), 1)
                act.nop().then_inc(v1_ready, 1)
            for i in range(KD):
                round_tile(TIN1 + 2 * KD + i + NSPLIT)
                if i == 0:
                    silu_qk(KD - 1)
                own.settle(take(("y", 16 + i), og[:, i, :], ACT.Sigmoid))
                act.nop().then_inc(freed(("y", 16 + i)), 1)
            act.nop().then_inc(og_ready, 1)
            act.wait_ge(lgl_ready, 1)
            own.start(A_(enrow, rows[:, 4, 0:NP_], ACT.Exp, scale=-1.0))
            own.start(A_(bcrow[:, NP_:NP_ + 2 * NS], bcrow[:, NP_:NP_ + 2 * NS], ACT.Exp))
            own.start(A_(bcrow[:, NP_ + 2 * NS:NP_ + 3 * NS], rows[:, 4, NP_:N], ACT.Exp, scale=-1.0))
            own.wait()
            act.nop().then_inc(exprow_ready, 1)
            act.wait_ge(qk_ready, KD)
            for m in range(4):
                for s in range(2):
                    own.start(A_(vtok[:, s, 2 * m * P:(2 * m + 2) * P].rearrange("p (j n) -> p j n", j=2),
                                 see(act, ("vt1", m))[:, :].rearrange("p (j s n) -> p j s n", j=2, s=2)[:, :, s, :],
                                 ACT.Copy))
                own.wait()
                act.nop().then_inc(freed(("vt1", m)), 1)
                act.nop().then_inc(vtok1_ready, 1)
            for m in range(2):
                take(("vs1", m), vsh[:, m * 512:(m + 1) * 512], ACT.Copy, n=512, rows=NS).then_inc(vsh1_ready, 1)
            own.settle(take("acol", acol.rearrange("p s h -> p (s h)"), ACT.Copy, n=2 * MH))
            act.nop().then_inc(freed("acol"), 1)

            def decays(h):
                act.wait_ge(arg_ready, h + 1)
                if h >= 2:
                    act.wait_ge(kw_ready, h - 1)
                own.start(A_(Dk[:, h % 2, 0:NP_], arg[:, h % 2, 0:NP_], ACT.Exp, bias=acol[:, 0, h:h + 1]))
                own.start(A_(Dk[:, h % 2, NP_:384], arg[:, h % 2, NP_:384], ACT.Exp, bias=acol[:, 1, h:h + 1]))
                own.wait()
                act.nop().then_inc(decay_ready, 1)

            def outer_products(h):
                for b in SAMPLES_BEHIND[h]:
                    if b >= 2:
                        act.wait_ge(cnew_ready, b - 1)
                    for i in range(2):
                        wb = see(act, ("wb", b, i))
                        for n in range(2):
                            own.start(A_(kvb[b % 2][:, 2 * i + n, :], wb[:, n * MDV:(n + 1) * MDV], ACT.Copy,
                                         scale=ki[:, 2 * i + n, b:b + 1]))
                        own.wait()
                        act.nop().then_inc(freed(("wb", b, i)), 1)
                    act.nop().then_inc(kv_ready, 1)

            decays(0)
            decays(1)
            for h in range(MH):
                outer_products(h)
                own.settle(take(("C", h), Cout[:, h, :], ACT.Copy, n=257))
                act.nop().then_inc(freed(("C", h)), 1)
                act.nop().then_inc(cout_ready, 1)
                if h + 2 < MH:
                    decays(h + 2)
            outer_products(MH)
            for h in range(MH):
                act.wait_ge(hc_ready, h + 1)
                A_(hsq[:, 2 * h:2 * h + 2, :], h1[:, 2 * h:2 * h + 2, :], ACT.Square).then_inc(hsq_ready, 1)
            A_(spare, one, ACT.Ln)
            for h in range(MH):
                take(("hv", h), hsq[:, 2 * h, :], ACT.Ln, scale=1.0 / MDV, bias=eps).then_inc(freed(("hv", h)), 1)
            for h in range(MH):
                act.wait_ge(freed(("hv", h)), J[("hv", h)] // 8 + 1)
                A_(hsq[:, 2 * h, :], hsq[:, 2 * h, :], ACT.Exp, scale=-0.5).then_inc(hstd_ready, 1)
            for h in range(MH):
                act.wait_ge(y1_ready, h + 1)
                round_input(og, 2 * h)
                round_input(og, 2 * h + 1)
            for g in range(TOUT1 + NSPLIT, NT):
                round_tile(g)
            act.wait_ge(cnew_ready, NS)
            layernorm(2)

            def round_granule(j, g, first=False):
                s = NL + g // 3
                if g % 3 == 0:
                    act.wait_ge(slot_loaded[s % RING], 16 * (s // RING + 1) + j * (16 * FE // RING))
                if not first:
                    act.wait_ge(granule_used, j * GPJ + (g + 1))
                A_(whi[:, g % NSPLIT, :], ring[:, s % RING, (g % 3) * D:(g % 3 + 1) * D], ACT.Copy).then_inc(whi_ready, 1)

            for g in range(NSPLIT):
                round_granule(0, g, first=True)

            act.wait_ge(stored1, 16 * 5)
            act.wait_ge(route1, 1)
            A_(w12[:, 0, :], w12[:, 0, :], ACT.Exp).then_inc(route2, 1)
            for t, (t0, n) in enumerate(TT):
                for a in range(2):
                    own.settle(take(("xt", t, a), xtok[0:n, t, a * 512:(a + 1) * 512], ACT.Copy, n=512, rows=n))
                    act.nop().then_inc(freed(("xt", t, a)), 1)
                    act.nop().then_inc(xtok_ready, 1)
            act.wait_ge(more_ready, 1)
            more = act.value_load(nmore[0:1, 0:1], min_val=0, max_val=MAXPASS - 1)

            def take_gathered(j):
                for a in range(2):
                    act.wait_ge(xg_psum, j * 2 + (a + 1))
                    A_(xgh[:, 4 * a:4 * a + 4, :].rearrange("p k n -> p (k n)"), bank[6 + a], ACT.Copy)\
                        .then_inc(xgh_ready, 1)

            def expert(j, last=False):
                for g in range(NSPLIT, GPJ):
                    round_granule(j, g)
                    if g in SILU_AT:
                        b = SILU_AT[g]
                        act.wait_ge(granule_used, j * GPJ + (W13_AT[b] + 8 + NSPLIT))
                        A_(sE, bank[2 * (b % 2)], ACT.Silu).then_inc(silE_ready, 1)
                    if g in TURNED_AT:
                        b = TURNED_AT[g]
                        act.wait_ge(t_psum, j * NBLK + (b + 1))
                        A_(hTh[:, b % 2].rearrange("p f n -> p (f n)"), bank[TURN_BANK[b]], ACT.Copy).then_inc(hTh_ready, 1)
                act.wait_ge(gt_psum, j + 1)
                A_(GT, bank[3][:, 0:N], ACT.Copy).then_inc(gt_ready, 1)
                if not last:
                    take_gathered(j + 1)
                act.wait_ge(y_psum, j + 1)
                A_(yE[:, 0:BLK], bank[4], ACT.Copy).then_inc(yE_ready, 1)
                if not last:
                    for g in range(GPJ, GPJ + NSPLIT - 1):
                        round_granule(j, g)
                act.wait_ge(granule_used, j * GPJ + (GPJ + NSPLIT))
                A_(yE[:, BLK:D], bank[5], ACT.Copy).then_inc(yE_ready, 1)
                if not last:
                    round_granule(j, GPJ + NSPLIT - 1)

            take_gathered(0)
            act.nop().then_inc(yE_ready, 1)
            with act.Fori(0, more * NE + (NE - 1)) as j:
                expert(j)
            expert(more * NE + (NE - 1), last=True)
            layernorm(3)

        @block.vector
        def _(dve):
            own = Own(dve, dve_own)
            V = nc.vector

            def rest_of_input(src, k, stage):
                dve.wait_ge(xh_ready, KD * stage + k + 1)
                V.tensor_tensor(Xl[:, k, :], src[:, k, :], Xh[:, k, :].bitcast(F32), ALU.subtract).then_inc(xl_ready, 1)

            def rest_of_tiles(first, last):
                for g in range(first, last):
                    load, part, _ = tiles[g]
                    dve.wait_ge(high_ready, g + 1)
                    V.tensor_tensor(wlo[:, g % NSPLIT, :], ring[:, load % RING, part * D:(part + 1) * D],
                                    whi[:, g % NSPLIT, :].bitcast(F32), ALU.subtract).then_inc(low_ready, 1)

            for k in range(KD):
                rest_of_input(X, k, 0)
            rest_of_tiles(0, NSPLIT)
            dve.wait_ge(small_loaded, 16 * 7)
            V.tensor_tensor(lbt[:, 0, :], vec_("lb0", 0, HG), vec_("lb1", 0, HG), ALU.subtract).then_inc(lb_diff_ready, 1)
            dve.wait_ge(lb_ready, 1)
            own.settle(V.tensor_scalar(lbt[:, 2, :], lbt[:, 1, :], -1.0, 1.0, ALU.mult, ALU.add))
            V.tensor_copy(unit[:], ident[0:NS, 0:NS]).then_inc(unit_ready, 1)
            for h in range(HG):
                dve.wait_ge(sig_ready, h + 1)
                own.start(V.tensor_scalar(g0[:, h, :], g0[:, h, :], lbt[:, 2, h:h + 1], lbt[:, 1, h:h + 1], ALU.mult, ALU.add))
                dve.wait_ge(freed(("z", h)), J[("z", h)] // 8 + 1)
                own.start(V.tensor_scalar(k0[:, h, :], k0[:, h, :], lbt[:, 2, h:h + 1], None, ALU.mult))
                own.wait()
                dve.nop().then_inc(f_ready, 1)
                rest_of_tiles(NSPLIT + h, NSPLIT + h + 1)
            for j in range(GPAIR):
                own.settle(V.tensor_scalar(glt[:, 0, j, :], see(dve, ("glag", j))[:, 0:N], vec_("bgk", j), None, ALU.add))
                V.tensor_scalar(glt[:, 2, j, :], glt[:, 0, j, :], 0.0, None, ALU.min).then_inc(gla_u_ready, 1)
                dve.wait_ge(gla_u_ready, j + 1)
                dve.nop().then_inc(freed(("glag", j)), 1)
            rest_of_tiles(8, 20)
            dve.wait_ge(gla_l_ready, 1)
            own.settle(V.tensor_tensor(glt[:, 2], glt[:, 2], glt[:, 1], ALU.subtract))
            own.settle(V.tensor_scalar(g0[:, HG:KT, :], glt[:, 2], 1.0 / GATE_NORM, None, ALU.mult))
            dve.wait_ge(scan_mask_loaded, 16)
            own.settle(V.tensor_tensor_scan(b0f, maskf, g0f, 0.0, ALU.mult, ALU.add))
            bb = chunks(b0)
            V.tensor_tensor(chunks(g0), bb, bc(bb[:, :, :, CH // 2 - 1:CH // 2], [P, KT, NC, CH]), ALU.subtract)\
                .then_inc(dist_ready, 1)
            V.tensor_tensor(eml[:, 2], bb[:, :, :, CH - 1], bb[:, :, :, CH // 2 - 1], ALU.subtract).then_inc(dist_ready, 1)
            dve.wait_ge(dist_ready, 2)
            dve.nop().then_inc(dist_ready, 1)
            rest_of_tiles(20, 28)
            dve.wait_ge(expd_ready, 1)
            dve.wait_ge(freed(("z", 19)), J[("z", 19)] // 8 + 1)
            dve.wait_ge(f_ready, HG)
            dve.wait_ge(q_zeroed, GL)
            qc = q0[:, 0:HG, 0:NP_]
            own.start(V.tensor_tensor(qc, qc, eq0[:, 0:HG, 0:NP_], ALU.mult))
            for j in range(GPAIR):
                qc = q0[:, HG + 2 * j:HG + 2 * j + 2, 0:NP_]
                own.start(V.tensor_tensor(qc, qc, bc(eq0[:, HG + j:HG + j + 1, 0:NP_], [P, 2, NP_]), ALU.mult))
            own.wait()
            dve.nop().then_inc(qp_ready, 1)
            dve.wait_ge(expnd_ready, 1)
            V.tensor_tensor(chunks(k0), chunks(k0), chunks(g0), ALU.mult).then_inc(kp_ready, 1)
            for m in range(KT // 2):
                own.settle(V.tensor_copy(ktok0[:, 2 * m:2 * m + 2].rearrange("p j a n -> p (j a n)"), see(dve, ("kt", m))[:, :]))
                dve.nop().then_inc(freed(("kt", m)), 1)
                dve.wait_ge(freed(("kt", m)), J[("kt", m)] // 8 + 1)
                dve.nop().then_inc(ktok_ready, 1)

            def split_values(name, high_ready, split_ready):
                for m in range(2):
                    dve.wait_ge(high_ready, m + 1)
                    cols = slice(m * 512, (m + 1) * 512)
                    own.settle(V.tensor_tensor(vsl[:, cols], see(dve, (name, m))[0:NS, :], vsh[:, cols].bitcast(F32),
                                               ALU.subtract))
                    dve.nop().then_inc(freed((name, m)), 1)
                    dve.nop().then_inc(split_ready, 1)

            split_values("vst", vsh_ready, vs_ready)
            rest_of_tiles(TOUT0, TOUT0 + NSPLIT)

            def probabilities(c):
                lo = CH * (c % 2)
                own.settle(V.tensor_tensor(prob0[lo:lo + CH, c // 2],
                                           see(dve, ("sc", c))[lo:lo + CH, :].rearrange("p (h n) -> p h n", h=HV),
                                           bc(con_("causal64")[lo:lo + CH].unsqueeze(1), [CH, HV, CH]), ALU.mult))
                dve.nop().then_inc(freed(("sc", c)), 1)
                dve.wait_ge(freed(("sc", c)), J[("sc", c)] // 8 + 1)
                dve.nop().then_inc(prob_ready, 1)

            def factor(i, c, j0=0, j1=KT):
                return bc(eml[:, i, j0:j1, c:c + 1], [P, j1 - j0, P])

            def advance(c):
                target = S if c == 0 else Tmp
                for nme, j0, j1 in (("u0", 0, HG), ("u1", HG, KT)):
                    own.settle(V.tensor_tensor(target[:, j0:j1, :],
                                               see(dve, (nme, c))[:, 0:(j1 - j0) * P].rearrange("p (j n) -> p j n", n=P),
                                               factor(2, c, j0, j1), ALU.mult))
                    dve.nop().then_inc(freed((nme, c)), 1)
                if c:
                    own.settle(V.tensor_tensor(S, S, factor(1, c), ALU.mult))
                    own.settle(V.tensor_tensor(S, S, Tmp, ALU.add))
                if c < NC - 1:
                    if c:
                        dve.wait_ge(psum_ready, J[("o", c)] + 1)
                    V.tensor_tensor(Sp, S, factor(0, c + 1), ALU.mult).then_inc(sp_ready, 1)
                else:
                    dve.nop().then_inc(s_final, 1)

            probabilities(0)
            probabilities(1)
            advance(0)
            probabilities(2)
            probabilities(3)
            for c in range(1, NC + 1):
                if c < NC:
                    advance(c)
                if c == 1:
                    dve.wait_ge(sdec_ready, 1)
                for b in SAMPLES_BEHIND[c]:
                    own.start(V.tensor_tensor(Tmp[:, 0:HG, :], see(dve, ("vb0", b))[:, :].rearrange("p (j n) -> p j n", j=HG),
                                              bc(k0[:, 0:HG, NP_ + b:NP_ + b + 1], [P, HG, P]), ALU.mult))
                    v = see(dve, ("vb1", b))[:, :].rearrange("p (h n) -> p h n", h=GL)
                    for i in range(2):
                        r = slice(GLA_DK * i, GLA_DK * (i + 1))
                        own.start(V.tensor_tensor(Tmp[r, HG:KT, :], v[r, i:GL:2, :],
                                                  bc(k0[r, HG:KT, NP_ + b:NP_ + b + 1], [GLA_DK, GPAIR, P]), ALU.mult))
                    own.wait()
                    for nme in ("vb0", "vb1"):
                        dve.nop().then_inc(freed((nme, b)), 1)
                    V.tensor_tensor(S0[:, :, b, :], S0[:, :, b, :], Tmp, ALU.add).then_inc(snew_ready, 1)
                    dve.wait_ge(snew_ready, b + 1)
            dve.wait_ge(o_ready, 1)
            dve.wait_ge(freed(("z", 15)), J[("z", 15)] // 8 + 1)
            for h in range(HV):
                w = vec_("gn_hg") if h < HG else vec_("gn_gla")
                dve.wait_ge(rms_ready, h + 1)
                own.settle(V.scalar_tensor_tensor(out=o0[:, h, :], in0=o0[:, h, :], scalar=w, in1=SQ[:, h, :],
                                                  op0=ALU.mult, op1=ALU.mult))
                V.tensor_tensor(gate0[:, h, :], gate0[:, h, :], o0[:, h, :], ALU.mult).then_inc(y_ready, 1)
                dve.wait_ge(y_ready, h + 1)
                if h:
                    rest_of_input(gate0, h - 1, 1)
            rest_of_input(gate0, HV - 1, 1)

            SPLIT_IN = {0: [(TOUT0 + NSPLIT + k,) for k in range(KD)],
                        1: [()] * KD,
                        2: [(TOUT1 + NSPLIT + k,) for k in range(NSPLIT)] + [()] * 4}

            def residual(n):
                for k in range(KD):
                    for g in SPLIT_IN[n][k]:
                        rest_of_tiles(g, g + 1)
                    V.scalar_tensor_tensor(out=R[:, k, :], in0=X[:, k, :], scalar=ALPHA, in1=see(dve, ("mix", n, k))[:, 0:N],
                                           op0=ALU.mult, op1=ALU.add).then_inc(r_ready, 1)
                    dve.wait_ge(r_ready, KD * n + k + 1)
                    dve.nop().then_inc(freed(("mix", n, k)), 1)

            def layernorm(n):
                if n < 3:
                    out = see(dve, ("mean", n))
                else:
                    dve.wait_ge(psum_ready, NJOB + 1)
                    out = bank[0]
                for i in range(KD // 2):
                    r = R[:, 2 * i:2 * i + 2, :]
                    V.scalar_tensor_tensor(out=r, in0=bc(out[:, 0:N].unsqueeze(1), [P, 2, N]), scalar=-1.0 / D, in1=r,
                                           op0=ALU.mult, op1=ALU.add).then_inc(centred, 1)
                dve.wait_ge(rstd_ready, n + 1)
                dve.wait_ge(centred, KD // 2 * (n + 1))
                if n < 3:
                    dve.nop().then_inc(freed(("mean", n)), 1)
                for k in range(KD + 2):
                    if k < KD:
                        V.scalar_tensor_tensor(out=R[:, k, :], in0=R[:, k, :], scalar=vec_(LN_OF[n][0], k), in1=nm[:],
                                               op0=ALU.mult, op1=ALU.mult).then_inc(scaled, 1)
                    if n < 2 and k >= 2:
                        rest_of_input(X, k - 2, n + 2)
                dve.wait_ge(x_ready, KD * (n + 1))

            residual(0)
            layernorm(0)
            for f in range(FD):
                dve.wait_ge(silu_ready, f + 1)
                V.tensor_tensor(hT[:, f, :], sil[:, f % 2, :], see(dve, ("h3", f))[:, 0:N], ALU.mult).then_inc(h_ready, 1)
                dve.wait_ge(h_ready, f + 1)
                dve.nop().then_inc(freed(("h3", f)), 1)
                rest_of_tiles(T13 + 2 * f + NSPLIT, T13 + 2 * f + NSPLIT + 2)

            def rest_of_hidden(f):
                dve.wait_ge(hh_ready, f + 1)
                V.tensor_tensor(Xl[:, f % KD, :], hT[:, f, :], Xh[:, f % KD, :].bitcast(F32), ALU.subtract).then_inc(hl_ready, 1)

            for f in range(HAHEAD):
                rest_of_hidden(f)
            for f in range(FD):
                rest_of_tiles(T2 + f + NSPLIT, T2 + f + NSPLIT + 1)
                if f + HAHEAD < FD:
                    rest_of_hidden(f + HAHEAD)
            residual(1)
            layernorm(1)

            dve.wait_ge(stored0, 32)
            own.start(V.tensor_scalar(rows[:, 0, :], see(dve, "gi")[0:MH, 0:N], bgate[:, 0:1], None, ALU.add))
            own.start(V.tensor_scalar(rows[:, 1, :], see(dve, "gf")[0:MH, 0:N], bgate[:, 1:2], None, ALU.add))
            own.start(V.memset(up[:, :, 0:3], 0.0))
            own.wait()
            dve.nop().then_inc(freed("gi"), 1)
            dve.nop().then_inc(freed("gf"), 1)
            dve.nop().then_inc(lgi_ready, 1)
            dve.wait_ge(conv_loaded, 32)
            for i in range(KD):
                rest_of_tiles(TIN1 + 2 * i + NSPLIT, TIN1 + 2 * i + 2 + NSPLIT)
                dve.wait_ge(freed(("y", i)), J[("y", i)] // 8 + 1)
                if i >= 2:
                    dve.wait_ge(qk_ready, i - 1)
                for r in range(4):
                    w = vec_(f"convw{r}", i)
                    for out, src in ((uc[:, i % 2, 0:NP_], up[:, i, r:r + NP_]), (uc[:, i % 2, NP_:N], us[:, i, r, :])):
                        if r == 0:
                            ins = V.tensor_scalar(out, src, w, vec_("convb", i), ALU.mult, ALU.add)
                        else:
                            ins = V.scalar_tensor_tensor(out=out, in0=src, scalar=w, in1=out, op0=ALU.mult, op1=ALU.add)
                        own.start(ins)
                    own.wait()
                dve.nop().then_inc(conv_done, 1)
            rest_of_tiles(TIN1 + 2 * KD + NSPLIT, TIN1 + 2 * KD + NSPLIT + 2)
            dve.wait_ge(qk_ready, MH)
            V.tensor_scalar(qs, qk[:, 0:MH, NP_:N], ML_SCALE, None, ALU.mult).then_inc(qs_ready, 1)
            dve.wait_ge(qs_ready, 1)
            own.settle(V.tensor_scalar(rows[:, 3, :], rows[:, 1, :], 0.0, None, ALU.min))
            dve.wait_ge(lga_ready, 1)
            own.settle(V.tensor_tensor(rows[:, 1, :], rows[:, 3, :], rows[:, 2, :], ALU.subtract))
            pr = slice(0, NP_)
            sm = slice(NP_, N)
            own.settle(V.tensor_tensor_scan(rows[:, 2, pr], bc(one[0:MH], [MH, NP_]), rows[:, 1, pr], 0.0, ALU.mult, ALU.add))
            own.settle(V.tensor_tensor(lm, rows[:, 1, sm], m0[:], ALU.add))
            own.settle(V.tensor_tensor(rows[:, 4, sm], lm, rows[:, 0, sm], ALU.max))
            own.start(V.tensor_tensor(bcrow[:, NP_:NP_ + NS], rows[:, 0, sm], rows[:, 4, sm], ALU.subtract))
            own.start(V.tensor_tensor(bcrow[:, NP_ + NS:NP_ + 2 * NS], lm, rows[:, 4, sm], ALU.subtract))
            own.settle(V.tensor_tensor(rows[:, 0, pr], rows[:, 0, pr], rows[:, 2, pr], ALU.subtract))
            own.settle(V.tensor_tensor_scan(rows[:, 3, pr], rows[:, 0, pr], rows[:, 0, pr], 0.0, ALU.max, ALU.max))
            own.start(V.tensor_tensor(rows[:, 4, pr], rows[:, 2, pr], rows[:, 3, pr], ALU.add))
            own.start(V.tensor_scalar(bcrow[:, 0:NP_], rows[:, 3, pr], -1.0, None, ALU.mult))
            own.wait()
            dve.nop().then_inc(rows_ready, 1)
            dve.nop().then_inc(lgl_ready, 1)
            rest_of_tiles(TIN1 + 2 * KD + NSPLIT + 2, TOUT1 + NSPLIT)
            for g in range(PAIRS):
                ns = see(dve, ("ns", g))[:, 0:MH * 4].rearrange("p (h v b) -> p h v b", h=MH, v=2)
                for v in range(2):
                    own.start(V.tensor_copy(h1[:, v:KD:2, NP_ + 2 * g:NP_ + 2 * g + 2], ns[:, :, v, :]))
                own.wait()
                dve.nop().then_inc(freed(("ns", g)), 1)
            dve.wait_ge(qk_ready, KD)
            split_values("vs1", vsh1_ready, vs1_ready)

            def arguments(h):
                a, neg = h % 2, con_("neg")
                m = see(dve, ("bc", h))
                own.start(V.tensor_tensor(arg[:, a, 0:P], m[:, 0:P], neg, ALU.add))
                own.start(V.tensor_copy(arg[:, a, P:NP_], m[:, P:NP_]))
                own.start(V.tensor_tensor(arg[:, a, NP_:384], m[:, P:NP_], neg, ALU.add))
                own.wait()
                dve.nop().then_inc(freed(("bc", h)), 1)
                dve.nop().then_inc(arg_ready, 1)

            own.settle(V.tensor_copy(fwb.rearrange("p h w b -> p (h w b)"), see(dve, "fw")[:, 0:MH * 3 * NS]))
            dve.nop().then_inc(freed("fw"), 1)
            dve.nop().then_inc(fwb_ready, 1)
            arguments(0)
            arguments(1)
            own.settle(V.tensor_tensor(ki, qk[:, MH:2 * MH, NP_:N], fwb[:, :, 0, :], ALU.mult))
            own.settle(V.tensor_tensor(n0, n0, fwb[:, :, 1, :], ALU.mult))
            own.settle(V.tensor_tensor(n0, n0, ki, ALU.add))
            own.start(V.tensor_tensor(qns[:, 0], n0, qs, ALU.mult))
            own.start(V.tensor_tensor(qns[:, 1], ki, qs, ALU.mult))
            own.wait()
            dve.nop().then_inc(qn_ready, 1)
            for h in range(MH):
                a = h % 2
                dve.wait_ge(decay_ready, h + 1)
                if h >= 2:
                    dve.wait_ge(psum_ready, J[("C", h - 2)] + 1)
                kt = see(dve, ("kt1", h))
                own.start(V.tensor_scalar(kw[:, a, 0, :], kt[:, 0:P], Dk[:, a, NP_ - 1:NP_], None, ALU.mult))
                own.start(V.tensor_scalar(kw[:, a, 1, :], kt[:, P:2 * P], Dk[:, a, 383:384], None, ALU.mult))
                own.start(V.scalar_tensor_tensor(out=Pr[:, a, :], in0=see(dve, ("sc1", h))[:, 0:384], scalar=ML_SCALE,
                                                 in1=Dk[:, a, :], op0=ALU.mult, op1=ALU.mult))
                own.wait()
                for s_ in (freed(("kt1", h)), freed(("sc1", h)), p1_ready, kw_ready):
                    dve.nop().then_inc(s_, 1)
                if 2 <= h + 1 < MH:
                    arguments(h + 1)
                if h == 0:
                    qn = see(dve, "qn")[:, 0:MH * NS].rearrange("p (h b) -> p h b", h=MH)
                    own.settle(V.tensor_scalar(dens, qn, -1.0, None, ALU.mult))
                    own.settle(V.tensor_tensor(dens, dens, qn, ALU.max))
                    own.settle(V.tensor_tensor(dens, dens, fwb[:, :, 2, :], ALU.max))
                    own.settle(V.reciprocal(dens, dens))
                    def over_v(t):
                        return bc(t.unsqueeze(2), [P, MH, 2, NS])
                    hs = h1[:, :, NP_:N].rearrange("p (h v) b -> p h v b", v=2)
                    kq = see(dve, "qn")[:, MH * NS:2 * MH * NS].rearrange("p (h b) -> p h b", h=MH)
                    own.start(V.tensor_tensor(kv, v1[:, :, NP_:N].rearrange("p (h v) b -> p h v b", v=2), over_v(kq), ALU.mult))
                    own.settle(V.tensor_tensor(hs, hs, over_v(fwb[:, :, 1, :]), ALU.mult))
                    dve.nop().then_inc(freed("qn"), 1)
                    own.settle(V.tensor_tensor(hs, hs, kv, ALU.add))
                    own.settle(V.tensor_tensor(hs, hs, over_v(dens), ALU.mult))
                    dve.nop().then_inc(hs_ready, 1)
                t1, t2 = arg[:, a, 0:NP_], nm[:, 0:NP_]
                own.settle(V.tensor_scalar(t1, see(dve, ("den", h))[:, 0:NP_], -1.0, None, ALU.mult))
                own.settle(V.tensor_tensor(t1, t1, see(dve, ("den", h))[:, 0:NP_], ALU.max))
                own.settle(V.tensor_tensor(t1, t1, see(dve, ("en", h))[:, 0:NP_], ALU.max))
                own.settle(V.reciprocal(t2, t1))
                own.settle(V.tensor_tensor(h1[:, 2 * h:2 * h + 2, 0:NP_],
                                           see(dve, ("num", h))[:, :].rearrange("p (v n) -> p v n", v=2),
                                           bc(t2.unsqueeze(1), [P, 2, NP_]), ALU.mult))
                for s_ in (freed(("den", h)), freed(("en", h)), freed(("num", h)), h1_ready):
                    dve.nop().then_inc(s_, 1)
            for h in range(MH):
                hh = h1[:, 2 * h:2 * h + 2, :]
                V.scalar_tensor_tensor(out=hh, in0=bc(see(dve, ("hm", h))[:, 0:N].unsqueeze(1), [P, 2, N]),
                                       scalar=-1.0 / MDV, in1=hh, op0=ALU.mult, op1=ALU.add).then_inc(hc_ready, 1)
            dve.wait_ge(hc_ready, MH)
            for h in range(MH):
                dve.nop().then_inc(freed(("hm", h)), 1)
            dve.wait_ge(og_ready, 1)
            for h in range(MH):
                dve.wait_ge(hstd_ready, h + 1)
                for v in range(2):
                    own.settle(V.scalar_tensor_tensor(out=h1[:, 2 * h + v, :], in0=h1[:, 2 * h + v, :],
                                                      scalar=vec_("hn", 2 * h + v), in1=hsq[:, 2 * h, :],
                                                      op0=ALU.mult, op1=ALU.mult))
                own.settle(V.tensor_tensor(og[:, 2 * h:2 * h + 2, :], og[:, 2 * h:2 * h + 2, :],
                                           h1[:, 2 * h:2 * h + 2, :], ALU.mult))
                dve.nop().then_inc(y1_ready, 1)
                if h:
                    rest_of_input(og, 2 * h - 2, 4)
                    rest_of_input(og, 2 * h - 1, 4)
            rest_of_input(og, KD - 2, 4)
            rest_of_input(og, KD - 1, 4)
            residual(2)
            layernorm(2)

            def rest_of_granule(j, g):
                s = NL + g // 3
                dve.wait_ge(whi_ready, j * GPJ + (g + 1))
                V.tensor_tensor(wlo[:, g % NSPLIT, :], ring[:, s % RING, (g % 3) * D:(g % 3 + 1) * D],
                                whi[:, g % NSPLIT, :].bitcast(F32), ALU.subtract).then_inc(wlo_ready, 1)

            for g in range(NSPLIT):
                rest_of_granule(0, g)

            dve.wait_ge(stored1, 16 * 5)
            own.start(V.memset(L, 0.0))
            own.wait()
            for t, (t0, n) in enumerate(TT):
                own.settle(V.tensor_copy(L[0:n, t, :], see(dve, ("lg", t))[0:n, 0:NE]))
                dve.nop().then_inc(freed(("lg", t)), 1)
                own.settle(V.max(mx[:, t, :], L[:, t, :]))
                own.settle(V.max_index(idx[:, t, :], mx[:, t, :], L[:, t, :]))
            own.start(V.tensor_tensor(w12[:, 0, :], mx[:, :, 1], mx[:, :, 0], ALU.subtract))
            own.start(V.tensor_copy(ixf, idx[:]))
            own.wait()
            dve.nop().then_inc(route1, 1)
            dve.wait_ge(route2, 1)
            own.settle(V.tensor_scalar(w12[:, 2, :], w12[:, 0, :], 1.0, None, ALU.add))
            own.settle(V.reciprocal(w12[:, 1, :], w12[:, 2, :]))
            own.settle(V.tensor_tensor(w12[:, 2, :], w12[:, 0, :], w12[:, 1, :], ALU.mult))
            io = bc(con_("iota")[:, 0:NE].unsqueeze(1), [P, 3, NE])
            for i in range(2):
                own.settle(V.tensor_tensor(oh, io, bc(ixf[:, :, i:i + 1], [P, 3, NE]), ALU.is_equal))
                if i == 0:
                    own.settle(V.tensor_copy(sel, oh))
                    own.settle(V.tensor_tensor(gat, oh, bc(w12[:, 1, :].unsqueeze(2), [P, 3, NE]), ALU.mult))
                else:
                    own.settle(V.tensor_tensor(sel, sel, oh, ALU.add))
                    own.settle(V.tensor_tensor(oh, oh, bc(w12[:, 2, :].unsqueeze(2), [P, 3, NE]), ALU.mult))
                    own.settle(V.tensor_tensor(gat, gat, oh, ALU.add))
            own.settle(V.tensor_scalar(sel[:, 2, :], sel[:, 2, :], con_("valid"), None, ALU.mult))
            dve.nop().then_inc(sel_ready, 1)
            own.settle(V.tensor_reduce(mcnt[:, 0:1], see(dve, "count")[:, 0:NE], AX.X, ALU.max))
            dve.nop().then_inc(freed("count"), 1)
            own.settle(V.tensor_scalar(mcnt[:, 1:2], mcnt[:, 0:1], float(CAP), None, ALU.is_gt))
            own.settle(V.tensor_scalar(mcnt[:, 2:3], mcnt[:, 0:1], float(2 * CAP), None, ALU.is_gt))
            own.settle(V.tensor_tensor(mcnt[:, 3:4], mcnt[:, 1:2], mcnt[:, 2:3], ALU.add))
            V.tensor_copy(nmore[:], mcnt[0:1, 3:4]).then_inc(more_ready, 1)
            own.settle(V.tensor_scalar(rnk, see(dve, "rank")[:, 0:3 * NE].rearrange("p (t e) -> p t e", t=3), 1.0, None, ALU.add))
            dve.nop().then_inc(freed("rank"), 1)
            own.settle(V.tensor_tensor(rnk, rnk, sel, ALU.mult))
            own.start(V.memset(jrank, -1.0))
            own.start(V.memset(jgate, 0.0))
            own.wait()
            for p in range(MAXPASS):
                own.start(V.tensor_scalar(jrank[:, :, p * NE:(p + 1) * NE], rnk, -1.0 - p * CAP, None, ALU.add))
                own.start(V.tensor_copy(jgate[:, :, p * NE:(p + 1) * NE], gat))
            own.start(V.tensor_scalar(R[:], X[:], ALPHA, None, ALU.mult))
            own.wait()
            dve.nop().then_inc(jobs_ready, 1)
            dve.wait_ge(more_ready, 1)
            more = dve.value_load(nmore[0:1, 0:1], min_val=0, max_val=MAXPASS - 1)

            def selection(j):
                V.tensor_copy(crank.unsqueeze(2), jrank[:, :, bass.ds(j, 1)]).then_inc(racc_ready, 1)
                V.tensor_copy(cgate.unsqueeze(2), jgate[:, :, bass.ds(j, 1)]).then_inc(racc_ready, 1)
                dve.wait_ge(racc_ready, j * 2 + 2)
                for t in range(3):
                    V.tensor_scalar(G[:, t, :], con_("iota"), crank[:, t:t + 1], None, ALU.is_equal).then_inc(gathered, 1)
                dve.wait_ge(gathered, j * 3 + 3)

            def gated():
                for t in range(3):
                    ins = V.tensor_scalar(Gg[:, t, :], con_("iota"), crank[:, t:t + 1], cgate[:, t:t + 1],
                                          ALU.is_equal, ALU.mult)
                return ins

            def split_gathered(j):
                for a in range(2):
                    dve.wait_ge(xgh_ready, j * 2 + (a + 1))
                    V.tensor_tensor(xgl[:, 4 * a:4 * a + 4, :].rearrange("p k n -> p (k n)"), bank[6 + a],
                                    xgh[:, 4 * a:4 * a + 4, :].bitcast(F32).rearrange("p k n -> p (k n)"),
                                    ALU.subtract).then_inc(xgl_ready, 1)

            dve.nop().then_inc(xgl_ready, 1)
            dve.nop().then_inc(sc_added, 1)
            selection(0)
            dve.nop().then_inc(g_ready, 1)
            gated().then_inc(gg_ready, 1)
            split_gathered(0)

            def expert(j, last=False):
                for g in range(NSPLIT, GPJ):
                    rest_of_granule(j, g)
                    if g in SILU_AT:
                        b = SILU_AT[g]
                        dve.wait_ge(silE_ready, j * NBLK + (b + 1))
                        V.tensor_tensor(hb, sE, bank[2 * (b % 2) + 1], ALU.mult).then_inc(hb_ready, 1)
                    if g in TURNED_AT:
                        b = TURNED_AT[g]
                        dve.wait_ge(hTh_ready, j * NBLK + (b + 1))
                        V.tensor_tensor(hTl[:, b % 2].rearrange("p f n -> p (f n)"), bank[TURN_BANK[b]],
                                        hTh[:, b % 2].bitcast(F32).rearrange("p f n -> p (f n)"),
                                        ALU.subtract).then_inc(hT_ready, 1)
                    if g == GPJ // 2 and not last:
                        selection(j + 1)
                        dve.nop().then_inc(g_ready, 1)
                if not last:
                    split_gathered(j + 1)
                    dve.wait_ge(gt_psum, j + 1)
                    gated().then_inc(gg_ready, 1)
                    rest_of_granule(j, GPJ)
                for k in range(KD):
                    if k in (0, 2, 5) and not last:
                        rest_of_granule(j, GPJ + 1 + (0, 2, 5).index(k))
                    dve.wait_ge(sc_psum, j * KD + (k + 1))
                    V.tensor_tensor(R[:, k, :], R[:, k, :], bank[SCATTER_BANK[k]][:, 0:N], ALU.add).then_inc(sc_added, 1)

            with dve.Fori(0, more * NE + (NE - 1)) as j:
                expert(j)
            expert(more * NE + (NE - 1), last=True)
            dve.wait_ge(sc_added, more * (NE * KD) + (NE * KD + 1))
            for k in range(KD):
                dve.nop().then_inc(r_ready, 1)
            layernorm(3)
            dve.nop().then_inc(out_ready, 1)

        @block.gpsimd
        def _(pool):
            Pv = nc.gpsimd
            for j in range(GPAIR):
                Pv.memset(q0[GLA_DK:P, HG + 2 * j, :], 0.0).then_inc(q_zeroed, 1)
                Pv.memset(q0[0:GLA_DK, HG + 2 * j + 1, :], 0.0).then_inc(q_zeroed, 1)
            pool.wait_ge(q_zeroed, GL)
            pool.wait_ge(state0_loaded, 16)
            pool.wait_ge(expd_ready, 1)
            n = 0
            for j in range(KT):
                Pv.tensor_tensor(S0[:, j], S0[:, j], bc(as0[:, j].unsqueeze(2), [P, NS, P]), ALU.mult).then_inc(pool_own, 1)
                n += 1
            pool.wait_ge(pool_own, n)
            pool.nop().then_inc(sdec_ready, 1)
            pool.wait_ge(s_final, 1)
            pool.dma_start(A["o_state0p"], S).then_inc(stored0, 16)
            pool.wait_ge(snew_ready, NS)
            pool.dma_start(A["o_state0s"], state[:, 0:6144]).then_inc(stored0, 16)
            pool.wait_ge(u_ready, KD)
            pool.wait_ge(freed(("y", KD - 1)), J[("y", KD - 1)] // 8 + 1)
            pool.wait_ge(conv_loaded, 32)
            with nc.allow_non_contiguous_dma(reason="three columns of each row"):
                pool.dma_start(A["o_convp"], up[:, :, NP_:NP_ + 3]).then_inc(stored1, 16)
                pool.dma_start(A["o_convs"], us[:, :, 1:4, :].rearrange("p j r b -> p j (r b)")).then_inc(stored1, 16)
                pool.wait_ge(rows_ready, 1)
                pool.dma_start(A["o_m"], rows[:, 4, NP_ - 1:N]).then_inc(stored1, 16)
            pool.wait_ge(state1_loaded, 16)
            pool.wait_ge(fwb_ready, 1)
            pool.wait_ge(psum_ready, J[("ns", PAIRS - 1)] + 1)
            for h in range(MH):
                Pv.tensor_tensor(Cs[:, h], Cs[:, h], bc(fwb[:, h, 1, :].unsqueeze(2), [P, NS, MDV]), ALU.mult)\
                    .then_inc(pool_own, 1)
                n += 1
            pool.wait_ge(pool_own, n)
            for b in range(NS):
                pool.wait_ge(kv_ready, b + 1)
                Pv.tensor_tensor(Cs[:, :, b, :], Cs[:, :, b, :], kvb[b % 2], ALU.add).then_inc(cnew_ready, 1)
            pool.wait_ge(cout_ready, MH)
            pool.dma_start(A["o_Cp"], Cout).then_inc(stored1, 16)
            pool.dma_start(A["o_ns"], n0).then_inc(stored1, 16)
            pool.wait_ge(cnew_ready, NS)
            pool.dma_start(A["o_Cs"], state[:, 0:8192]).then_inc(stored, 16)
            pool.wait_ge(out_ready, 1)
            pool.dma_start(A["o_y"], X[:]).then_inc(stored, 16)
            pool.wait_ge(stored0, 32)
            pool.wait_ge(stored1, 16 * 5)
            pool.wait_ge(stored, 16 * 2)


_OUT = {
    "o_y": (P, KD, N), "o_state0p": (P, KT, P), "o_state0s": (P, KT * NS * P), "o_convp": (P, KD, 3),
    "o_convs": (P, KD, 3 * NS), "o_m": (MH, 1 + NS), "o_Cp": (P, MH, MDV + 1), "o_ns": (P, MH, NS),
    "o_Cs": (P, MH * NS * MDV),
}


def _tiles(w):
    k, n = w.shape
    return w.reshape(k // P, P, n // P, P).transpose(2, 1, 0, 3).reshape(n // P, P, k)


def _columns(v):
    return v.reshape(-1, P).T


def _constants():
    p = np.arange(P)[:, None]
    f = np.arange(P)[None, :]
    parts = {
        "ident": (p == f), "ones": np.ones((P, P)), "causal64": (p % CH <= f[:, :CH]),
        "neg": np.where(p > f, -1e30, 0.0), "before": (p < f), "iota": np.broadcast_to(f, (P, P)),
        "valid": (p < NS), "eps": np.full((P, 1), EPS), "one": np.ones((P, 1)),
    }
    con = np.concatenate([np.asarray(parts[n], np.float32) for n in CON], 1)
    mask = np.ones((KT, N), np.float32)
    mask[:, 0:NP_:CH] = 0
    mask[:, NP_:] = 0
    return con, np.ascontiguousarray(np.broadcast_to(mask.reshape(1, -1), (P, KT * N)))


def _layout(i):
    i = {k: np.asarray(v) for k, v in i.items()}
    a = {}
    x = np.concatenate([i["x_prompt"][0], i["x_sample"][:, 0]], 0)
    a["x"] = x.T.reshape(KD, P, N).transpose(1, 0, 2)
    w = i["w_in_even"][0]
    ends = np.cumsum([0, 512, 512, 512, 512, 256, 256, 512, 512, RANK])
    hq, hf, hi, hg, gq, gk, gv, gg, gr = (w[:, s:e] for s, e in zip(ends[:-1], ends[1:]))
    a["w_in0"] = np.concatenate([_tiles(t) for t in (hf, hq, hg, gg, gk, gq, hi, gv)], 0)
    a["w_gr"] = gr.reshape(KD, P, RANK).transpose(1, 0, 2)
    a["w_gk"] = i["w_gk"][0]
    a["w_out0"] = _tiles(i["w_out_even"][0])
    a["w13"] = np.concatenate([_tiles(i["w1_dense"][0]), _tiles(i["w3_dense"][0])], 2)
    a["w2"] = i["w2_dense"][0].reshape(FD, P, D)
    w = i["w_in_odd"][0]
    a["w_in1"] = _tiles(w[:, :3 * D])
    a["w_gate"] = w[:, 3 * D:].reshape(KD, P, 2 * MH).transpose(1, 0, 2)
    a["w_out1"] = _tiles(i["w_out_odd"][0])
    a["w_router"] = i["w_router"][0].reshape(KD, P, NE).transpose(1, 0, 2)

    def up(w):
        return w.reshape(NE, KD // 2, 2, P, NBLK, BLK).transpose(0, 4, 1, 3, 2, 5).reshape(NE, NBLK, KD // 2, P, D)

    parts = {"w1": up(i["w1_moe"][0]), "w3": up(i["w3_moe"][0]), "w2": i["w2_moe"][0].reshape(NE, NBLK, BLK // P, P, D)}
    moe = np.empty((NE, FE, P, 3, D), np.float32)
    for g, (name, b, c) in enumerate(ORDER):
        moe[:, g // 3, :, g % 3] = parts[name][:, b, c]
    a["w_moe"] = moe.reshape(NE * FE, P, 3 * D)
    lb = i["hg_lower_bounds"]
    v = {"lb0": lb[0], "lb1": lb[1], "bgk": i["b_gk"][0], "gn_hg": i["gn_hg"][0], "gn_gla": i["gn_gla"][0],
         "convb": i["conv_b"][0], "hn": i["hn_w"][0]}
    for n in LN_VECS:
        v[n] = i[f"{n[:3]}_{n[3]}"][int(n[4])]
    for j in range(4):
        v[f"convw{j}"] = i["conv_w"][0, j]
    a["vec"] = np.concatenate([_columns(v[n]) for n in VEC], 1)
    a["b_gate"] = i["b_gate_odd"][0].reshape(2, MH).T
    a["m0"] = i["state_mlstm_m"][0].T
    hgs = i["state_hgrn"][0].transpose(2, 1, 0, 3)
    gls = i["state_gla"][0].reshape(NS, GPAIR, 2 * GLA_DK, P).transpose(2, 1, 0, 3)
    a["state0"] = np.concatenate([hgs, gls], 1).reshape(P, -1)
    a["state1"] = i["state_mlstm_C"][0].transpose(2, 1, 0, 3).reshape(P, -1)
    a["n0"] = i["state_mlstm_n"][0].transpose(2, 1, 0)
    a["conv0"] = i["state_mlstm_conv"][0].reshape(NS, 3, KD, P).transpose(3, 2, 1, 0).reshape(P, KD, 3 * NS)
    a["con"], a["scan_mask"] = _constants()
    return {k: np.ascontiguousarray(t) for k, t in a.items()}


def kernel(**inputs):
    import concourse.bacc as _bacc
    from concourse.bass_utils import run_bass_kernel_spmd as _run

    arrays = _layout(inputs)
    nc = _bacc.Bacc("TRN2", target_bir_lowering=False, num_devices=1, dynamic_dma_scratch_size=4096)
    A = {n: nc.dram_tensor(f"in_{n}", t.shape, mybir.dt.from_np(t.dtype), kind="ExternalInput").ap()
         for n, t in arrays.items()}
    for n, shape in _OUT.items():
        A[n] = nc.dram_tensor(n, shape, F32, kind="ExternalOutput").ap()
    decoder_step(nc, A)
    r = _run(nc, [{f"in_{n}": t for n, t in arrays.items()}], core_ids=[0]).results[0]
    o = {n: np.asarray(r[n]).reshape(s) for n, s in _OUT.items()}
    y = o["o_y"].transpose(2, 1, 0).reshape(N, D)
    sp = o["o_state0p"]
    ss = o["o_state0s"].reshape(P, KT, NS, P)
    hg_p = sp[:, :HG].transpose(1, 0, 2)[None, None]
    gla_p = sp[:, HG:].transpose(1, 0, 2).reshape(GL, GLA_DK, P)[None, None]
    hg_s = ss[:, :HG].transpose(2, 1, 0, 3)[None]
    gla_s = ss[:, HG:].transpose(2, 1, 0, 3).reshape(NS, GL, GLA_DK, P)[None]
    C_p = o["o_Cp"][:, :, :MDV].transpose(1, 0, 2)[None, None]
    n_p = o["o_Cp"][:, :, MDV].T[None, None]
    m_p = o["o_m"][:, 0][None, None]
    conv_p = o["o_convp"].transpose(2, 1, 0).reshape(3, D)[None, None]
    C_s = o["o_Cs"].reshape(P, MH, NS, MDV).transpose(2, 1, 0, 3)[None]
    n_s = o["o_ns"].transpose(2, 1, 0)[None]
    m_s = o["o_m"][:, 1:].T[None]
    conv_s = o["o_convs"].reshape(P, KD, 3, NS).transpose(3, 2, 1, 0).reshape(NS, 3, D)[None]
    out = (y[:NP_][None], y[NP_:][:, None], hg_p, gla_p, C_p, n_p, m_p, conv_p, hg_s, gla_s, C_s, n_s, m_s, conv_s)
    return tuple(np.ascontiguousarray(t) for t in out)
```
